# Optimizing a Trainium2 kernel written in Bass

```python
import math
import jax, jax.numpy as jnp
from jax import lax
import numpy as np

D_MODEL = 1024
BATCH = 1
SEQ = 256
DEPTH = 1

MIX_WIDTH = D_MODEL
MLA_WIDTH = MIX_WIDTH // 2
RET_WIDTH = MIX_WIDTH - MLA_WIDTH
MLA_HEADS = 4
MLA_NOPE_DIM = 128
MLA_ROPE_DIM = 64
MLA_QK_DIM = MLA_NOPE_DIM + MLA_ROPE_DIM
MLA_V_DIM = MLA_WIDTH // MLA_HEADS
MLA_Q_RANK = 256
MLA_KV_RANK = 128
Q_BLOCK = 128
RET_HEADS = 4
RET_HEAD_DIM = RET_WIDTH // RET_HEADS
RET_CHUNK = 128
MEM_TOKENS = 256
CROSS_HEADS = 4
CROSS_HEAD_DIM = D_MODEL // CROSS_HEADS
N_GROUPS = 4
EXPERTS_PER_GROUP = 8
N_EXPERTS = N_GROUPS * EXPERTS_PER_GROUP
TOP_K = 2
EXPERT_FF = 256
ROPE_BASE = 10000.0
EPS = 1e-6
NEG_INF = -1e30
IN_SPLITS = (MLA_Q_RANK, MLA_KV_RANK, MLA_ROPE_DIM, RET_WIDTH, RET_WIDTH, RET_WIDTH, RET_WIDTH)
IN_COLS = sum(IN_SPLITS)


def rms_norm(x, g):
    xf = x.astype(jnp.float32)
    y = xf * lax.rsqrt(jnp.mean(xf * xf, axis=-1, keepdims=True) + EPS)
    return (y * g.astype(jnp.float32)).astype(x.dtype)

def rope(x, positions):
    half = x.shape[-1] // 2
    inv_freq = ROPE_BASE ** (-jnp.arange(half, dtype=jnp.float32) / half)
    ang = positions.astype(jnp.float32)[:, :, None] * inv_freq
    cos = jnp.cos(ang)[:, :, None, :]
    sin = jnp.sin(ang)[:, :, None, :]
    xf = x.astype(jnp.float32)
    x1, x2 = xf[..., :half], xf[..., half:]
    return jnp.concatenate([x1 * cos - x2 * sin, x2 * cos + x1 * sin], axis=-1).astype(x.dtype)

def causal_block_attention(q, k, v):
    B, S, H, dq = q.shape
    dv = v.shape[-1]
    nb = S // Q_BLOCK
    scale = dq ** -0.5
    qb = q.reshape(B, nb, Q_BLOCK, H, dq).transpose(1, 0, 2, 3, 4)
    k_idx = jnp.arange(S)

    def one_block(args):
        q_blk, b = args
        s = jnp.einsum('bqhd,bkhd->bhqk', q_blk, k, preferred_element_type=jnp.float32) * scale
        q_idx = b * Q_BLOCK + jnp.arange(Q_BLOCK)
        s = jnp.where(k_idx[None, :] <= q_idx[:, None], s, NEG_INF)
        p = jax.nn.softmax(s, axis=-1).astype(v.dtype)
        return jnp.einsum('bhqk,bkhd->bqhd', p, v)

    out = lax.map(one_block, (qb, jnp.arange(nb)))
    return out.transpose(1, 0, 2, 3, 4).reshape(B, S, H, dv)

def retention_chunkwise(q, k, v):
    B, S, H, dk = q.shape
    dv = v.shape[-1]
    nc = S // RET_CHUNK

    def to_chunks(t):
        return t.astype(jnp.float32).reshape(B, nc, RET_CHUNK, H, t.shape[-1]).transpose(1, 0, 3, 2, 4)

    lg = jnp.log(1.0 - jnp.exp2(-5.0 - jnp.arange(H, dtype=jnp.float32)))
    idx = jnp.arange(RET_CHUNK, dtype=jnp.float32)
    diff = idx[:, None] - idx[None, :]
    intra = jnp.where(diff >= 0, jnp.exp(jnp.maximum(diff, 0.0)[None] * lg[:, None, None]), 0.0)
    q_decay = jnp.exp((idx + 1.0)[None] * lg[:, None])[:, :, None]
    k_decay = jnp.exp((RET_CHUNK - 1.0 - idx)[None] * lg[:, None])[:, :, None]
    chunk_decay = jnp.exp(RET_CHUNK * lg)[:, None, None]

    def step(state, qkv):
        qc, kc, vc = qkv
        scores = jnp.einsum('bhid,bhjd->bhij', qc, kc) * intra
        o = (jnp.einsum('bhij,bhjv->bhiv', scores, vc)
             + jnp.einsum('bhid,bhdv->bhiv', qc * q_decay, state))
        state = state * chunk_decay + jnp.einsum('bhjd,bhjv->bhdv', kc * k_decay, vc)
        return state, o

    state0 = jnp.zeros((B, H, dk, dv), jnp.float32)
    _, o = lax.scan(step, state0, (to_chunks(q), to_chunks(k), to_chunks(v)))
    return o.transpose(1, 0, 3, 2, 4).reshape(B, S, H, dv)

def mla_group(c_q, c_kv, k_pe, positions, q_norm_g, w_uq, kv_norm_g, w_ukv, q_qk_g, k_qk_g):
    B, S, _ = c_q.shape
    q = (rms_norm(c_q, q_norm_g) @ w_uq).reshape(B, S, MLA_HEADS, MLA_QK_DIM)
    kv = (rms_norm(c_kv, kv_norm_g) @ w_ukv).reshape(B, S, MLA_HEADS, MLA_NOPE_DIM + MLA_V_DIM)
    k_nope, v = kv[..., :MLA_NOPE_DIM], kv[..., MLA_NOPE_DIM:]
    k_rope = jnp.broadcast_to(k_pe[:, :, None, :], (B, S, MLA_HEADS, MLA_ROPE_DIM))
    k = jnp.concatenate([k_nope, k_rope], axis=-1)
    q = rms_norm(q, q_qk_g)
    k = rms_norm(k, k_qk_g)
    q = jnp.concatenate([q[..., :MLA_NOPE_DIM], rope(q[..., MLA_NOPE_DIM:], positions)], axis=-1)
    k = jnp.concatenate([k[..., :MLA_NOPE_DIM], rope(k[..., MLA_NOPE_DIM:], positions)], axis=-1)
    o = causal_block_attention(q, k, v)
    return o.reshape(B, S, MLA_WIDTH)

def retention_group(rq, rk, rv, rg, positions, gn_g):
    B, S, _ = rq.shape
    q = rope(rq.reshape(B, S, RET_HEADS, RET_HEAD_DIM), positions)
    k = rope(rk.reshape(B, S, RET_HEADS, RET_HEAD_DIM), positions) * (RET_HEAD_DIM ** -0.5)
    v = rv.reshape(B, S, RET_HEADS, RET_HEAD_DIM)
    o = retention_chunkwise(q, k, v)
    mu = jnp.mean(o, axis=-1, keepdims=True)
    var = jnp.mean(jnp.square(o - mu), axis=-1, keepdims=True)
    o = ((o - mu) * lax.rsqrt(var + EPS)).reshape(B, S, RET_WIDTH) * gn_g.astype(jnp.float32)
    return (o * jax.nn.silu(rg.astype(jnp.float32))).astype(rq.dtype)

def memory_cross_attention(h, m, w_q, w_kv, q_qk_g, k_qk_g, w_o):
    B, S, _ = h.shape
    M = m.shape[1]
    q = rms_norm((h @ w_q).reshape(B, S, CROSS_HEADS, CROSS_HEAD_DIM), q_qk_g)
    kv = m @ w_kv
    k = rms_norm(kv[..., :D_MODEL].reshape(B, M, CROSS_HEADS, CROSS_HEAD_DIM), k_qk_g)
    v = kv[..., D_MODEL:].reshape(B, M, CROSS_HEADS, CROSS_HEAD_DIM)
    s = jnp.einsum('bshd,bmhd->bhsm', q, k, preferred_element_type=jnp.float32) * (CROSS_HEAD_DIM ** -0.5)
    p = jax.nn.softmax(s, axis=-1).astype(v.dtype)
    o = jnp.einsum('bhsm,bmhd->bshd', p, v).reshape(B, S, D_MODEL)
    return o @ w_o

def hierarchical_moe(h, w_group, b_group, w_expert, b_expert, w_gate, w_up, w_down):
    def per_row(hr):
        S = hr.shape[0]
        g_logits = jnp.einsum('sd,dg->sg', hr, w_group, preferred_element_type=jnp.float32)
        g_prob = jax.nn.softmax(g_logits, axis=-1)
        g_sel = jnp.argmax(g_logits + b_group.astype(jnp.float32), axis=-1)
        g_w = jnp.take_along_axis(g_prob, g_sel[:, None], axis=-1)
        e_all = jnp.einsum('sd,de->se', hr, w_expert, preferred_element_type=jnp.float32)
        e_all = e_all.reshape(S, N_GROUPS, EXPERTS_PER_GROUP)
        e_logits = jnp.take_along_axis(e_all, g_sel[:, None, None], axis=1)[:, 0]
        e_bias = b_expert.astype(jnp.float32).reshape(N_GROUPS, EXPERTS_PER_GROUP)[g_sel]
        e_prob = jax.nn.softmax(e_logits, axis=-1)
        _, top_idx = lax.top_k(e_logits + e_bias, TOP_K)
        top_p = jnp.take_along_axis(e_prob, top_idx, axis=-1)
        top_p = top_p / jnp.sum(top_p, axis=-1, keepdims=True)
        local_w = jnp.sum(jax.nn.one_hot(top_idx, EXPERTS_PER_GROUP, dtype=jnp.float32) * top_p[..., None], axis=1)
        gate = (jax.nn.one_hot(g_sel, N_GROUPS, dtype=jnp.float32)[:, :, None]
                * local_w[:, None, :] * g_w[:, :, None]).reshape(S, N_EXPERTS)
        a = jnp.einsum('sd,edf->sef', hr, w_gate)
        u = jnp.einsum('sd,edf->sef', hr, w_up)
        act = jax.nn.silu(a) * u * gate[:, :, None].astype(hr.dtype)
        return jnp.einsum('sef,efd->sd', act, w_down)

    return lax.map(per_row, h)

def first_inputs(seed: int = 0) -> dict:
    key = jax.random.key(seed)
    ks = jax.random.split(key, 32)

    def w(k, shape, fan_in):
        return jax.random.normal(k, (DEPTH,) + shape, jnp.float32) * (fan_in ** -0.5)

    def gain(k, n):
        return 1.0 + 0.02 * jax.random.normal(k, (DEPTH, n), jnp.float32)

    def bias(k, n):
        return 0.01 * jax.random.normal(k, (DEPTH, n), jnp.float32)

    x = jax.random.normal(ks[0], (BATCH, SEQ, D_MODEL), jnp.float32)
    mem = jax.random.normal(ks[1], (BATCH, MEM_TOKENS, D_MODEL), jnp.float32)
    offsets = jax.random.randint(ks[2], (BATCH, 1), 0, 1024, dtype=jnp.int32)
    positions = offsets + jnp.arange(SEQ, dtype=jnp.int32)[None, :]
    return {
        'x': x,
        'mem': mem,
        'positions': positions,
        'attn_norm_g': gain(ks[3], D_MODEL),
        'w_in': w(ks[4], (D_MODEL, IN_COLS), D_MODEL),
        'mla_q_norm_g': gain(ks[5], MLA_Q_RANK),
        'mla_w_uq': w(ks[6], (MLA_Q_RANK, MLA_HEADS * MLA_QK_DIM), MLA_Q_RANK),
        'mla_kv_norm_g': gain(ks[7], MLA_KV_RANK),
        'mla_w_ukv': w(ks[8], (MLA_KV_RANK, MLA_HEADS * (MLA_NOPE_DIM + MLA_V_DIM)), MLA_KV_RANK),
        'mla_q_qk_g': gain(ks[9], MLA_QK_DIM),
        'mla_k_qk_g': gain(ks[10], MLA_QK_DIM),
        'ret_gn_g': gain(ks[11], RET_WIDTH),
        'w_out': w(ks[12], (MIX_WIDTH, D_MODEL), MIX_WIDTH),
        'cross_norm_g': gain(ks[13], D_MODEL),
        'mem_norm_g': gain(ks[14], D_MODEL),
        'cross_w_q': w(ks[15], (D_MODEL, D_MODEL), D_MODEL),
        'cross_w_kv': w(ks[16], (D_MODEL, 2 * D_MODEL), D_MODEL),
        'cross_q_qk_g': gain(ks[17], CROSS_HEAD_DIM),
        'cross_k_qk_g': gain(ks[18], CROSS_HEAD_DIM),
        'cross_w_o': w(ks[19], (D_MODEL, D_MODEL), D_MODEL),
        'moe_norm_g': gain(ks[20], D_MODEL),
        'router_w_group': w(ks[21], (D_MODEL, N_GROUPS), D_MODEL),
        'router_b_group': bias(ks[22], N_GROUPS),
        'router_w_expert': w(ks[23], (D_MODEL, N_EXPERTS), D_MODEL),
        'router_b_expert': bias(ks[24], N_EXPERTS),
        'expert_w_gate': w(ks[25], (N_EXPERTS, D_MODEL, EXPERT_FF), D_MODEL),
        'expert_w_up': w(ks[26], (N_EXPERTS, D_MODEL, EXPERT_FF), D_MODEL),
        'expert_w_down': w(ks[27], (N_EXPERTS, EXPERT_FF, D_MODEL), EXPERT_FF),
    }

def first_block(x, mem, positions, attn_norm_g, w_in, mla_q_norm_g, mla_w_uq, mla_kv_norm_g, mla_w_ukv,
              mla_q_qk_g, mla_k_qk_g, ret_gn_g, w_out, cross_norm_g, mem_norm_g, cross_w_q, cross_w_kv,
              cross_q_qk_g, cross_k_qk_g, cross_w_o, moe_norm_g, router_w_group, router_b_group,
              router_w_expert, router_b_expert, expert_w_gate, expert_w_up, expert_w_down):
    split_points = [int(s) for s in np.cumsum(IN_SPLITS)[:-1]]
    for l in range(DEPTH):
        h = rms_norm(x, attn_norm_g[l])
        proj = h @ w_in[l]
        c_q, c_kv, k_pe, rq, rk, rv, rg = jnp.split(proj, split_points, axis=-1)
        a_out = mla_group(c_q, c_kv, k_pe, positions, mla_q_norm_g[l], mla_w_uq[l],
                          mla_kv_norm_g[l], mla_w_ukv[l], mla_q_qk_g[l], mla_k_qk_g[l])
        r_out = retention_group(rq, rk, rv, rg, positions, ret_gn_g[l])
        x = x + jnp.concatenate([a_out, r_out], axis=-1) @ w_out[l]
        hc = rms_norm(x, cross_norm_g[l])
        m = rms_norm(mem, mem_norm_g[l])
        x = x + memory_cross_attention(hc, m, cross_w_q[l], cross_w_kv[l], cross_q_qk_g[l],
                                       cross_k_qk_g[l], cross_w_o[l])
        hm = rms_norm(x, moe_norm_g[l])
        x = x + hierarchical_moe(hm, router_w_group[l], router_b_group[l], router_w_expert[l],
                                 router_b_expert[l], expert_w_gate[l], expert_w_up[l], expert_w_down[l])
    return x


D_RNN = D_MODEL
RG_HEADS = 4
RG_BLOCK = D_RNN // RG_HEADS
RG_C = 8.0
CONV4_WIDTH = 4
D_CONV = D_MODEL
CONV3_WIDTH = 3
D_FF = ((8 * D_MODEL + 3 * 256 - 1) // (3 * 256)) * 256
PLE_DIM = 256
IN_SPLITS_2 = (D_RNN, D_RNN, D_CONV, D_CONV, D_CONV, D_MODEL, D_MODEL)
W_IN = sum(IN_SPLITS_2)
IN_OFFSETS = tuple(int(v) for v in np.cumsum(IN_SPLITS_2)[:-1])


def rmsnorm(x, g):
    xf = x.astype(jnp.float32)
    y = xf * lax.rsqrt(jnp.mean(xf * xf, axis=-1, keepdims=True) + EPS)
    return (y * g.astype(jnp.float32)).astype(x.dtype)

def causal_depthwise_conv(x, w):
    k_w = w.shape[0]
    t = x.shape[1]
    xp = jnp.pad(x, ((0, 0), (k_w - 1, 0), (0, 0)))
    y = xp[:, 0:t] * w[0]
    for k in range(1, k_w):
        y = y + xp[:, k:k + t] * w[k]
    return y

def block_diag_linear(x, w, b):
    bsz, t, _ = x.shape
    xh = x.reshape(bsz, t, RG_HEADS, RG_BLOCK)
    y = jnp.einsum("bthi,hij->bthj", xh, w) + b
    return y.reshape(bsz, t, RG_HEADS * RG_BLOCK)

def rg_lru(x, w_r, b_r, w_i, b_i, lam):
    r = jax.nn.sigmoid(block_diag_linear(x, w_r, b_r).astype(jnp.float32))
    i = jax.nn.sigmoid(block_diag_linear(x, w_i, b_i).astype(jnp.float32))
    log_a = -RG_C * r * jax.nn.softplus(-lam.astype(jnp.float32))
    a = jnp.exp(log_a)
    mult = jnp.sqrt(-jnp.expm1(2.0 * log_a))
    u = mult * (i * x.astype(jnp.float32))

    def step(h, au):
        a_t, u_t = au
        h = a_t * h + u_t
        return h, h

    h0 = jnp.zeros((x.shape[0], x.shape[2]), jnp.float32)
    _, hs = lax.scan(step, h0, (jnp.swapaxes(a, 0, 1), jnp.swapaxes(u, 0, 1)))
    return jnp.swapaxes(hs, 0, 1).astype(x.dtype)

def hybrid_layer(x, p_i, g_mix, w_in, conv4_w, conv4_b, w_rg_r, b_rg_r, w_rg_i, b_rg_i,
                 lru_lambda, conv3_w, w_out, g_ffn, w_gate_up, w_down, g_ple, w_ple_gate, w_ple):
    h = rmsnorm(x, g_mix)
    z = h @ w_in
    rnn_x, rnn_y, conv_b, conv_c, conv_x, gate_rnn, gate_conv = jnp.split(z, IN_OFFSETS, axis=-1)
    rnn_x = causal_depthwise_conv(rnn_x, conv4_w) + conv4_b
    y_rnn = jax.nn.gelu(rnn_y) * rg_lru(rnn_x, w_rg_r, b_rg_r, w_rg_i, b_rg_i, lru_lambda)
    y_conv = conv_b * causal_depthwise_conv(conv_c * conv_x, conv3_w)
    merged = jax.nn.sigmoid(gate_rnn) * y_rnn + jax.nn.sigmoid(gate_conv) * y_conv
    x = x + merged @ w_out
    h = rmsnorm(x, g_ffn)
    g, u = jnp.split(h @ w_gate_up, 2, axis=-1)
    x = x + (jax.nn.silu(g) * u) @ w_down
    gate = jax.nn.sigmoid(rmsnorm(x, g_ple) @ w_ple_gate)
    x = x + gate * (p_i @ w_ple)
    return x

def second_inputs(seed: int = 0) -> dict:
    key = jax.random.key(seed)
    ks = jax.random.split(key, 20)

    def nrm(k, shape, fan_in):
        return jax.random.normal(k, shape, jnp.float32) * (fan_in ** -0.5)

    def gain(k, shape):
        return 1.0 + 0.05 * jax.random.normal(k, shape, jnp.float32)

    def bias(k, shape):
        return 0.02 * jax.random.normal(k, shape, jnp.float32)

    x = jax.random.normal(ks[0], (BATCH, SEQ, D_MODEL), jnp.float32)
    p = jax.random.normal(ks[1], (DEPTH, BATCH, SEQ, PLE_DIM), jnp.float32)
    g_mix = gain(ks[2], (DEPTH, D_MODEL))
    w_in = nrm(ks[3], (DEPTH, D_MODEL, W_IN), D_MODEL)
    conv4_w = nrm(ks[4], (DEPTH, CONV4_WIDTH, D_RNN), CONV4_WIDTH)
    conv4_b = bias(ks[5], (DEPTH, D_RNN))
    w_rg_r = nrm(ks[6], (DEPTH, RG_HEADS, RG_BLOCK, RG_BLOCK), RG_BLOCK)
    b_rg_r = bias(ks[7], (DEPTH, RG_HEADS, RG_BLOCK))
    w_rg_i = nrm(ks[8], (DEPTH, RG_HEADS, RG_BLOCK, RG_BLOCK), RG_BLOCK)
    b_rg_i = bias(ks[9], (DEPTH, RG_HEADS, RG_BLOCK))
    a_c = jax.random.uniform(ks[10], (DEPTH, D_RNN), jnp.float32, minval=0.9, maxval=0.999)
    a0 = a_c ** (1.0 / RG_C)
    lru_lambda = jnp.log(a0) - jnp.log1p(-a0)
    conv3_w = nrm(ks[11], (DEPTH, CONV3_WIDTH, D_CONV), CONV3_WIDTH)
    w_out = nrm(ks[12], (DEPTH, D_MODEL, D_MODEL), D_MODEL)
    g_ffn = gain(ks[13], (DEPTH, D_MODEL))
    w_gate_up = nrm(ks[14], (DEPTH, D_MODEL, 2 * D_FF), D_MODEL)
    w_down = nrm(ks[15], (DEPTH, D_FF, D_MODEL), D_FF)
    g_ple = gain(ks[16], (DEPTH, D_MODEL))
    w_ple_gate = nrm(ks[17], (DEPTH, D_MODEL, D_MODEL), D_MODEL)
    w_ple = nrm(ks[18], (DEPTH, PLE_DIM, D_MODEL), PLE_DIM)
    g_final = gain(ks[19], (D_MODEL,))
    return {"x": x, "p": p, "g_mix": g_mix, "w_in": w_in, "conv4_w": conv4_w,
            "conv4_b": conv4_b, "w_rg_r": w_rg_r, "b_rg_r": b_rg_r, "w_rg_i": w_rg_i,
            "b_rg_i": b_rg_i, "lru_lambda": lru_lambda, "conv3_w": conv3_w, "w_out": w_out,
            "g_ffn": g_ffn, "w_gate_up": w_gate_up, "w_down": w_down, "g_ple": g_ple,
            "w_ple_gate": w_ple_gate, "w_ple": w_ple, "g_final": g_final}

def second_block(x, p, g_mix, w_in, conv4_w, conv4_b, w_rg_r, b_rg_r, w_rg_i, b_rg_i,
              lru_lambda, conv3_w, w_out, g_ffn, w_gate_up, w_down, g_ple, w_ple_gate,
              w_ple, g_final):
    for i in range(DEPTH):
        x = hybrid_layer(x, p[i], g_mix[i], w_in[i], conv4_w[i], conv4_b[i], w_rg_r[i],
                         b_rg_r[i], w_rg_i[i], b_rg_i[i], lru_lambda[i], conv3_w[i], w_out[i],
                         g_ffn[i], w_gate_up[i], w_down[i], g_ple[i], w_ple_gate[i], w_ple[i])
    return rmsnorm(x, g_final)


def setup_inputs(seed=0):
    out = dict(first_inputs(seed))
    for name, value in second_inputs(seed + 1).items():
        if name != "x":
            out[name + "_2"] = value
    return out


def reference(
    x, mem, positions, attn_norm_g, w_in, mla_q_norm_g, mla_w_uq, mla_kv_norm_g, mla_w_ukv,
    mla_q_qk_g, mla_k_qk_g, ret_gn_g, w_out, cross_norm_g, mem_norm_g, cross_w_q, cross_w_kv,
    cross_q_qk_g, cross_k_qk_g, cross_w_o, moe_norm_g, router_w_group, router_b_group,
    router_w_expert, router_b_expert, expert_w_gate, expert_w_up, expert_w_down, p_2, g_mix_2,
    w_in_2, conv4_w_2, conv4_b_2, w_rg_r_2, b_rg_r_2, w_rg_i_2, b_rg_i_2, lru_lambda_2,
    conv3_w_2, w_out_2, g_ffn_2, w_gate_up_2, w_down_2, g_ple_2, w_ple_gate_2, w_ple_2,
    g_final_2,
):
    x = first_block(
        x, mem, positions, attn_norm_g, w_in, mla_q_norm_g, mla_w_uq, mla_kv_norm_g, mla_w_ukv,
        mla_q_qk_g, mla_k_qk_g, ret_gn_g, w_out, cross_norm_g, mem_norm_g, cross_w_q,
        cross_w_kv, cross_q_qk_g, cross_k_qk_g, cross_w_o, moe_norm_g, router_w_group,
        router_b_group, router_w_expert, router_b_expert, expert_w_gate, expert_w_up,
        expert_w_down,
    )
    return second_block(
        x, p_2, g_mix_2, w_in_2, conv4_w_2, conv4_b_2, w_rg_r_2, b_rg_r_2, w_rg_i_2, b_rg_i_2,
        lru_lambda_2, conv3_w_2, w_out_2, g_ffn_2, w_gate_up_2, w_down_2, g_ple_2, w_ple_gate_2,
        w_ple_2, g_final_2,
    )


_drawn_inputs = setup_inputs


def setup_inputs(seed=0):
    import zlib

    import numpy as np

    out = dict(_drawn_inputs(seed))
    spreads = {}
    factors = {'mla_q_norm_g': 7.698,
     'mla_kv_norm_g': 8.0,
     'mla_q_qk_g': 8.0,
     'mla_k_qk_g': 8.0,
     'ret_gn_g': 12.741,
     'cross_norm_g': 8.0,
     'mem_norm_g': 4.609,
     'cross_q_qk_g': 4.7,
     'cross_k_qk_g': 5.085,
     'b_rg_r_2': 200.0,
     'b_rg_i_2': 200.0,
     'g_ple_2': 200.0,
     'moe_norm_g': 8.0,
     'router_b_group': 8.0,
     'router_b_expert': 8.0,
     'g_mix_2': 8.0,
     'conv4_b_2': 64.0,
     'w_rg_r_2': 64.0,
     'w_rg_i_2': 38.0,
     'lru_lambda_2': 50.064,
     'g_ffn_2': 47.667,
     'p_2': 8.0,
     'conv4_w_2': 8.0,
     'w_ple_gate_2': 8.0,
     'w_ple_2': 8.0}
    for name, (base, spread) in spreads.items():
        noise = np.random.default_rng([zlib.crc32(name.encode()), seed]).standard_normal(out[name].shape)
        drawn = base * np.exp(spread * noise) if base else spread * noise
        out[name] = __import__('jax').numpy.asarray(drawn.astype(out[name].dtype))
    for name, factor in factors.items():
        out[name] = (out[name] * factor).astype(out[name].dtype)
    return out
```

```python
from contextlib import ExitStack

import numpy as np

import concourse.bass as bass
from concourse import mybir

F32 = mybir.dt.float32
F32R = mybir.dt.float32r
I32 = mybir.dt.int32
ALU = mybir.AluOpType
ACT = mybir.ActivationFunctionType
AX = mybir.AxisListType.X

P = 128
D = 1024
T = 2
KD = D // P
EPS = 1e-6
SLOT = 2048
RING = 3
HEADS = 4
NOPE, ROPE, QK = 128, 64, 192
CROSS = 256
GROUPS, PER_GROUP = 4, 8
EXPERTS = GROUPS * PER_GROUP
FF = 256
D_FF = 2816
STEPS_FFN = D_FF // FF
RET = 128
NEG = -1e30
VEC_ROWS = (4 + 3 + 4) * KD


def constants():
    ident = np.eye(P, dtype=np.float32)
    i = np.arange(P)
    mask = np.zeros((P, 2 * P), np.float32)
    mask[:, P:] = np.where(i[None, :] <= i[:, None], 0.0, NEG)
    j, q = np.arange(P)[:, None], np.arange(2 * P)[None, :]
    decay = []
    for h in range(HEADS):
        g = np.log(1.0 - 2.0 ** (-5.0 - h))
        decay.append(np.where(q >= j, np.exp((q - j) * g), 0.0) * RET ** -0.5)
    decay = np.stack(decay, 1).reshape(P, -1)
    inv = [np.float32(10000.0) ** (-np.arange(n, dtype=np.float32) / np.float32(n)) for n in (ROPE // 2, RET // 2)]
    inv = np.broadcast_to(np.concatenate(inv), (P, 96))
    first = np.broadcast_to(np.arange(PER_GROUP, 0, -1), (P, PER_GROUP))
    return np.concatenate([ident, mask, decay, inv, first], 1).astype(np.float32)


MAGIC = 1.5 * 2.0 ** 23
PI_BELOW = 3.1415925
HEAD_LINKS = 15
CONST_COLS = P + 2 * P + HEADS * 2 * P + 96 + PER_GROUP


def two_pi_parts():
    left, parts = 2 * np.pi, []
    for _ in range(3):
        unit = 2.0 ** (np.floor(np.log2(left)) - 7)
        parts.append(float(np.floor(left / unit) * unit))
        left -= parts[-1]
    return parts + [float(np.float32(left))]


def build(nc, a, out):
    with ExitStack() as ctx:
        program(nc, a, out, ctx)


def program(nc, a, out, ctx):
    def sb(name, shape, dt=F32):
        return ctx.enter_context(nc.sbuf_tensor(name, shape, dt))

    sems = {}

    def sem(name):
        if name not in sems:
            sems[name] = ctx.enter_context(nc.semaphore(name))
        return sems[name]

    bank = [ctx.enter_context(nc.psum_tensor(f"bank{b}", [P, 512], F32)) for b in range(8)]

    stage = sb("stage", [P, RING, SLOT])
    w_hi = sb("w_hi", [P, RING, SLOT], F32R)
    w_lo = sb("w_lo", [P, RING, SLOT], F32R)
    x = sb("x", [P, T, D])
    xs = sb("xs", [P, T, D])
    xT_hi = sb("xT_hi", [P, KD, 2 * P], F32R)
    xT_lo = sb("xT_lo", [P, KD, 2 * P], F32R)
    aT_hi = sb("aT_hi", [P, 2, 2 * P], F32R)
    aT_lo = sb("aT_lo", [P, 2, 2 * P], F32R)
    cT_hi = sb("cT_hi", [P, 3, 2 * P], F32R)
    cT_lo = sb("cT_lo", [P, 3, 2 * P], F32R)
    const = sb("const", [P, CONST_COLS])
    ident = const[:, 0:P]
    mask = const[:, P:3 * P]
    decay = const[:, 3 * P:11 * P].rearrange("p (h q) -> p h q", h=HEADS)
    inv_freq = const[:, 11 * P:11 * P + 96]
    first_weight = const[:, 11 * P + 96:]
    norm_g = sb("norm_g", [P, 7, KD])
    MEM_G, ATTN_G, CROSS_G, MOE_G, MIX_G, FFN_G, PLE_G = range(7)
    qn_g = sb("qn_g", [P, 2])
    kvn_g = sb("kvn_g", [P, 1])
    nope_g = sb("nope_g", [P, 2])
    rope_g = sb("rope_g", [P, 2, ROPE])
    cqk_g = sb("cqk_g", [P, 2, 2])
    gn_g = sb("gn_g", [P, 512])
    r_bias = sb("r_bias", [P, GROUPS + EXPERTS])
    r_w = sb("r_w", [P, KD * (GROUPS + EXPERTS)])
    r_hi = sb("r_hi", [P, KD * (GROUPS + EXPERTS)], F32R)
    r_lo = sb("r_lo", [P, KD * (GROUPS + EXPERTS)], F32R)
    pos_i = sb("pos_i", [P, T], I32)
    pos_f = sb("pos_f", [P, T])
    trig = sb("trig", [P, 2, T, 96])
    vec_in = sb("vec_in", [VEC_ROWS, P])
    vec = sb("vec", [P, VEC_ROWS])
    conv4_w = vec[:, 0:4 * KD]
    conv3_w = vec[:, 4 * KD:7 * KD]
    conv4_b, half_br, half_bi, lam = (vec[:, (7 + n) * KD:(8 + n) * KD] for n in range(4))
    softplus2 = sb("softplus2", [P, KD])
    sums, inverse, rstd = (sb(n, [P, T]) for n in ("sums", "inverse", "rstd"))
    head_sums, head_inv, head_rstd = (sb(n, [P, 16]) for n in ("head_sums", "head_inv", "head_rstd"))
    lat_sums, lat_inv, lat_rstd = (sb(n, [P, 4]) for n in ("lat_sums", "lat_inv", "lat_rstd"))
    gn_stats = sb("gn_stats", [P, T * HEADS, 6])
    gn_mv = sb("gn_mv", [P, T * HEADS, 2])
    gn_inv, gn_rstd = sb("gn_inv", [P, T * HEADS]), sb("gn_rstd", [P, T * HEADS])
    top, neg_top, exp_sum, exp_inv = (sb(n, [P, 2 * T * HEADS]) for n in ("top", "neg_top", "exp_sum", "exp_inv"))
    logits = sb("logits", [P, T, GROUPS + EXPERTS])
    diffs = sb("diffs", [P, T, GROUPS + PER_GROUP])
    exps = sb("exps", [P, T, GROUPS + PER_GROUP])
    route = sb("route", [P, 9, T * EXPERTS])
    lam_t = sb("lam_t", [P, 6, KD])
    gates = sb("gates", [P, T, EXPERTS])
    half = sb("half", [P, 1])
    eps_col, warm = sb("eps_col", [P, 1]), sb("warm", [P, 1])
    hidden = sb("hidden", [P, T, FF])
    silu_t = sb("silu_t", [P, T, FF])
    silu_g = sb("silu_g", [P, T, FF])
    attention_memory = ExitStack()
    arena_words = 16896 + 384
    arena = attention_memory.enter_context(nc.sbuf_tensor("arena", [P, arena_words], F32))
    taken = [0]

    def part(words):
        at = taken[0]
        taken[0] += words
        assert taken[0] <= arena_words, taken[0]
        return arena[:, at:at + words]

    k_crossT = part(KD * 256).rearrange("p (j t) -> p j t", j=KD)
    v_cross = part(T * D).rearrange("p (t n) -> p t n", t=T)
    angle = v_cross.rearrange("p t n -> p (t n)")[:, 0:4 * T * 96].rearrange("p (s n) -> p s n", s=4)
    share1 = part(T * D)
    k_cross = share1.rearrange("p (t n) -> p t n", t=T)
    q_mla = share1[:, 0:T * 768].rearrange("p (t h d) -> p t h d", t=T, h=HEADS)
    scores = share1[:, 0:1536]
    q_cross = share1.rearrange("p (t n) -> p t n", t=T)
    share2 = part(2048)
    k_mla = share2[:, 0:1536].rearrange("p (t h d) -> p t h d", t=T, h=HEADS)
    probsT = share2[:, 0:1536]
    v_mla = part(T * 512).rearrange("p (t h d) -> p t h d", t=T, h=HEADS)
    latent = part(T * 448).rearrange("p (t n) -> p t n", t=T)
    r_q = part(T * 512)
    r_k = part(T * 512)
    r_v = part(T * 512).rearrange("p (t n) -> p t n", t=T)
    r_gate = r_q.rearrange("p (t n) -> p t n", t=T)
    r_s0 = r_q.rearrange("p (h q) -> p h q", h=HEADS)
    r_s1 = r_k[:, 0:512].rearrange("p (h q) -> p h q", h=HEADS)
    rot_q, rot_k = (xs[:, t] for t in range(T))
    turned = part(4096)
    r_qT, r_kT = (turned[:, n * 1024:(n + 1) * 1024].rearrange("p (h t) -> p h t", h=HEADS) for n in (0, 1))
    qT_n, qT_r, kT_n, kT_r = (turned[:, n * 1024:(n + 1) * 1024].rearrange("p (h t) -> p h t", h=HEADS) for n in range(4))
    q_crossT = turned[:, 0:2048].rearrange("p (j t) -> p j t", j=KD)
    c_scores = share1.rearrange("p (t h m) -> p t h m", t=T, h=HEADS)
    c_probsT = share2.rearrange("p (t h m) -> p t h m", t=T, h=HEADS)
    qk_r = [xs[:, :, 256 * w:256 * w + 256].rearrange("p t (h d) -> p t h d", h=HEADS) for w in (0, 1)]

    attention_memory.close()

    recurrent_memory = ExitStack()

    def rb(name, shape, dt=F32):
        return recurrent_memory.enter_context(nc.sbuf_tensor(name, shape, dt))

    xpad = rb("xpad", [P, 2, 259])
    cpad = rb("cpad", [P, 2, 258])
    y_sq, y_in, y_tanh, c_in, q_inv, decay_a, u_in, states, gr_tanh, gc_tanh, merged = (
        rb(n, [P, 512]) for n in ("y_sq", "y_in", "y_tanh", "c_in", "q_inv", "decay_a", "u_in", "states", "gr_tanh",
                                  "gc_tanh", "merged"))
    rx, conv3, r_tanh, tau, i_tanh, root_tau = (
        rb(n, [P, 2, 256]) for n in ("rx", "conv3", "r_tanh", "tau", "i_tanh", "root_tau"))
    rx_hi, rx_lo = rb("rx_hi", [P, 512], F32R), rb("rx_lo", [P, 512], F32R)
    mT_hi, mT_lo = rb("mT_hi", [P, KD, 2 * P], F32R), rb("mT_lo", [P, KD, 2 * P], F32R)
    recurrent_memory.close()

    embed, ple_gate = sb("embed", [P, T, D]), sb("ple_gate", [P, T, D])
    fin_g = sb("fin_g", [P, D])
    p_in = sb("p_in", [P, T, 256])

    def columns(w, c0, n, h):
        return w.rearrange("(p k) n -> p k n", k=KD)[:, 4 * h:4 * h + 4, c0:c0 + n], 4 * n

    w_in, w_kv = a["w_in"][0], a["cross_w_kv"][0]
    before = []
    for c in range(4):
        before += [columns(w_kv, 512 * c, 512, h) for h in range(2)]
    U_LAT = len(before)
    before += [columns(w_in, 0, 448, h) for h in range(2)]
    U_RQ = len(before)
    for c in range(3):
        before += [columns(w_in, 448 + 512 * c, 512, h) for h in range(2)]
    U_RK, U_RV, U_UQ = U_RQ + 2, U_RQ + 4, U_RQ + 6
    before.append((a["mla_w_uq"][0].rearrange("(p k) n -> p (k n)", k=2), 1536))
    before.append((a["mla_w_ukv"][0], 1024))
    U_UKV, U_RG = U_UQ + 1, U_UQ + 2
    before += [columns(w_in, 448 + 512 * 3, 512, h) for h in range(2)]
    U_OUT = len(before)
    U_CQ, U_CO = U_OUT + 4, U_OUT + 8
    for w in ("w_out", "cross_w_q", "cross_w_o"):
        for c in range(2):
            before += [columns(a[w][0], 512 * c, 512, h) for h in range(2)]
    U_MOE = len(before)
    U_HEADS = U_MOE + 3 * EXPERTS
    UNITS_HEAD = 9
    U_OUT2 = U_HEADS + UNITS_HEAD * HEADS
    U_FFN = U_OUT2 + 4
    U_PLE = U_FFN + 3 * STEPS_FFN
    U_END = U_PLE + 5
    middle = []
    for c in range(2):
        for h in range(2):
            middle.append((a["w_out_2"][0].rearrange("(k p) n -> p k n", k=KD)[:, 4 * h:4 * h + 4, 512 * c:512 * c + 512], 2048))
    last = [(a["w_ple_2"][0].rearrange("(p k) n -> p (k n)", k=2), 2048)]
    for c in range(2):
        last += [columns(a["w_ple_gate_2"][0], 512 * c, 512, h) for h in range(2)]

    def cols_of(u):
        if u < U_MOE:
            return before[u][1]
        return 2048

    def count(u0, per=0, i=0):
        return i * per + u0 if per else u0

    def slot_uses(u0, per=0, i=0):
        return i * (16 * per // RING) + 16 * (u0 // RING + 1) if per else 16 * (u0 // RING + 1)

    landed = [sem(f"weights_landed{s}") for s in range(RING)]
    hi_ready, lo_ready, unit_done = sem("w_hi_ready"), sem("w_lo_ready"), sem("unit_done")

    def load_unit(sp, src, cols, u0, per=0, i=0):
        if u0 >= RING:
            sp.wait_ge(hi_ready, count(u0 - RING + 1, per, i))
            sp.wait_ge(lo_ready, count(u0 - RING + 1, per, i))
        s = u0 % RING
        dst = stage[:, s, 0:cols]
        if len(src.shape) == 3:
            dst = dst.rearrange("p (k n) -> p k n", k=src.shape[1])
        sp.dma_start(dst, src).then_inc(landed[s], 16)

    def split_hi(act, cols, u0, per=0, i=0):
        s = u0 % RING
        act.wait_ge(landed[s], slot_uses(u0, per, i))
        if u0 >= RING:
            act.wait_ge(unit_done, count(u0 - RING + 1, per, i))
        nc.scalar.activation(w_hi[:, s, 0:cols], stage[:, s, 0:cols], ACT.Copy).then_inc(hi_ready, 1)

    def split_lo(dve, cols, u0, per=0, i=0):
        s = u0 % RING
        dve.wait_ge(hi_ready, count(u0 + 1, per, i))
        nc.vector.tensor_tensor(w_lo[:, s, 0:cols], stage[:, s, 0:cols], w_hi[:, s, 0:cols].bitcast(F32),
                                ALU.subtract).then_inc(lo_ready, 1)

    products = ([f"mem{n}" for n in range(4)] + ["vec"] + [f"kc{n}" for n in range(4)]
                + [f"attn{n}" for n in range(4)]
                + ["cq", "ckv", "rq0", "rq1", "rk0", "rk1", "rs0", "rs1", "rs2", "ro0", "ro1"]
                + [f"{w}{n}" for w in ("qn", "qr", "kn", "kr") for n in (0, 1)]
                + ["s0", "s1", "s2", "pT0", "pT1", "pT2", "o0", "o1"]
                + [f"cat{n}" for n in range(4)] + [f"crossq{n}" for n in range(4)]
                + [f"{w}{n}" for w in ("qc", "cs", "cp", "co") for n in range(4)]
                + [f"catc{n}" for n in range(4)] + [f"moe{n}" for n in range(4)] + ["router"]
                + [f"mix{n}" for n in range(4)] + [f"ffn{n}" for n in range(4)]
                + ["pT"] + [f"ple{n}" for n in range(4)])
    where = {name: (4 + n % 4, n // 4) for n, name in enumerate(products)}
    filled = [sem(f"bank{b}_filled") for b in range(4, 8)]
    freed = [sem(f"bank{b}_freed") for b in range(4, 8)]

    def to_fill(pe, name):
        b, g = where[name]
        if g:
            pe.wait_ge(freed[b - 4], g)
        return bank[b]

    def fills(ins, name):
        ins.then_inc(filled[where[name][0] - 4], 1)

    def product(eng, name):
        b, g = where[name]
        eng.wait_ge(filled[b - 4], g + 1)
        return bank[b]

    def frees(ins, name):
        ins.then_inc(freed[where[name][0] - 4], 1)

    def been_read(eng, name):
        b, g = where[name]
        eng.wait_ge(freed[b - 4], g + 1)

    def row(v):
        return v.rearrange("(o n) -> o n", o=1)

    first_loads = [(ident, a["const"][:, 0:P]),
                   (norm_g[:, MEM_G], a["mem_norm_g"][0].rearrange("(p k) -> p k", k=KD))]
    small_loads = [(const[:, P:], a["const"][:, P:])]
    for n, g in enumerate(("mem_norm_g", "attn_norm_g", "cross_norm_g", "moe_norm_g", "g_mix_2", "g_ffn_2", "g_ple_2")):
        if n != MEM_G:
            small_loads.append((norm_g[:, n], a[g][0].rearrange("(p k) -> p k", k=KD)))
    small_loads += [
        (vec_in[0:4 * KD], a["conv4_w_2"][0].rearrange("w (k p) -> (w k) p", p=P)),
        (vec_in[4 * KD:7 * KD], a["conv3_w_2"][0].rearrange("w (k p) -> (w k) p", p=P)),
        (vec_in[7 * KD:8 * KD], a["conv4_b_2"][0].rearrange("(k p) -> k p", p=P)),
        (vec_in[8 * KD:9 * KD], a["b_rg_r_2"][0].rearrange("h (k p) -> (h k) p", p=P)),
        (vec_in[9 * KD:10 * KD], a["b_rg_i_2"][0].rearrange("h (k p) -> (h k) p", p=P)),
        (vec_in[10 * KD:11 * KD], a["lru_lambda_2"][0].rearrange("(k p) -> k p", p=P)),
        (qn_g[:], a["mla_q_norm_g"][0].rearrange("(p k) -> p k", k=2)),
        (kvn_g[:], a["mla_kv_norm_g"][0].rearrange("(p k) -> p k", k=1)),
        (gn_g[:], a["ret_gn_g"].to_broadcast([P, 512])),
        (r_bias[:, 0:GROUPS], a["router_b_group"].to_broadcast([P, GROUPS])),
        (r_bias[:, GROUPS:], a["router_b_expert"].to_broadcast([P, EXPERTS])),
        (r_w[:, 0:KD * GROUPS], a["router_w_group"][0].rearrange("(p k) n -> p (k n)", k=KD)),
        (r_w[:, KD * GROUPS:], a["router_w_expert"][0].rearrange("(p k) n -> p (k n)", k=KD)),
    ]
    for n, g in enumerate(("mla_q_qk_g", "mla_k_qk_g")):
        small_loads.append((nope_g[:, n:n + 1], a[g][0, 0:NOPE].rearrange("(p k) -> p k", k=1)))
        small_loads.append((rope_g[:, n], a[g][:, NOPE:QK].to_broadcast([P, ROPE])))
    for n, g in enumerate(("cross_q_qk_g", "cross_k_qk_g")):
        for k in range(2):
            small_loads.append((cqk_g[:, n, k:k + 1], a[g][0, P * k:P * k + P].rearrange("(p k) -> p k", k=1)))
    for t in range(T):
        small_loads.append((pos_i[:, t:t + 1], a["positions"][0, P * t:P * t + P].rearrange("(p k) -> p k", k=1)))

    chunk_freed = [sem("pair0_freed"), sem("pair1_freed")]
    (C_K, C_V, C_LAT, C_RQ, C_RK, C_RV, C_UQ, C_UKV, C_RG, C_OUT, C_CQ, C_CO, C_OUT2, C_PLE, C_GATE) = (
        0, 2, 4, 5, 6, 7, 8, 10, 12, 13, 15, 17, 19, 21, 23)

    def pair(c):
        return bank[2 * (c % 2):2 * (c % 2) + 2]

    signalled = [c for c in range(C_GATE + 2) if not (C_OUT <= c < C_CQ or C_CO <= c < C_PLE)]

    def chunk_read(eng, c):
        eng.wait_ge(chunk_freed[c % 2], sum(d % 2 == c % 2 for d in signalled if d <= c))

    def flat3(v):
        return v.rearrange("p k t -> p (k t)")

    def copy_half(eng, name, j, dst, scale):
        b = product(eng, name)
        return nc.scalar.activation(dst, b[:, 256 * j:256 * j + 256], ACT.Copy, scale=scale)

    def up_done(base, e):
        return base + 2 if isinstance(e, int) and e == 0 else e * 3 + (base + 1)

    def routing(dve, then):
        tt, ts, stt = nc.vector.tensor_tensor, nc.vector.tensor_scalar, nc.vector.scalar_tensor_tensor

        def scratch(n, width):
            return route[:, n, 0:T * width].rearrange("p (t e) -> p t e", t=T)

        def over(v, n):
            return v.to_broadcast([P, T, n])

        def largest(dst, src):
            then(nc.vector.tensor_reduce(dst.rearrange("p t o -> p (t o)"), src, AX, ALU.max))

        def total(dst, src):
            then(nc.vector.tensor_reduce(dst.rearrange("p t o -> p (t o)"), src, AX, ALU.add))

        def first_of_largest(dst, src, best, n):
            weight = first_weight[:, 0:n].unsqueeze(1).to_broadcast([P, T, n])
            largest(best, src)
            then(tt(dst, src, over(best, n), ALU.is_equal))
            then(tt(dst, dst, weight, ALU.mult))
            largest(best, dst)
            then(tt(dst, dst, over(best, n), ALU.is_equal))

        def pick(dst, src, wide):
            then(tt(wide, src, group_hot.unsqueeze(3).to_broadcast([P, T, GROUPS, PER_GROUP]), ALU.mult))
            then(nc.vector.tensor_reduce(dst, wide.rearrange("p t g e -> p t e g"), AX, ALU.add))

        been_read(dve, "router")
        g_logit = logits[:, :, 0:GROUPS]
        e_logit = logits[:, :, GROUPS:].rearrange("p t (g e) -> p t g e", g=GROUPS)
        best = scratch(0, 1)
        biased, group_hot = scratch(1, GROUPS), scratch(2, GROUPS)
        largest(best, g_logit)
        then(tt(diffs[:, :, 0:GROUPS], g_logit, over(best, GROUPS), ALU.subtract))
        then(tt(biased, g_logit, r_bias[:, 0:GROUPS].unsqueeze(1).to_broadcast([P, T, GROUPS]), ALU.add))
        first_of_largest(group_hot, biased, best, GROUPS)
        wide_ = route[:, 3].rearrange("p (t g e) -> p t g e", t=T, g=GROUPS)
        mine, bias = scratch(4, PER_GROUP), scratch(5, PER_GROUP)
        pick(mine, e_logit, wide_)
        pick(bias, r_bias[:, GROUPS:].rearrange("p (g e) -> p g e", g=GROUPS).unsqueeze(1).to_broadcast([P, T, GROUPS, PER_GROUP]), wide_)
        largest(best, mine)
        tt(diffs[:, :, GROUPS:], mine, over(best, PER_GROUP), ALU.subtract).then_inc(sem("route_diffs"), 1)
        dve.wait_ge(sem("route_diffs"), 1)
        then(tt(bias, bias, mine, ALU.add))
        hot1, hot2 = scratch(6, PER_GROUP), scratch(7, PER_GROUP)
        first_of_largest(hot1, bias, best, PER_GROUP)
        then(stt(bias, hot1, -3e38, bias, ALU.mult, ALU.add))
        first_of_largest(hot2, bias, best, PER_GROUP)
        then(tt(hot1, hot1, hot2, ALU.add))
        dve.wait_ge(sem("route_exps"), 1)
        ge, ee = exps[:, :, 0:GROUPS], exps[:, :, GROUPS:]
        total(best, ge)
        then(nc.vector.reciprocal(best, best))
        then(tt(ge, ge, over(best, GROUPS), ALU.mult))
        then(tt(ge, ge, group_hot, ALU.mult))
        g_weight = scratch(8, 1)
        total(g_weight, ge)
        total(best, ee)
        then(nc.vector.reciprocal(best, best))
        then(tt(ee, ee, over(best, PER_GROUP), ALU.mult))
        then(tt(ee, ee, hot1, ALU.mult))
        total(best, ee)
        then(nc.vector.reciprocal(best, best))
        then(tt(ee, ee, over(best, PER_GROUP), ALU.mult))
        then(tt(ee, ee, over(g_weight, PER_GROUP), ALU.mult))
        then(ts(ee, ee, 0.5, None, ALU.mult))
        then(tt(gates[:].rearrange("p t (g e) -> p t g e", g=GROUPS), ee.unsqueeze(2).to_broadcast([P, T, GROUPS, PER_GROUP]),
                group_hot.unsqueeze(3).to_broadcast([P, T, GROUPS, PER_GROUP]), ALU.mult))

    block = ctx.enter_context(nc.Block())

    @block.sync
    def _(sp):
        for t in range(T):
            sp.dma_start(xs[:, t], a["mem"][0, P * t:P * t + P]).then_inc(sem(f"mem_loaded{t}"), 16)
        load_unit(sp, *before[0], 0)
        load_unit(sp, *before[1], 1)
        sp.dma_start(x[:], a["x"][0].rearrange("(t p) d -> p t d", p=P)).then_inc(sem("x_loaded"), 16)
        for u in range(2, U_MOE):
            load_unit(sp, *before[u], u)

        def swiglu_loads(gate_of, up_of, down_of, base, steps):
            load_unit(sp, gate_of(0), 2048, base)
            load_unit(sp, up_of(0), 2048, base + 1)
            with sp.Fori(0, steps - 1) as i:
                load_unit(sp, gate_of(i + 1), 2048, base + 2, 3, i)
                load_unit(sp, up_of(i + 1), 2048, base + 3, 3, i)
                load_unit(sp, down_of(i), 2048, base + 4, 3, i)
            load_unit(sp, down_of(steps - 1), 2048, base + 3 * steps - 1)

        def expert(w, k):
            rows = a[w][0].rearrange("e (p k) n -> e p (k n)", k=k)
            return lambda e: rows[bass.ds(e, 1)].rearrange("e p n -> p (e n)")

        swiglu_loads(expert("expert_w_gate", KD), expert("expert_w_up", KD), expert("expert_w_down", 2), U_MOE, EXPERTS)

        w_in2 = a["w_in_2"][0].rearrange("(p k) n -> p k n", k=KD)
        rg = [a[w][0].rearrange("h (k p) n -> h p k n", k=2) for w in ("w_rg_r_2", "w_rg_i_2")]
        with sp.Fori(0, HEADS) as h:
            for j, group in enumerate((0, 1, 3, 4, 2)):
                load_unit(sp, w_in2[:, :, bass.ds(h * 256 + group * D, 256)], 2048, U_HEADS + j, UNITS_HEAD, h)
            for j in range(2):
                src = rg[j][bass.ds(h, 1)].rearrange("h p k n -> p (h k) n")
                load_unit(sp, src, 512, U_HEADS + 5 + j, UNITS_HEAD, h)
            for j, group in enumerate((5, 6)):
                load_unit(sp, w_in2[:, :, bass.ds(h * 256 + group * D, 256)], 2048, U_HEADS + 7 + j, UNITS_HEAD, h)
        for n, unit in enumerate(middle):
            load_unit(sp, *unit, U_OUT2 + n)

        gu2 = a["w_gate_up_2"][0].rearrange("(p k) n -> p k n", k=KD)
        down2 = a["w_down_2"][0].rearrange("(c p k) n -> c p (k n)", k=2, p=P)
        swiglu_loads(lambda c: gu2[:, :, bass.ds(c * FF, FF)], lambda c: gu2[:, :, bass.ds(c * FF + D_FF, FF)],
                     lambda c: down2[bass.ds(c, 1)].rearrange("c p n -> p (c n)"), U_FFN, STEPS_FFN)
        for n, unit in enumerate(last):
            load_unit(sp, *unit, U_PLE + n)
        for t in range(T):
            sp.wait_ge(sem("result"), t + 1)
            sp.dma_start(out[0].rearrange("(t p) d -> p t d", p=P)[:, t], xs[:, t]).then_inc(sem("stored"), 16)
        sp.wait_ge(sem("stored"), 16 * T)

    @block.gpsimd
    def _(pool):
        nc.gpsimd.memset(eps_col[:], 1.0)
        nc.gpsimd.memset(half[:], 0.5).then_inc(sem("half_set"), 1)
        pool.wait_ge(sem("x_rnn"), 2)
        pool.dma_start(fin_g[:], row(a["g_final_2"]).to_broadcast([P, D])).then_inc(sem("last_loaded"), 16)
        pool.dma_start(p_in[:], a["p_2"][0, 0].rearrange("(t p) n -> p t n", p=P)).then_inc(sem("last_loaded"), 16)

    @block.scalar
    def _(act):
        for dst, src in first_loads:
            act.dma_start(dst, src).then_inc(sem("first_loaded"), 16)
        for dst, src in small_loads:
            act.dma_start(dst, src).then_inc(sem("constants_loaded"), 16)

        chain = [0]

        def then(ins):
            chain[0] += 1
            ins.then_inc(sem("act_chain"), 1)
            act.wait_ge(sem("act_chain"), chain[0])

        split = [0]

        def splits_to(u):
            while split[0] < u:
                split_hi(act, cols_of(split[0]), split[0])
                split[0] += 1

        def root(dst, src, inverse_ready, n=1):
            act.wait_ge(sem(inverse_ready), n)
            return nc.scalar.activation(dst, src, ACT.Sqrt)

        def warm_up(func):
            then(nc.scalar.activation(warm[:], eps_col[:], func))

        def scaled(src, junk, ready, name):
            warm_up(ACT.Sqrt)
            for s_, n in ready:
                act.wait_ge(sem(s_), n)
            nc.scalar.activation(junk[:, 0], src[:, 0], ACT.Square, accum_out=sums[:, 0:1]).then_inc(sem(name + "_sums"), 1)
            root(rstd[:], inverse[:], name + "_inverse").then_inc(sem(name + "_rstd"), 1)
            act.wait_ge(sem(name + "_rstd"), 1)
            if name != "final":
                nc.scalar.activation(xs[:, 0], src[:, 0], ACT.Copy, scale=rstd[:, 0:1]).then_inc(sem(name + "_scaled"), 1)

        def high_parts(name, gain):
            for n in range(4):
                b = product(act, f"{name}{n}")
                if gain is None:
                    ins = nc.scalar.activation(xT_hi[:, 2 * n:2 * n + 2].rearrange("p k t -> p (k t)"), b[:, :], ACT.Copy)
                else:
                    for j in range(2):
                        k = 2 * n + j
                        ins = nc.scalar.activation(xT_hi[:, k], b[:, 256 * j:256 * j + 256], ACT.Copy, scale=norm_g[:, gain, k:k + 1])
                ins.then_inc(sem(name + "_hi"), 1)

        def norm(src, ready, name, gain):
            scaled(src, xs, ready, name)
            high_parts(name, gain)

        def head_squares(src_of, n, width, name):
            for m in range(n):
                ins = nc.scalar.activation(flat3(hidden[:])[:, 0:width], src_of(m), ACT.Square, accum_out=head_sums[:, m:m + 1])
                if m < n - 1:
                    then(ins)
            ins.then_inc(sem(name + "_sums"), 1)

        def copy_to(dst, name, rows=P, **kw):
            b = product(act, name)
            n = int(np.prod(dst.shape[1:]))
            src = b[0:rows, 0:n]
            if len(dst.shape) == 3:
                src = src.rearrange("p (k n) -> p k n", k=dst.shape[1])
            return nc.scalar.activation(dst, src, ACT.Copy, **kw)

        act.wait_ge(sem("half_set"), 1)
        scaled(xs, k_cross, [("mem_loaded0", 16)], "mem")
        splits_to(1)
        act.wait_ge(sem("first_loaded"), 16 * len(first_loads))
        high_parts("mem", MEM_G)
        splits_to(2)
        act.wait_ge(sem("constants_loaded"), 16 * len(small_loads))
        frees(copy_to(vec[:], "vec"), "vec")
        act.wait_ge(sem("angles"), 1)
        nc.scalar.activation(trig[:, 1].rearrange("p t n -> p (t n)"), angle[:, 0], ACT.Sin)
        nc.scalar.activation(angle[:, 1], angle[:, 0], ACT.Abs).then_inc(sem("angles_abs"), 1)
        act.wait_ge(sem("angles_turned"), 1)
        nc.scalar.activation(trig[:, 0].rearrange("p t n -> p (t n)"), angle[:, 2], ACT.Sin).then_inc(sem("trig"), 1)
        been_read(act, "vec")
        then(nc.scalar.activation(lam_t[:, 0], lam, ACT.Abs))
        nc.scalar.activation(lam_t[:, 1], lam_t[:, 0], ACT.Exp, scale=-1.0).then_inc(sem("lambda_exp"), 1)
        nc.scalar.activation(r_hi[:], r_w[:], ACT.Copy).then_inc(sem("router_hi"), 1)

        for c in range(2):
            splits_to(2 * c + 4)
            act.wait_ge(unit_done, 2 * c + 2)
            for t in range(T):
                ins = nc.scalar.activation(k_cross[:, t, 512 * c:512 * c + 512], pair(C_K + c)[t][:, :], ACT.Copy)
            ins.then_inc(chunk_freed[(C_K + c) % 2], 1)
        chunk_read(act, C_K)
        chunk_read(act, C_K + 1)
        head_squares(lambda m: k_cross[:, m // 4, 256 * (m % 4):256 * (m % 4) + 256], 8, 256, "kc")
        root(head_rstd[:, 0:8], head_inv[:, 0:8], "kc_inverse").then_inc(sem("kc_rstd"), 1)
        for c in range(2):
            splits_to(2 * c + 8)
            act.wait_ge(unit_done, 2 * c + 6)
            for t in range(T):
                ins = nc.scalar.activation(v_cross[:, t, 512 * c:512 * c + 512], pair(C_V + c)[t][:, :], ACT.Copy)
            ins.then_inc(chunk_freed[(C_V + c) % 2], 1)
        splits_to(U_LAT + 2)
        scaled(x, xs, [("x_loaded", 16)], "attn")
        for n in range(4):
            for j in range(2):
                ins = copy_half(act, f"kc{n}", j, k_crossT[:, 2 * n + j], cqk_g[:, 1, j:j + 1])
            frees(ins, f"kc{n}")
        high_parts("attn", ATTN_G)

        splits_to(U_LAT + 4)
        act.wait_ge(unit_done, U_LAT + 2)
        for t in range(T):
            ins = nc.scalar.activation(latent[:, t], pair(C_LAT)[t][:, 0:448], ACT.Copy)
        ins.then_inc(chunk_freed[C_LAT % 2], 1)
        chunk_read(act, C_LAT)
        for m in range(4):
            src = latent[:, m % 2, 0:256] if m < 2 else latent[:, m % 2, 256:384]
            ins = nc.scalar.activation(hidden[:, 0, 0:src.shape[1]], src, ACT.Square, accum_out=lat_sums[:, m:m + 1])
            if m < 3:
                then(ins)
        ins.then_inc(sem("lat_sums"), 1)
        root(lat_rstd[:], lat_inv[:], "lat_inverse").then_inc(sem("lat_rstd"), 1)

        def wide_copy(c, u, dst, name=None):
            act.wait_ge(unit_done, u + 1)
            for t in range(T):
                ins = nc.scalar.activation(dst[:, t], pair(c)[t][:, :], ACT.Copy)
            ins.then_inc(chunk_freed[c % 2], 1)

        splits_to(U_RK + 2)
        wide_copy(C_RQ, U_RQ + 1, r_q.rearrange("p (t n) -> p t n", t=T))
        for k in range(2):
            ins = copy_half(act, "cq", k, cT_hi[:, k], qn_g[:, k:k + 1])
        ins.then_inc(sem("cT_hi"), 1)
        copy_half(act, "ckv", 0, cT_hi[:, 2], kvn_g[:, 0:1]).then_inc(sem("cT_hi"), 1)
        splits_to(U_RV + 2)
        wide_copy(C_RK, U_RK + 1, r_k.rearrange("p (t n) -> p t n", t=T))
        splits_to(U_UKV + 1)
        wide_copy(C_RV, U_RV + 1, r_v)
        splits_to(U_RG + 1)
        for n in range(2):
            frees(copy_to(r_qT[:, 2 * n:2 * n + 2], f"rq{n}"), f"rq{n}")
        for n in range(2):
            frees(copy_to(r_kT[:, 2 * n:2 * n + 2], f"rk{n}"), f"rk{n}")
        act.wait_ge(unit_done, U_UQ + 1)
        for c in range(2):
            for t in range(T):
                ins = nc.scalar.activation(q_mla[:, t, 2 * c:2 * c + 2].rearrange("p h d -> p (h d)"),
                                           pair(C_UQ + c)[t][:, 0:384], ACT.Copy)
            ins.then_inc(chunk_freed[(C_UQ + c) % 2], 1)
        splits_to(U_RG + 2)
        act.wait_ge(unit_done, U_UKV + 1)
        for c in range(2):
            for t in range(T):
                src = pair(C_UKV + c)[t][:, :].rearrange("p (h w d) -> p h w d", h=2, w=2)
                nc.scalar.activation(k_mla[:, t, 2 * c:2 * c + 2, 0:NOPE], src[:, :, 0], ACT.Copy)
                ins = nc.scalar.activation(v_mla[:, t, 2 * c:2 * c + 2], src[:, :, 1], ACT.Copy)
            ins.then_inc(chunk_freed[(C_UKV + c) % 2], 1)
        chunk_read(act, C_UKV)
        chunk_read(act, C_UKV + 1)
        act.wait_ge(sem("k_pe_placed"), 1)
        head_squares(lambda m: (q_mla if m < 8 else k_mla)[:, m // 4 % 2, m % 4], 16, QK, "qk")
        root(head_rstd[:], head_inv[:], "qk_inverse").then_inc(sem("qk_rstd"), 1)
        root(gn_rstd[:], gn_inv[:], "gn_inverse").then_inc(sem("gn_rstd"), 1)
        splits_to(U_OUT + 2)
        act.wait_ge(unit_done, U_RG + 2)
        for t in range(T):
            nc.scalar.activation(r_gate[:, t], pair(C_RG)[t][:, :], ACT.Tanh, scale=0.5).then_inc(sem("rg_tanh"), 1)
        for w, dst, dst_r in ((0, qT_n, qT_r), (1, kT_n, kT_r)):
            for n in range(2):
                name = ("qn", "kn")[w] + str(n)
                frees(copy_to(dst[:, 2 * n:2 * n + 2], name, scale=nope_g[:, w:w + 1]), name)
            for n in range(2):
                name = ("qr", "kr")[w] + str(n)
                frees(copy_to(dst_r[0:ROPE, 2 * n:2 * n + 2], name, rows=ROPE), name)
        act.wait_ge(sem("masked"), 1)
        for m in range(8):
            part_ = scores[:, 128 * m:128 * m + 128] if m < 4 else scores[:, 512 + 256 * (m - 4):768 + 256 * (m - 4)]
            nc.scalar.activation(part_, part_, ACT.Exp, bias=neg_top[:, m:m + 1], scale=QK ** -0.5,
                                 accum_out=exp_sum[:, m:m + 1]).then_inc(sem("exped"), 1)
        for n in range(3):
            frees(copy_to(probsT[:, 512 * n:512 * n + 512], f"pT{n}"), f"pT{n}")
        high_parts("cat", None)
        splits_to(U_CQ + 2)

        norm(x, [("x_attn", 2)], "crossq", CROSS_G)
        for c in range(2):
            splits_to(U_CQ + 2 * c + 4)
            wide_copy(C_CQ + c, U_CQ + 2 * c + 1, q_cross[:, :, 512 * c:512 * c + 512])
        chunk_read(act, C_CQ)
        chunk_read(act, C_CQ + 1)
        head_squares(lambda m: q_cross[:, m // 4, 256 * (m % 4):256 * (m % 4) + 256], 8, 256, "qc")
        root(head_rstd[:, 0:8], head_inv[:, 0:8], "qc_inverse").then_inc(sem("qc_rstd"), 1)
        for n in range(4):
            for j in range(2):
                ins = copy_half(act, f"qc{n}", j, q_crossT[:, 2 * n + j], cqk_g[:, 0, j:j + 1])
            frees(ins, f"qc{n}")
        for n in range(4):
            t, pair_of = n // 2, n % 2
            act.wait_ge(sem("cross_top"), n + 1)
            b = bank[where[f"cs{n}"][0]]
            for j in range(2):
                m = 2 * n + j
                ins = nc.scalar.activation(c_scores[:, t, 2 * pair_of + j], b[:, 256 * j:256 * j + 256], ACT.Exp,
                                           bias=neg_top[:, m:m + 1], scale=CROSS ** -0.5, accum_out=exp_sum[:, m:m + 1])
            frees(ins, f"cs{n}")
        for n in range(4):
            frees(copy_to(c_probsT[:, n // 2, 2 * (n % 2):2 * (n % 2) + 2], f"cp{n}"), f"cp{n}")
        high_parts("catc", None)
        splits_to(U_MOE + 2)
        norm(x, [("x_cross", 2)], "moe", MOE_G)
        b = product(act, "router")
        frees(nc.scalar.activation(logits[:], b[:, 0:P].rearrange("p (t n) -> p t n", t=T)[:, :, 0:GROUPS + EXPERTS], ACT.Copy), "router")
        act.wait_ge(sem("route_diffs"), 1)
        nc.scalar.activation(exps[:], diffs[:], ACT.Exp).then_inc(sem("route_exps"), 1)

        def swiglu(name, base, steps):
            def tanhs(e):
                act.wait_ge(unit_done, up_done(base, e))
                for t in range(T):
                    nc.scalar.activation(silu_t[:, t], bank[4 + t][:, 0:FF], ACT.Tanh, scale=0.5).then_inc(sem(name + "_tanh"), 1)

            def high(e):
                act.wait_ge(sem(name + "_turned"), e + 1)
                nc.scalar.activation(aT_hi[:].rearrange("p k t -> p (k t)"), bank[6][:, :], ACT.Copy).then_inc(sem(name + "_aT_hi"), 1)

            def step(i, first=False):
                if not first:
                    split_hi(act, SLOT, base + 1, 3, i)
                split_hi(act, SLOT, base + 2, 3, i)
                tanhs(i)
                split_hi(act, SLOT, base + 3, 3, i)
                high(i)

            step(0, first=True)
            with act.Fori(1, steps - 1) as i:
                step(i)
            split_hi(act, SLOT, base + 1 + 3 * (steps - 1))
            tanhs(steps - 1)
            high(steps - 1)
            split_hi(act, SLOT, base + 3 * steps - 1)

        swiglu("moe", U_MOE, EXPERTS)
        split[0] = U_HEADS
        splits_to(U_HEADS + 2)
        norm(x, [("x_moe", 4)], "mix", MIX_G)

        with act.Fori(0, HEADS) as h:
            def unit(j):
                split_hi(act, 512 if j in (5, 6) else SLOT, U_HEADS + j, UNITS_HEAD, h)

            def done(j):
                act.wait_ge(unit_done, h * UNITS_HEAD + (U_HEADS + j + 1))

            def blocks(b):
                return b[:, :].rearrange("p (f t) -> p f t", f=2)

            unit(2)
            done(0)
            nc.scalar.activation(xpad[:, :, 3:259], blocks(bank[0]), ACT.Copy).then_inc(sem("rx_copied"), 1)
            unit(3)
            done(1)
            nc.scalar.activation(y_sq[:], bank[1][:, :], ACT.Square)
            nc.scalar.activation(y_in[:], bank[1][:, :], ACT.Copy).then_inc(sem("y_copied"), 1)
            act.wait_ge(sem("conv4_done"), h + 1)
            nc.scalar.activation(rx_hi[:], rx[:].rearrange("p f t -> p (f t)"), ACT.Copy).then_inc(sem("rx_hi"), 1)
            unit(4)
            done(2)
            nc.scalar.activation(c_in[:], bank[2][:, :], ACT.Copy).then_inc(sem("c_copied"), 1)
            act.wait_ge(sem("gelu_inner"), h + 1)
            nc.scalar.activation(y_tanh[:], y_sq[:], ACT.Tanh, scale=float(np.sqrt(2 / np.pi))).then_inc(sem("gelu_tanh"), 1)
            unit(5)
            unit(6)
            unit(7)
            unit(8)
            for f in range(2):
                nc.scalar.activation(r_tanh[:, f], blocks(bank[7])[:, f], ACT.Tanh, scale=0.5,
                                     bias=half_br[:, bass.ds(h * 2 + f, 1)]).then_inc(sem("r_tanh"), 1)
            act.wait_ge(sem("r_tanh"), h * 2 + 2)
            for f in range(2):
                nc.scalar.activation(tau[:, f], r_tanh[:, f], ACT.Tanh, scale=softplus2[:, bass.ds(h * 2 + f, 1)],
                                     bias=softplus2[:, bass.ds(h * 2 + f, 1)]).then_inc(sem("tau"), 1)
            done(6)
            for f in range(2):
                nc.scalar.activation(i_tanh[:, f], blocks(bank[0])[:, f], ACT.Tanh, scale=0.5,
                                     bias=half_bi[:, bass.ds(h * 2 + f, 1)]).then_inc(sem("i_tanh"), 1)
            split_hi(act, SLOT, U_HEADS + 9, UNITS_HEAD, h)
            act.wait_ge(sem("tau"), h * 2 + 2)
            nc.scalar.activation(root_tau[:], tau[:], ACT.Sqrt).then_inc(sem("root_tau"), 1)
            split_hi(act, SLOT, U_HEADS + 10, UNITS_HEAD, h)
            done(7)
            nc.scalar.activation(gr_tanh[:], bank[5][:, :], ACT.Tanh, scale=0.5).then_inc(sem("gr_tanh"), 1)
            done(8)
            nc.scalar.activation(gc_tanh[:], bank[6][:, :], ACT.Tanh, scale=0.5).then_inc(sem("gc_tanh"), 1)
            act.wait_ge(sem("merged"), h + 1)
            nc.scalar.activation(flat3(mT_hi[:])[:, bass.ds(h * 512, 512)], merged[:], ACT.Copy, scale=0.5).then_inc(sem("mT_hi"), 1)

        split[0] = U_OUT2 + 2
        splits_to(U_FFN + 2)
        norm(x, [("x_rnn", 2)], "ffn", FFN_G)
        swiglu("ffn", U_FFN, STEPS_FFN)
        split[0] = U_PLE
        splits_to(U_PLE + 2)
        copy_to(aT_hi[:], "pT").then_inc(sem("pT_hi"), 1)
        norm(x, [("x_ffn", 4)], "ple", PLE_G)
        act.wait_ge(unit_done, U_PLE + 1)
        for c in range(2):
            for t in range(T):
                ins = nc.scalar.activation(embed[:, t, 512 * c:512 * c + 512], pair(C_PLE + c)[t][:, :], ACT.Copy)
            ins.then_inc(chunk_freed[(C_PLE + c) % 2], 1)
        for c in range(2):
            splits_to(min(U_END, U_PLE + 2 * c + 5))
            act.wait_ge(unit_done, U_PLE + 2 * c + 3)
            for t in range(T):
                ins = nc.scalar.activation(ple_gate[:, t, 512 * c:512 * c + 512], pair(C_GATE + c)[t][:, :], ACT.Tanh, scale=0.5)
            ins.then_inc(chunk_freed[(C_GATE + c) % 2], 1)
        scaled(x, xs, [("x_ple", 2)], "final")

    @block.vector
    def _(dve):
        chain = [0]

        def then(ins):
            chain[0] += 1
            ins.then_inc(sem("dve_chain"), 1)
            dve.wait_ge(sem("dve_chain"), chain[0])

        split = [0]

        def splits_to(u):
            while split[0] < u:
                split_lo(dve, cols_of(split[0]), split[0])
                split[0] += 1

        tt, ts, stt = nc.vector.tensor_tensor, nc.vector.tensor_scalar, nc.vector.scalar_tensor_tensor

        def inverse_of(dst, src, width, ready, n, signal):
            dve.wait_ge(sem(ready), n)
            then(ts(dst, src, 1.0 / width, EPS, ALU.mult, ALU.add))
            nc.vector.reciprocal(dst, dst).then_inc(sem(signal), 1)

        def low_half(name, j, lo, hi, gain):
            b = bank[where[name][0]]
            return stt(lo, b[:, 256 * j:256 * j + 256], gain, hi.bitcast(F32), ALU.mult, ALU.subtract)

        def low_parts(name, gain):
            for n in range(4):
                dve.wait_ge(sem(name + "_hi"), n + 1)
                b = bank[where[f"{name}{n}"][0]]
                if gain is None:
                    ins = tt(flat3(xT_lo[:, 2 * n:2 * n + 2]), b[:, :], flat3(xT_hi[:, 2 * n:2 * n + 2]).bitcast(F32), ALU.subtract)
                else:
                    for j in range(2):
                        k = 2 * n + j
                        ins = low_half(f"{name}{n}", j, xT_lo[:, k], xT_hi[:, k], norm_g[:, gain, k:k + 1])
                frees(ins, f"{name}{n}")

        def scaled(src, junk, ready, name):
            for s_, n in ready:
                dve.wait_ge(sem(s_), n)
            then(nc.vector.tensor_tensor_reduce(junk[:, 1], src[:, 1], src[:, 1], 1.0, 0.0, ALU.mult, ALU.add, sums[:, 1:2]))
            inverse_of(inverse[:], sums[:], D, name + "_sums", 1, name + "_inverse")
            dve.wait_ge(sem(name + "_rstd"), 1)
            if name != "final":
                ts(xs[:, 1], src[:, 1], rstd[:, 1:2], None, ALU.mult).then_inc(sem(name + "_scaled"), 1)

        def norm(ready, name, gain):
            scaled(x, xs, ready, name)
            low_parts(name, gain)

        def rope(src, dst, lo, hi, ta, tb):
            n = hi - lo
            cos, sin = (trig[:, w, :, lo:hi].unsqueeze(2).to_broadcast([P, T, HEADS, n]) for w in (0, 1))
            x1, x2 = src[:, :, :, 0:n], src[:, :, :, n:2 * n]
            tt(dst[:, :, :, 0:n], x1, cos, ALU.mult)
            tt(ta, x2, sin, ALU.mult)
            tt(dst[:, :, :, n:2 * n], x2, cos, ALU.mult)
            then(tt(tb, x1, sin, ALU.mult))
            tt(dst[:, :, :, 0:n], dst[:, :, :, 0:n], ta, ALU.subtract)
            return tt(dst[:, :, :, n:2 * n], dst[:, :, :, n:2 * n], tb, ALU.add)

        def heads4(v, d):
            return v.rearrange("p (t h d) -> p t h d", t=T, d=d)

        tmp_a, tmp_b = silu_t[:].rearrange("p t f -> p (t f)"), silu_g[:].rearrange("p t f -> p (t f)")

        scaled(xs, k_cross, [("mem_loaded1", 16)], "mem")
        splits_to(1)
        dve.wait_ge(sem("first_loaded"), 16 * len(first_loads))
        low_parts("mem", MEM_G)
        splits_to(2)
        dve.wait_ge(sem("constants_loaded"), 16 * len(small_loads))
        then(nc.vector.tensor_copy(pos_f[:], pos_i[:]))
        for t in range(T):
            ins = ts(angle[:, 0, 96 * t:96 * t + 96], inv_freq, pos_f[:, t:t + 1], None, ALU.mult)
        then(ins)
        then(ts(angle[:, 3], angle[:, 0], float(np.float32(1 / (2 * np.pi))), MAGIC, ALU.mult, ALU.add))
        then(ts(angle[:, 3], angle[:, 3], MAGIC, None, ALU.subtract))
        for piece in two_pi_parts():
            then(stt(angle[:, 0], angle[:, 3], -piece, angle[:, 0], ALU.mult, ALU.add))
        ts(angle[:, 0], angle[:, 0], PI_BELOW, -PI_BELOW, ALU.min, ALU.max).then_inc(sem("angles"), 1)
        dve.wait_ge(sem("angles_abs"), 1)
        ts(angle[:, 2], angle[:, 1], -1.0, float(np.float32(np.pi / 2)), ALU.mult, ALU.add).then_inc(sem("angles_turned"), 1)
        dve.wait_ge(sem("lambda_exp"), 1)
        y, z, w, s = (lam_t[:, n] for n in (1, 2, 3, 4))
        then(ts(z, y, 2.0, None, ALU.add))
        then(nc.vector.reciprocal(z, z))
        then(tt(z, z, y, ALU.mult))
        then(tt(w, z, z, ALU.mult))
        then(ts(s, w, 1.0 / 19, None, ALU.mult))
        for n in range(8, 0, -1):
            then(stt(s, s, 1.0 / (2 * n + 1), w, ALU.add, ALU.mult))
        then(stt(s, s, 1.0, z, ALU.add, ALU.mult))
        then(ts(softplus2[:], lam, -1.0, 0.0, ALU.mult, ALU.max))
        then(stt(softplus2[:], s, 2.0, softplus2[:], ALU.mult, ALU.add))
        then(ts(softplus2[:], softplus2[:], 2.0, None, ALU.mult))
        ts(half_br, half_br, 0.5, None, ALU.mult)
        then(ts(half_bi, half_bi, 0.5, None, ALU.mult))
        dve.wait_ge(sem("router_hi"), 1)
        tt(r_lo[:], r_w[:], r_hi[:].bitcast(F32), ALU.subtract).then_inc(sem("router_lo"), 1)

        splits_to(6)
        inverse_of(head_inv[:, 0:8], head_sums[:, 0:8], CROSS, "kc_sums", 1, "kc_inverse")
        dve.wait_ge(sem("kc_rstd"), 1)
        for m in range(8):
            part_ = k_cross[:, m // 4, 256 * (m % 4):256 * (m % 4) + 256]
            ins = ts(part_, part_, head_rstd[:, m:m + 1], None, ALU.mult)
        ins.then_inc(sem("kc_scaled"), 1)
        splits_to(U_LAT + 2)
        norm([("x_loaded", 16)], "attn", ATTN_G)

        splits_to(U_LAT + 4)
        dve.wait_ge(sem("lat_sums"), 1)
        ts(lat_inv[:, 0:2], lat_sums[:, 0:2], 1.0 / 256, EPS, ALU.mult, ALU.add)
        then(ts(lat_inv[:, 2:4], lat_sums[:, 2:4], 1.0 / 128, EPS, ALU.mult, ALU.add))
        nc.vector.reciprocal(lat_inv[:], lat_inv[:]).then_inc(sem("lat_inverse"), 1)
        dve.wait_ge(sem("lat_rstd"), 1)
        for t in range(T):
            ts(latent[:, t, 0:256], latent[:, t, 0:256], lat_rstd[:, t:t + 1], None, ALU.mult)
            ins = ts(latent[:, t, 256:384], latent[:, t, 256:384], lat_rstd[:, 2 + t:3 + t], None, ALU.mult)
        ins.then_inc(sem("lat_scaled"), 1)
        splits_to(U_RK + 2)
        dve.wait_ge(sem("cT_hi"), 1)
        for k in range(2):
            ins = low_half("cq", k, cT_lo[:, k], cT_hi[:, k], qn_g[:, k:k + 1])
        frees(ins, "cq")
        dve.wait_ge(sem("cT_hi"), 2)
        frees(low_half("ckv", 0, cT_lo[:, 2], cT_hi[:, 2], kvn_g[:, 0:1]), "ckv")
        dve.wait_ge(sem("trig"), 1)
        chunk_read(dve, C_RQ)
        rope(heads4(r_q, 128), heads4(rot_q, 128), 32, 96, heads4(tmp_a, 64), heads4(tmp_b, 64)).then_inc(sem("rot_ready"), 1)
        dve.wait_ge(sem("rot_ready"), 1)
        splits_to(U_RV + 2)
        chunk_read(dve, C_RK)
        rope(heads4(r_k, 128), heads4(rot_k, 128), 32, 96, heads4(tmp_a, 64), heads4(tmp_b, 64)).then_inc(sem("rot_ready"), 1)
        dve.wait_ge(sem("rot_ready"), 2)
        splits_to(U_RG + 1)
        nc.vector.tensor_copy(k_mla[:, :, :, NOPE:QK], latent[:, :, 384:448].unsqueeze(2).to_broadcast([P, T, HEADS, ROPE]))\
            .then_inc(sem("k_pe_placed"), 1)
        splits_to(U_RG + 2)
        for n in range(2):
            b = product(dve, f"rs{n}")
            frees(tt(r_s0[:, 2 * n:2 * n + 2], b[:, :].rearrange("p (h q) -> p h q", h=2), decay[:, 2 * n:2 * n + 2], ALU.mult), f"rs{n}")
        b = product(dve, "rs2")
        frees(tt(r_s1, b[:, :].rearrange("p (h q) -> p h q", h=HEADS), decay[:, :, 0:P], ALU.mult), "rs2")
        inverse_of(head_inv[:], head_sums[:], QK, "qk_sums", 1, "qk_inverse")
        for t in range(T):
            b = product(dve, f"ro{t}")
            for h in range(HEADS):
                ins = nc.vector.bn_stats(gn_stats[:, 4 * t + h], b[:, 128 * h:128 * h + 128])
        then(ins)
        for m in range(T * HEADS):
            ins = nc.vector.bn_aggr(gn_mv[:, m], gn_stats[:, m])
        then(ins)
        then(ts(gn_inv[:], gn_mv[:, :, 1], EPS, None, ALU.add))
        nc.vector.reciprocal(gn_inv[:], gn_inv[:]).then_inc(sem("gn_inverse"), 1)
        dve.wait_ge(sem("qk_rstd"), 1)
        for w, v in enumerate((q_mla, k_mla)):
            for m in range(8):
                part_ = v[:, m // 4, m % 4]
                ins = ts(part_, part_, head_rstd[:, 8 * w + m:8 * w + m + 1], None, ALU.mult)
        ins.then_inc(sem("qk_scaled"), 1)
        dve.wait_ge(sem("qk_scaled"), 1)
        for w, v in enumerate((q_mla, k_mla)):
            positions = v[:, :, :, NOPE:QK]
            gain = rope_g[:, w].unsqueeze(1).unsqueeze(1).to_broadcast([P, T, HEADS, ROPE])
            then(tt(positions, positions, gain, ALU.mult))
            rope(positions, qk_r[w], 0, 32, heads4(tmp_a[:, 0:256], 32), heads4(tmp_b[:, 0:256], 32)).then_inc(sem("qk_turned"), 1)
            dve.wait_ge(sem("qk_turned"), w + 1)
        dve.wait_ge(sem("gn_rstd"), 1)
        for t in range(T):
            b = bank[where[f"ro{t}"][0]]
            for h in range(HEADS):
                m = 4 * t + h
                ins = ts(xs[:, t, 512 + 128 * h:640 + 128 * h], b[:, 128 * h:128 * h + 128], gn_mv[:, m, 0:1],
                         gn_rstd[:, m:m + 1], ALU.subtract, ALU.mult)
            frees(ins, f"ro{t}")
        splits_to(U_OUT + 2)
        been_read(dve, "ro1")
        for t in range(T):
            stt(xs[:, t, 512:1024], xs[:, t, 512:1024], 0.5, gn_g[:], ALU.mult, ALU.mult).then_inc(sem("gn_gained"), 1)
        for t in range(T):
            dve.wait_ge(sem("rg_tanh"), t + 1)
            ins = stt(r_gate[:, t], r_gate[:, t], 1.0, pair(C_RG)[t][:, :], ALU.add, ALU.mult)
        ins.then_inc(chunk_freed[C_RG % 2], 1)
        chunk_read(dve, C_RG)
        for t in range(T):
            tt(xs[:, t, 512:1024], xs[:, t, 512:1024], r_gate[:, t], ALU.mult).then_inc(sem("cat_scaled"), 1)
        b = product(dve, "s0")
        frees(tt(scores[:, 0:512].rearrange("p (h k) -> p h k", h=HEADS), b[:, :].rearrange("p (h k) -> p h k", h=HEADS),
                 mask[:, P:].unsqueeze(1).to_broadcast([P, HEADS, P]), ALU.add), "s0")
        for n in (1, 2):
            b = product(dve, f"s{n}")
            frees(tt(scores[:, 512 * n:512 * n + 512].rearrange("p (h k) -> p h k", h=2), b[:, :].rearrange("p (h k) -> p h k", h=2),
                     mask.unsqueeze(1).to_broadcast([P, 2, 2 * P]), ALU.add), f"s{n}")
        for n in range(3):
            been_read(dve, f"s{n}")
        nc.vector.tensor_reduce(top[:, 0:4], scores[:, 0:512].rearrange("p (h k) -> p h k", h=4), AX, ALU.max)
        then(nc.vector.tensor_reduce(top[:, 4:8], scores[:, 512:1536].rearrange("p (h k) -> p h k", h=4), AX, ALU.max))
        ts(neg_top[:, 0:8], top[:, 0:8], -(QK ** -0.5), None, ALU.mult).then_inc(sem("masked"), 1)
        dve.wait_ge(sem("exped"), 8)
        then(nc.vector.reciprocal(exp_inv[:, 0:8], exp_sum[:, 0:8]))
        for t in range(T):
            b = product(dve, f"o{t}")
            ins = tt(xs[:, t, 0:512].rearrange("p (h d) -> p h d", h=HEADS), b[:, :].rearrange("p (h d) -> p h d", h=HEADS),
                     exp_inv[:, 4 * t:4 * t + 4].unsqueeze(2).to_broadcast([P, HEADS, P]), ALU.mult)
            frees(ins, f"o{t}")
        low_parts("cat", None)
        splits_to(U_CQ + 2)

        def add_chunks(chunk, u, signal):
            for c in range(2):
                dve.wait_ge(unit_done, u + 2 * c + 2)
                for t in range(T):
                    dst = x[:, t, 512 * c:512 * c + 512]
                    ins = tt(dst, dst, pair(chunk + c)[t][:, :], ALU.add)
                ins.then_inc(sem(signal), 1)

        add_chunks(C_OUT, U_OUT, "x_attn")
        norm([("x_attn", 2)], "crossq", CROSS_G)
        splits_to(U_CQ + 6)
        inverse_of(head_inv[:, 0:8], head_sums[:, 0:8], CROSS, "qc_sums", 1, "qc_inverse")
        dve.wait_ge(sem("qc_rstd"), 1)
        for m in range(8):
            part_ = q_cross[:, m // 4, 256 * (m % 4):256 * (m % 4) + 256]
            ins = ts(part_, part_, head_rstd[:, m:m + 1], None, ALU.mult)
        ins.then_inc(sem("qc_scaled"), 1)
        for n in range(4):
            b = product(dve, f"cs{n}")
            then(nc.vector.tensor_reduce(top[:, 2 * n:2 * n + 2], b[:, :].rearrange("p (h k) -> p h k", h=2), AX, ALU.max))
            ts(neg_top[:, 2 * n:2 * n + 2], top[:, 2 * n:2 * n + 2], -(CROSS ** -0.5), None, ALU.mult).then_inc(sem("cross_top"), 1)
        for n in range(4):
            been_read(dve, f"cs{n}")
        then(nc.vector.reciprocal(exp_inv[:, 0:8], exp_sum[:, 0:8]))
        for n in range(4):
            t, pair_of = n // 2, n % 2
            b = product(dve, f"co{n}")
            ins = tt(xs[:, t, 512 * pair_of:512 * pair_of + 512].rearrange("p (h d) -> p h d", h=2),
                     b[:, :].rearrange("p (h d) -> p h d", h=2),
                     exp_inv[:, 2 * n:2 * n + 2].unsqueeze(2).to_broadcast([P, 2, CROSS]), ALU.mult)
            frees(ins, f"co{n}")
        low_parts("catc", None)
        splits_to(U_MOE + 2)
        add_chunks(C_CO, U_CO, "x_cross")
        norm([("x_cross", 2)], "moe", MOE_G)
        routing(dve, then)

        def swiglu(name, base, steps, gate_of):
            def hiddens(e):
                for t in range(T):
                    dve.wait_ge(sem(name + "_tanh"), e * 2 + (t + 1))
                    stt(silu_g[:, t], silu_t[:, t], 1.0, bank[4 + t][:, 0:FF], ALU.add, ALU.mult).then_inc(sem(name + "_silu"), 1)
                for t in range(T):
                    dve.wait_ge(sem(name + "_silu"), e * 2 + (t + 1))
                    stt(hidden[:, t], bank[4 + t][:, FF:2 * FF], gate_of(t, e), silu_g[:, t], ALU.mult, ALU.mult)\
                        .then_inc(sem(name + "_hidden"), 1)

            def low(e):
                dve.wait_ge(sem(name + "_aT_hi"), e + 1)
                tt(flat3(aT_lo[:]), bank[6][:, :], flat3(aT_hi[:]).bitcast(F32), ALU.subtract).then_inc(sem(name + "_aT_lo"), 1)

            def step(i, first=False):
                if not first:
                    split_lo(dve, SLOT, base + 1, 3, i)
                split_lo(dve, SLOT, base + 2, 3, i)
                hiddens(i)
                split_lo(dve, SLOT, base + 3, 3, i)
                low(i)

            step(0, first=True)
            with dve.Fori(1, steps - 1) as i:
                step(i)
            split_lo(dve, SLOT, base + 1 + 3 * (steps - 1))
            hiddens(steps - 1)
            low(steps - 1)
            split_lo(dve, SLOT, base + 3 * steps - 1)

        def add_down(last_unit, signal):
            dve.wait_ge(unit_done, last_unit + 1)
            for n in range(4):
                dst = x[:, n % 2, 512 * (n // 2):512 * (n // 2) + 512]
                tt(dst, dst, bank[n][:, :], ALU.add).then_inc(sem(signal), 1)

        swiglu("moe", U_MOE, EXPERTS, lambda t, e: gates[:, t, bass.ds(e, 1)])
        split[0] = U_HEADS
        splits_to(U_HEADS + 2)
        add_down(U_HEADS - 1, "x_moe")
        norm([("x_moe", 4)], "mix", MIX_G)
        nc.vector.memset(xpad[:, :, 0:3], 0.0)
        nc.vector.memset(cpad[:, :, 0:2], 0.0).then_inc(sem("padded"), 1)
        dve.wait_ge(sem("padded"), 1)

        with dve.Fori(0, HEADS) as h:
            links = [0]

            def link(ins):
                links[0] += 1
                ins.then_inc(sem("head_chain"), 1)
                dve.wait_ge(sem("head_chain"), h * HEAD_LINKS + links[0])

            def unit(j):
                split_lo(dve, 512 if j in (5, 6) else SLOT, U_HEADS + j, UNITS_HEAD, h)

            def done(j):
                dve.wait_ge(unit_done, h * UNITS_HEAD + (U_HEADS + j + 1))

            def col(v, tap, f):
                return v[:, bass.ds(h * 2 + (tap * KD + f), 1)]

            unit(2)
            dve.wait_ge(sem("rx_copied"), h + 1)
            for f in range(2):
                ins = ts(rx[:, f], xpad[:, f, 0:256], col(conv4_w, 0, f), col(conv4_b, 0, f), ALU.mult, ALU.add)
            for tap in range(1, 4):
                link(ins)
                for f in range(2):
                    ins = stt(rx[:, f], xpad[:, f, tap:tap + 256], col(conv4_w, tap, f), rx[:, f], ALU.mult, ALU.add)
            ins.then_inc(sem("conv4_done"), 1)
            unit(3)
            dve.wait_ge(sem("y_copied"), h + 1)
            link(ts(y_sq[:], y_sq[:], 0.044715, 1.0, ALU.mult, ALU.add))
            tt(y_sq[:], y_sq[:], y_in[:], ALU.mult).then_inc(sem("gelu_inner"), 1)
            dve.wait_ge(sem("rx_hi"), h + 1)
            tt(rx_lo[:], rx[:].rearrange("p f t -> p (f t)"), rx_hi[:].bitcast(F32), ALU.subtract).then_inc(sem("rx_lo"), 1)
            unit(4)
            unit(5)
            dve.wait_ge(sem("gelu_tanh"), h + 1)
            link(stt(y_in[:], y_tanh[:], 1.0, y_in[:], ALU.add, ALU.mult))
            dve.wait_ge(sem("c_copied"), h + 1)
            done(3)
            tt(cpad[:, :, 2:258], bank[3][:, :].rearrange("p (f t) -> p f t", f=2),
               c_in[:].rearrange("p (f t) -> p f t", f=2), ALU.mult).then_inc(sem("cx_read"), 1)
            dve.wait_ge(sem("cx_read"), h + 1)
            for f in range(2):
                ins = ts(conv3[:, f], cpad[:, f, 0:256], col(conv3_w, 0, f), None, ALU.mult)
            for tap in range(1, 3):
                link(ins)
                for f in range(2):
                    ins = stt(conv3[:, f], cpad[:, f, tap:tap + 256], col(conv3_w, tap, f), conv3[:, f], ALU.mult, ALU.add)
            link(ins)
            unit(6)
            done(4)
            y_conv = conv3[:].rearrange("p f t -> p (f t)")
            tt(y_conv, bank[4][:, :], y_conv, ALU.mult).then_inc(sem("b_read"), 1)
            unit(7)
            unit(8)
            split_lo(dve, SLOT, U_HEADS + 9, UNITS_HEAD, h)
            dve.wait_ge(sem("tau"), h * 2 + 2)
            tf = tau[:].rearrange("p f t -> p (f t)")
            link(ts(q_inv[:], tf, 1.0, None, ALU.add))
            link(nc.vector.reciprocal(q_inv[:], q_inv[:]))
            ts(decay_a[:], q_inv[:], 2.0, -1.0, ALU.mult, ALU.add)
            dve.wait_ge(sem("i_tanh"), h * 2 + 2)
            stt(u_in[:], i_tanh[:].rearrange("p f t -> p (f t)"), 1.0, rx[:].rearrange("p f t -> p (f t)"), ALU.add, ALU.mult)
            dve.wait_ge(sem("root_tau"), h + 1)
            link(tt(q_inv[:], root_tau[:].rearrange("p f t -> p (f t)"), q_inv[:], ALU.mult))
            link(tt(u_in[:], u_in[:], q_inv[:], ALU.mult))
            for f in range(2):
                ins = nc.vector.tensor_tensor_scan(states[:, 256 * f:256 * f + 256], decay_a[:, 256 * f:256 * f + 256],
                                                   u_in[:, 256 * f:256 * f + 256], 0.0, ALU.mult, ALU.add)
            link(ins)
            link(tt(y_in[:], y_in[:], states[:], ALU.mult))
            split_lo(dve, SLOT, U_HEADS + 10, UNITS_HEAD, h)
            dve.wait_ge(sem("gr_tanh"), h + 1)
            stt(y_in[:], gr_tanh[:], 1.0, y_in[:], ALU.add, ALU.mult)
            dve.wait_ge(sem("gc_tanh"), h + 1)
            link(stt(y_conv, gc_tanh[:], 1.0, y_conv, ALU.add, ALU.mult))
            stt(merged[:], y_in[:], 0.5, y_conv, ALU.mult, ALU.add).then_inc(sem("merged"), 1)
            dve.wait_ge(sem("mT_hi"), h + 1)
            stt(flat3(mT_lo[:])[:, bass.ds(h * 512, 512)], merged[:], 0.5,
                flat3(mT_hi[:])[:, bass.ds(h * 512, 512)].bitcast(F32), ALU.mult, ALU.subtract).then_inc(sem("mT_lo"), 1)
            assert links[0] == HEAD_LINKS, links[0]

        split[0] = U_OUT2 + 2
        splits_to(U_FFN + 2)
        add_chunks(C_OUT2, U_OUT2, "x_rnn")
        norm([("x_rnn", 2)], "ffn", FFN_G)
        dve.wait_ge(sem("half_set"), 1)
        swiglu("ffn", U_FFN, STEPS_FFN, lambda t, e: half[:, 0:1])
        split[0] = U_PLE
        splits_to(U_PLE + 2)
        dve.wait_ge(sem("pT_hi"), 1)
        frees(tt(flat3(aT_lo[:]), bank[where["pT"][0]][:, :], flat3(aT_hi[:]).bitcast(F32), ALU.subtract), "pT")
        add_down(U_PLE - 1, "x_ffn")
        norm([("x_ffn", 4)], "ple", PLE_G)
        for c in range(2):
            splits_to(min(U_END, U_PLE + 2 * c + 5))
            chunk_read(dve, C_GATE + c)
            g, e = ple_gate[:, :, 512 * c:512 * c + 512], embed[:, :, 512 * c:512 * c + 512]
            then(stt(g, g, 1.0, e, ALU.add, ALU.mult))
            dst = x[:, :, 512 * c:512 * c + 512]
            stt(dst, g, 0.5, dst, ALU.mult, ALU.add).then_inc(sem("x_ple"), 1)
        scaled(x, xs, [("x_ple", 2)], "final")
        dve.wait_ge(sem("last_loaded"), 32)
        for t in range(T):
            stt(xs[:, t], x[:, t], rstd[:, t:t + 1], fin_g[:], ALU.mult, ALU.mult).then_inc(sem("result"), 1)

    @block.tensor
    def _(pe):
        mm = nc.tensor.matmul

        def three(o, k_hi, k_lo, v_hi, v_lo, start, stop):
            mm(o, k_hi, v_hi, start=start, stop=False)
            mm(o, k_hi, v_lo, start=False, stop=False)
            return mm(o, k_lo, v_hi, start=False, stop=stop)

        def transpose(o, src):
            return nc.tensor.transpose(o, src, ident)

        def chunk_free(c):
            if c >= 2:
                chunk_read(pe, c - 2)

        def wide_unit(u, c, h, cols, th, tl, xt=None):
            s = u % RING
            pe.wait_ge(lo_ready, u + 1)
            for k in range(4):
                if xt is not None and k % 2 == 0:
                    been_read(pe, f"{xt}{2 * h + k // 2}")
                for t in range(T):
                    kk, at = 4 * h + k, cols * k
                    ins = three(pair(c)[t][:, 0:cols], th[:, kk, P * t:P * t + P], tl[:, kk, P * t:P * t + P],
                                w_hi[:, s, at:at + cols], w_lo[:, s, at:at + cols], start=kk == 0, stop=kk == KD - 1)
            ins.then_inc(unit_done, 1)

        def wide(c, u, cols=512, xt=None, th=xT_hi, tl=xT_lo, free=True):
            if free:
                chunk_free(c)
            for h in range(2):
                wide_unit(u + h, c, h, cols, th, tl, xt)

        def turn_xs(name, waits):
            for s, n in waits:
                pe.wait_ge(sem(s), n)
            view = xs[:].rearrange("p t (q k) -> p t k q", k=KD)
            for n in range(4):
                b = to_fill(pe, f"{name}{n}")
                for j in range(2):
                    for t in range(T):
                        ins = transpose(b[:, 256 * j + P * t:256 * j + P * t + P], view[:, t, 2 * n + j])
                fills(ins, f"{name}{n}")

        def turn_tiles(name, src_of, n=2):
            for i in range(n):
                b = to_fill(pe, f"{name}{i}")
                for j in range(2):
                    for t in range(T):
                        src = src_of(2 * i + j, t)
                        ins = transpose(b[0:src.shape[1], 256 * j + P * t:256 * j + P * t + P], src)
                fills(ins, f"{name}{i}")

        pe.wait_ge(sem("first_loaded"), 16 * len(first_loads))
        turn_xs("mem", [("mem_scaled", T)])
        pe.wait_ge(sem("constants_loaded"), 16 * len(small_loads))
        b = to_fill(pe, "vec")
        fills(nc.tensor.transpose(b[:, 0:VEC_ROWS], vec_in[:], ident[0:VEC_ROWS, 0:VEC_ROWS]), "vec")
        for c in range(4):
            wide(C_K + c, 2 * c, xt="mem")
        pe.wait_ge(sem("kc_scaled"), 1)
        turn_tiles("kc", lambda j, t: k_cross[:, t, P * j:P * j + P], 4)
        turn_xs("attn", [("attn_scaled", T)])
        wide(C_LAT, U_LAT, 448, xt="attn")
        wide(C_RQ, U_RQ)
        pe.wait_ge(sem("lat_scaled"), 1)
        b = to_fill(pe, "cq")
        for k in range(2):
            for t in range(T):
                ins = transpose(b[:, 256 * k + P * t:256 * k + P * t + P],
                                latent[:, t, 0:256].rearrange("p (q k) -> p k q", k=2)[:, k])
        fills(ins, "cq")
        b = to_fill(pe, "ckv")
        for t in range(T):
            ins = transpose(b[:, P * t:P * t + P], latent[:, t, 256:384])
        fills(ins, "ckv")
        wide(C_RK, U_RK)
        wide(C_RV, U_RV)
        been_read(pe, "cq")
        pe.wait_ge(lo_ready, U_UQ + 1)
        s = U_UQ % RING
        for c in range(2):
            chunk_free(C_UQ + c)
            for k in range(2):
                for t in range(T):
                    at = 768 * k + 384 * c
                    ins = three(pair(C_UQ + c)[t][:, 0:384], cT_hi[:, k, P * t:P * t + P], cT_lo[:, k, P * t:P * t + P],
                                w_hi[:, s, at:at + 384], w_lo[:, s, at:at + 384], start=k == 0, stop=k == 1)
        ins.then_inc(unit_done, 1)
        pe.wait_ge(sem("rot_ready"), 2)
        turn_tiles("rq", lambda h, t: rot_q.rearrange("p (t h d) -> p t h d", t=T, h=HEADS)[:, t, h])
        turn_tiles("rk", lambda h, t: rot_k.rearrange("p (t h d) -> p t h d", t=T, h=HEADS)[:, t, h])
        been_read(pe, "ckv")
        pe.wait_ge(lo_ready, U_UKV + 1)
        s = U_UKV % RING
        for c in range(2):
            chunk_free(C_UKV + c)
            for t in range(T):
                ins = three(pair(C_UKV + c)[t][:, :], cT_hi[:, 2, P * t:P * t + P], cT_lo[:, 2, P * t:P * t + P],
                            w_hi[:, s, 512 * c:512 * c + 512], w_lo[:, s, 512 * c:512 * c + 512], start=True, stop=True)
        ins.then_inc(unit_done, 1)
        for n in range(2):
            been_read(pe, f"rq{n}")
            been_read(pe, f"rk{n}")
        for n in range(2):
            b = to_fill(pe, f"rs{n}")
            for j in range(2):
                h = 2 * n + j
                ins = mm(b[:, 256 * j:256 * j + 256], r_kT[:, h, 0:P], r_qT[:, h, :], start=True, stop=True)
            fills(ins, f"rs{n}")
        b = to_fill(pe, "rs2")
        for h in range(HEADS):
            ins = mm(b[:, P * h:P * h + P], r_kT[:, h, P:2 * P], r_qT[:, h, P:2 * P], start=True, stop=True)
        fills(ins, "rs2")
        chunk_free(C_RG)
        wide_unit(U_RG, C_RG, 0, 512, xT_hi, xT_lo)
        for n in range(3):
            been_read(pe, f"rs{n}")
        for t in range(T):
            b = to_fill(pe, f"ro{t}")
            for h in range(HEADS):
                o = b[:, P * h:P * h + P]
                ins = mm(o, r_s0[:, h, P * t:P * t + P], r_v[:, 0, P * h:P * h + P], start=True, stop=t == 0)
                if t:
                    ins = mm(o, r_s1[:, h], r_v[:, 1, P * h:P * h + P], start=False, stop=True)
            fills(ins, f"ro{t}")
        wide_unit(U_RG + 1, C_RG, 1, 512, xT_hi, xT_lo)
        for w, v in enumerate((q_mla, k_mla)):
            pe.wait_ge(sem("qk_turned"), w + 1)
            turn_tiles("qk"[w] + "n", lambda h, t: v[:, t, h, 0:NOPE])
            turn_tiles("qk"[w] + "r", lambda h, t: qk_r[w][:, t, h])
        for name in ("qn", "qr", "kn", "kr"):
            for n in range(2):
                been_read(pe, f"{name}{n}")

        def score(o, h, q, keys):
            mm(o, qT_n[:, h, q], kT_n[:, h, keys], start=True, stop=False)
            return mm(o, qT_r[0:ROPE, h, q], kT_r[0:ROPE, h, keys], start=False, stop=True)

        b = to_fill(pe, "s0")
        for h in range(HEADS):
            ins = score(b[:, P * h:P * h + P], h, slice(0, P), slice(0, P))
        fills(ins, "s0")
        for n in (1, 2):
            b = to_fill(pe, f"s{n}")
            for j in range(2):
                ins = score(b[:, 256 * j:256 * j + 256], 2 * (n - 1) + j, slice(P, 2 * P), slice(0, 2 * P))
            fills(ins, f"s{n}")
        pe.wait_ge(sem("exped"), 8)
        for n in range(3):
            b = to_fill(pe, f"pT{n}")
            for j in range(4):
                ins = transpose(b[:, P * j:P * j + P], scores[:, 512 * n + P * j:512 * n + P * j + P])
            fills(ins, f"pT{n}")
        for n in range(3):
            been_read(pe, f"pT{n}")
        for t in range(T):
            b = to_fill(pe, f"o{t}")
            for h in range(HEADS):
                for k in range(t + 1):
                    at = P * h if t == 0 else 512 + 256 * h + P * k
                    ins = mm(b[:, P * h:P * h + P], probsT[:, at:at + P], v_mla[:, k, h], start=k == 0, stop=k == t)
            fills(ins, f"o{t}")
        been_read(pe, "o0")
        been_read(pe, "o1")
        turn_xs("cat", [("cat_scaled", T)])
        for c in range(2):
            wide(C_OUT + c, U_OUT + 2 * c, xt="cat")

        turn_xs("crossq", [("crossq_scaled", T)])
        pe.wait_ge(sem("x_attn"), 2)
        for c in range(2):
            wide(C_CQ + c, U_CQ + 2 * c, xt="crossq", free=False)
        pe.wait_ge(sem("qc_scaled"), 1)
        turn_tiles("qc", lambda j, t: q_cross[:, t, P * j:P * j + P], 4)
        for n in range(4):
            been_read(pe, f"qc{n}")
            been_read(pe, f"kc{n}")
        for n in range(4):
            t, b = n // 2, to_fill(pe, f"cs{n}")
            for j in range(2):
                h = 2 * (n % 2) + j
                for k in range(2):
                    ins = mm(b[:, 256 * j:256 * j + 256], q_crossT[:, 2 * h + k, P * t:P * t + P], k_crossT[:, 2 * h + k],
                             start=k == 0, stop=k == 1)
            fills(ins, f"cs{n}")
        for n in range(4):
            been_read(pe, f"cs{n}")
            t, b = n // 2, to_fill(pe, f"cp{n}")
            for j in range(2):
                for k in range(2):
                    ins = transpose(b[:, 256 * j + P * k:256 * j + P * k + P], c_scores[:, t, 2 * (n % 2) + j, P * k:P * k + P])
            fills(ins, f"cp{n}")
        for n in range(4):
            been_read(pe, f"cp{n}")
            t, b = n // 2, to_fill(pe, f"co{n}")
            for j in range(2):
                h = 2 * (n % 2) + j
                for k in range(2):
                    ins = mm(b[:, 256 * j:256 * j + 256], c_probsT[:, t, h, P * k:P * k + P],
                             v_cross[:, k, 256 * h:256 * h + 256], start=k == 0, stop=k == 1)
            fills(ins, f"co{n}")
        for n in range(4):
            been_read(pe, f"co{n}")
        turn_xs("catc", [])
        for c in range(2):
            chunk_read(pe, C_CQ + c)
        for c in range(2):
            wide(C_CO + c, U_CO + 2 * c, xt="catc", free=False)

        turn_xs("moe", [("moe_scaled", T)])
        for n in range(4):
            been_read(pe, f"moe{n}")
        pe.wait_ge(sem("router_lo"), 1)
        b = to_fill(pe, "router")
        for t in range(T):
            for at, n in ((0, GROUPS), (KD * GROUPS, EXPERTS)):
                for k in range(KD):
                    o = b[:, 64 * t + at // KD:64 * t + at // KD + n]
                    ins = three(o, xT_hi[:, k, P * t:P * t + P], xT_lo[:, k, P * t:P * t + P],
                                r_hi[:, at + n * k:at + n * k + n], r_lo[:, at + n * k:at + n * k + n],
                                start=k == 0, stop=k == KD - 1)
        fills(ins, "router")
        been_read(pe, "router")
        pe.wait_ge(sem("x_cross"), 2)

        def swiglu(name, base, steps):
            def columns_of(which, u0, per, i):
                if u0 == base and per == 0:
                    for n in range(4):
                        if where[f"{name}{n}"][0] < 6:
                            been_read(pe, f"{name}{n}")
                pe.wait_ge(lo_ready, count(u0 + 1, per, i))
                s = u0 % RING
                for k in range(KD):
                    if u0 == base and per == 0 and k % 2 == 0:
                        been_read(pe, f"{name}{k // 2}")
                    for t in range(T):
                        ins = three(bank[4 + t][:, FF * which:FF * which + FF], xT_hi[:, k, P * t:P * t + P], xT_lo[:, k, P * t:P * t + P],
                                    w_hi[:, s, FF * k:FF * k + FF], w_lo[:, s, FF * k:FF * k + FF], start=k == 0, stop=k == KD - 1)
                ins.then_inc(unit_done, 1)

            def down(e, u0, per, i, first=False, last_step=False):
                pe.wait_ge(lo_ready, count(u0 + 1, per, i))
                pe.wait_ge(sem(name + "_aT_lo"), e + 1)
                s = u0 % RING
                for k in range(2):
                    for t in range(T):
                        for c in range(2):
                            at = D * k + 512 * c
                            ins = three(bank[2 * c + t][:, :], aT_hi[:, k, P * t:P * t + P], aT_lo[:, k, P * t:P * t + P],
                                        w_hi[:, s, at:at + 512], w_lo[:, s, at:at + 512],
                                        start=first and k == 0, stop=last_step and k == 1)
                ins.then_inc(unit_done, 1)

            def turn_hidden(e):
                pe.wait_ge(sem(name + "_hidden"), e * 2 + 2)
                view = hidden[:].rearrange("p t (q k) -> p t k q", k=2)
                for k in range(2):
                    for t in range(T):
                        ins = transpose(bank[6][:, 256 * k + P * t:256 * k + P * t + P], view[:, t, k])
                ins.then_inc(sem(name + "_turned"), 1)

            columns_of(0, base, 0, 0)
            columns_of(1, base + 1, 0, 0)
            turn_hidden(0)

            def step(i, first=False):
                pe.wait_ge(sem(name + "_hidden"), i * 2)
                columns_of(0, base - 1, 3, i)
                columns_of(1, base, 3, i)
                down(i - 1, base + 1, 3, i, first=first)
                turn_hidden(i)

            step(1, first=True)
            with pe.Fori(2, steps) as i:
                step(i)
            down(steps - 1, base + 3 * steps - 1, 0, 0, last_step=True)

        swiglu("moe", U_MOE, EXPERTS)

        turn_xs("mix", [("mix_scaled", T)])
        for n in range(4):
            been_read(pe, f"mix{n}")
        pe.wait_ge(sem("x_moe"), 4)
        with pe.Fori(0, HEADS) as h:
            def features(j, b):
                pe.wait_ge(lo_ready, h * UNITS_HEAD + (U_HEADS + j + 1))
                s = (U_HEADS + j) % RING
                for f in range(2):
                    for k in range(KD):
                        at = 256 * k + P * f
                        o = bank[b][:, 256 * f:256 * f + 256]
                        mm(o, w_hi[:, s, at:at + P], xT_hi[:, k, :], start=k == 0, stop=False)
                        mm(o, w_hi[:, s, at:at + P], xT_lo[:, k, :], start=False, stop=False)
                        ins = mm(o, w_lo[:, s, at:at + P], xT_hi[:, k, :], start=False, stop=k == KD - 1)
                ins.then_inc(unit_done, 1)

            def block_diagonal(j, b):
                pe.wait_ge(lo_ready, h * UNITS_HEAD + (U_HEADS + j + 1))
                s = (U_HEADS + j) % RING
                for f in range(2):
                    for k in range(2):
                        at = 256 * k + P * f
                        o = bank[b][:, 256 * f:256 * f + 256]
                        mm(o, w_hi[:, s, at:at + P], rx_hi[:, 256 * k:256 * k + 256], start=k == 0, stop=False)
                        mm(o, w_hi[:, s, at:at + P], rx_lo[:, 256 * k:256 * k + 256], start=False, stop=False)
                        ins = mm(o, w_lo[:, s, at:at + P], rx_hi[:, 256 * k:256 * k + 256], start=False, stop=k == 1)
                ins.then_inc(unit_done, 1)

            for j in range(5):
                features(j, j)
            pe.wait_ge(sem("rx_lo"), h + 1)
            block_diagonal(5, 7)
            pe.wait_ge(sem("rx_copied"), h + 1)
            block_diagonal(6, 0)
            features(7, 5)
            features(8, 6)

        for c in range(2):
            for half_ in range(2):
                pe.wait_ge(sem("mT_lo"), 2 * half_ + 2)
                wide_unit(U_OUT2 + 2 * c + half_, C_OUT2 + c, half_, 512, mT_hi, mT_lo)
        turn_xs("ffn", [("ffn_scaled", T)])
        pe.wait_ge(sem("x_rnn"), 2)
        swiglu("ffn", U_FFN, STEPS_FFN)

        pe.wait_ge(sem("last_loaded"), 32)
        b = to_fill(pe, "pT")
        view = p_in[:].rearrange("p t (q k) -> p t k q", k=2)
        for k in range(2):
            for t in range(T):
                ins = transpose(b[:, 256 * k + P * t:256 * k + P * t + P], view[:, t, k])
        fills(ins, "pT")
        been_read(pe, "pT")
        pe.wait_ge(sem("x_ffn"), 4)
        pe.wait_ge(lo_ready, U_PLE + 1)
        s = U_PLE % RING
        for c in range(2):
            for k in range(2):
                for t in range(T):
                    at = D * k + 512 * c
                    ins = three(pair(C_PLE + c)[t][:, :], aT_hi[:, k, P * t:P * t + P], aT_lo[:, k, P * t:P * t + P],
                                w_hi[:, s, at:at + 512], w_lo[:, s, at:at + 512], start=k == 0, stop=k == 1)
        ins.then_inc(unit_done, 1)
        turn_xs("ple", [("ple_scaled", T)])
        for c in range(2):
            chunk_read(pe, C_PLE + c)
        for c in range(2):
            wide(C_GATE + c, U_PLE + 1 + 2 * c, xt="ple", free=False)


_INS = ("x mem positions attn_norm_g w_in mla_q_norm_g mla_w_uq mla_kv_norm_g mla_w_ukv mla_q_qk_g mla_k_qk_g "
        "ret_gn_g w_out cross_norm_g mem_norm_g cross_w_q cross_w_kv cross_q_qk_g cross_k_qk_g cross_w_o moe_norm_g "
        "router_w_group router_b_group router_w_expert router_b_expert expert_w_gate expert_w_up expert_w_down p_2 "
        "g_mix_2 w_in_2 conv4_w_2 conv4_b_2 w_rg_r_2 b_rg_r_2 w_rg_i_2 b_rg_i_2 lru_lambda_2 conv3_w_2 w_out_2 "
        "g_ffn_2 w_gate_up_2 w_down_2 g_ple_2 w_ple_gate_2 w_ple_2 g_final_2").split()


def kernel(**inputs):
    import numpy as _np
    import concourse.bacc as _bacc
    from concourse import mybir as _mybir
    from concourse.bass_utils import run_bass_kernel_spmd as _run

    nc = _bacc.Bacc("TRN2", target_bir_lowering=False, num_devices=1)
    arrays, aps = {}, {}
    for name in _INS:
        arrays[f"in_{name}_dram"] = _np.ascontiguousarray(inputs[name])
    arrays["in_const_dram"] = constants()
    for name in _INS + ["const"]:
        v = arrays[f"in_{name}_dram"]
        aps[name] = nc.dram_tensor(f"in_{name}_dram", v.shape, _mybir.dt.from_np(v.dtype), kind="ExternalInput").ap()
    result = nc.dram_tensor("out_0_dram", (1, T * P, D), _mybir.dt.float32, kind="ExternalOutput").ap()
    build(nc, aps, result)
    r = _run(nc, [arrays], core_ids=[0])
    return r.results[0]["out_0_dram"]
```

```python
from contextlib import ExitStack

import numpy as np

import concourse.bass as bass
from concourse import mybir

F32 = mybir.dt.float32
F32R = mybir.dt.float32r
I32 = mybir.dt.int32
ALU = mybir.AluOpType
ACT = mybir.ActivationFunctionType
AX = mybir.AxisListType.X

P = 128
D = 1024
T = 2
KD = D // P
EPS = 1e-6
SLOT = 2048
RING = 3
HEADS = 4
NOPE, ROPE, QK = 128, 64, 192
CROSS = 256
GROUPS, PER_GROUP = 4, 8
EXPERTS = GROUPS * PER_GROUP
FF = 256
D_FF = 2816
STEPS_FFN = D_FF // FF
RET = 128
NEG = -1e30
VEC_ROWS = (4 + 3 + 4) * KD


def constants():
    ident = np.eye(P, dtype=np.float32)
    i = np.arange(P)
    mask = np.zeros((P, 2 * P), np.float32)
    mask[:, P:] = np.where(i[None, :] <= i[:, None], 0.0, NEG)
    j, q = np.arange(P)[:, None], np.arange(2 * P)[None, :]
    decay = []
    for h in range(HEADS):
        g = np.log(1.0 - 2.0 ** (-5.0 - h))
        decay.append(np.where(q >= j, np.exp((q - j) * g), 0.0) * RET ** -0.5)
    decay = np.stack(decay, 1).reshape(P, -1)
    inv = [np.float32(10000.0) ** (-np.arange(n, dtype=np.float32) / np.float32(n)) for n in (ROPE // 2, RET // 2)]
    inv = np.broadcast_to(np.concatenate(inv), (P, 96))
    first = np.broadcast_to(np.arange(PER_GROUP, 0, -1), (P, PER_GROUP))
    earlier = np.triu(np.ones((P, P)), 1)
    slots = np.broadcast_to(np.arange(P), (P, P))
    return np.concatenate([ident, mask, decay, inv, first, earlier, slots], 1).astype(np.float32)


MAGIC = 1.5 * 2.0 ** 23
PI_BELOW = 3.1415925
HEAD_LINKS = 15
CONST_COLS = P + 2 * P + HEADS * 2 * P + 96 + PER_GROUP + 2 * P


def two_pi_parts():
    left, parts = 2 * np.pi, []
    for _ in range(3):
        unit = 2.0 ** (np.floor(np.log2(left)) - 7)
        parts.append(float(np.floor(left / unit) * unit))
        left -= parts[-1]
    return parts + [float(np.float32(left))]


def build(nc, a, out):
    with ExitStack() as ctx:
        program(nc, a, out, ctx)


def program(nc, a, out, ctx):
    def sb(name, shape, dt=F32):
        return ctx.enter_context(nc.sbuf_tensor(name, shape, dt))

    sems = {}

    def sem(name):
        if name not in sems:
            sems[name] = ctx.enter_context(nc.semaphore(name))
        return sems[name]

    bank = [ctx.enter_context(nc.psum_tensor(f"bank{b}", [P, 512], F32)) for b in range(8)]

    stage = sb("stage", [P, RING, SLOT])
    w_hi = sb("w_hi", [P, RING, SLOT], F32R)
    w_lo = sb("w_lo", [P, RING, SLOT], F32R)
    x = sb("x", [P, T, D])
    xs = sb("xs", [P, T, D])
    xT_hi = sb("xT_hi", [P, KD, 2 * P], F32R)
    xT_lo = sb("xT_lo", [P, KD, 2 * P], F32R)
    aT_hi = sb("aT_hi", [P, 2, 2 * P], F32R)
    aT_lo = sb("aT_lo", [P, 2, 2 * P], F32R)
    cT_hi = sb("cT_hi", [P, 3, 2 * P], F32R)
    cT_lo = sb("cT_lo", [P, 3, 2 * P], F32R)
    const = sb("const", [P, CONST_COLS])
    ident = const[:, 0:P]
    mask = const[:, P:3 * P]
    decay = const[:, 3 * P:11 * P].rearrange("p (h q) -> p h q", h=HEADS)
    inv_freq = const[:, 11 * P:11 * P + 96]
    at_tables = 11 * P + 96 + PER_GROUP
    first_weight = const[:, 11 * P + 96:at_tables]
    earlier, slot_numbers = const[:, at_tables:at_tables + P], const[:, at_tables + P:]
    norm_g = sb("norm_g", [P, 7, KD])
    MEM_G, ATTN_G, CROSS_G, MOE_G, MIX_G, FFN_G, PLE_G = range(7)
    qn_g = sb("qn_g", [P, 2])
    kvn_g = sb("kvn_g", [P, 1])
    nope_g = sb("nope_g", [P, 2])
    rope_g = sb("rope_g", [P, 2, ROPE])
    cqk_g = sb("cqk_g", [P, 2, 2])
    gn_g = sb("gn_g", [P, 512])
    r_bias = sb("r_bias", [P, GROUPS + EXPERTS])
    CHOICES = GROUPS + EXPERTS
    r_w = sb("r_w", [P, KD, CHOICES])
    r_hi = sb("r_hi", [P, KD, CHOICES], F32R)
    r_lo = sb("r_lo", [P, KD, CHOICES], F32R)
    pos_i = sb("pos_i", [P, T], I32)
    pos_f = sb("pos_f", [P, T])
    trig = sb("trig", [P, 2, T, 96])
    vec_in = sb("vec_in", [VEC_ROWS, P])
    vec = sb("vec", [P, VEC_ROWS])
    conv4_w = vec[:, 0:4 * KD]
    conv3_w = vec[:, 4 * KD:7 * KD]
    conv4_b, half_br, half_bi, lam = (vec[:, (7 + n) * KD:(8 + n) * KD] for n in range(4))
    softplus2 = sb("softplus2", [P, KD])
    sums, inverse, rstd, half_rstd = (sb(n, [P, T]) for n in ("sums", "inverse", "rstd", "half_rstd"))
    ffn_scale = sb("ffn_scale", [P, T])
    q_scale = sb("q_scale", [P, T * HEADS])
    head_sums, head_inv, head_rstd = (sb(n, [P, 16]) for n in ("head_sums", "head_inv", "head_rstd"))
    lat_sums, lat_inv, lat_rstd = (sb(n, [P, 4]) for n in ("lat_sums", "lat_inv", "lat_rstd"))
    gn_stats = sb("gn_stats", [P, T * HEADS, 6])
    gn_mv = sb("gn_mv", [P, T * HEADS, 2])
    gn_inv, gn_rstd = sb("gn_inv", [P, T * HEADS]), sb("gn_rstd", [P, T * HEADS])
    top, neg_top, exp_sum, exp_inv = (sb(n, [P, 2 * T * HEADS]) for n in ("top", "neg_top", "exp_sum", "exp_inv"))
    logits = sb("logits", [P, T, GROUPS + EXPERTS])
    diffs = sb("diffs", [P, T, GROUPS + PER_GROUP])
    exps = sb("exps", [P, T, GROUPS + PER_GROUP])
    route = sb("route", [P, 9, T * EXPERTS])
    lam_t = sb("lam_t", [P, 6, KD])
    one_col, warm = sb("one_col", [P, 1]), sb("warm", [P, 1])
    hidden = sb("hidden", [P, T, FF])
    silu_t = sb("silu_t", [P, T, FF])
    silu_g = sb("silu_g", [P, T, FF])
    logitsT = silu_t[0:CHOICES, 0]
    attention_memory = ExitStack()
    arena_words = 16896 + 384
    arena = attention_memory.enter_context(nc.sbuf_tensor("arena", [P, arena_words], F32))
    taken = [0]

    def part(words):
        at = taken[0]
        taken[0] += words
        assert taken[0] <= arena_words, taken[0]
        return arena[:, at:at + words]

    k_crossT = part(KD * 256).rearrange("p (j t) -> p j t", j=KD)
    v_cross = part(T * D).rearrange("p (t n) -> p t n", t=T)
    share1 = part(T * D)
    k_cross = share1.rearrange("p (t n) -> p t n", t=T)
    q_mla = share1[:, 0:T * 768].rearrange("p (t h d) -> p t h d", t=T, h=HEADS)
    scores = share1[:, 0:1536]
    q_cross = share1.rearrange("p (t n) -> p t n", t=T)
    share2 = part(2048)
    k_mla = share2[:, 0:1536].rearrange("p (t h d) -> p t h d", t=T, h=HEADS)
    probsT = share2[:, 0:1536]
    v_mla = part(T * 512).rearrange("p (t h d) -> p t h d", t=T, h=HEADS)
    latent = part(T * 448).rearrange("p (t n) -> p t n", t=T)
    r_q = part(T * 512)
    r_k = part(T * 512)
    r_v = part(T * 512).rearrange("p (t n) -> p t n", t=T)
    r_gate = r_q.rearrange("p (t n) -> p t n", t=T)
    r_s0 = r_q.rearrange("p (h q) -> p h q", h=HEADS)
    r_s1 = r_k[:, 0:512].rearrange("p (h q) -> p h q", h=HEADS)
    rot_q, rot_k = (xs[:, t] for t in range(T))
    turned = part(4096)
    angle = turned[:, 3072:3072 + 4 * T * 96].rearrange("p (s n) -> p s n", s=4)
    r_qT, r_kT = (turned[:, n * 1024:(n + 1) * 1024].rearrange("p (h t) -> p h t", h=HEADS) for n in (0, 1))
    qT_n, qT_r, kT_n, kT_r = (turned[:, n * 1024:(n + 1) * 1024].rearrange("p (h t) -> p h t", h=HEADS) for n in range(4))
    q_crossT = turned[:, 0:2048].rearrange("p (j t) -> p j t", j=KD)
    c_scores = share1.rearrange("p (t h m) -> p t h m", t=T, h=HEADS)
    c_probsT = share2.rearrange("p (t h m) -> p t h m", t=T, h=HEADS)
    qk_r = [xs[:, :, 256 * w:256 * w + 256].rearrange("p t (h d) -> p t h d", h=HEADS) for w in (0, 1)]

    attention_memory.close()

    recurrent_memory = ExitStack()

    def rb(name, shape, dt=F32):
        return recurrent_memory.enter_context(nc.sbuf_tensor(name, shape, dt))

    xpad = rb("xpad", [P, 2, 259])
    cpad = rb("cpad", [P, 2, 258])
    y_sq, y_in, y_tanh, c_in, q_inv, decay_a, u_in, states, gr_tanh, gc_tanh, merged = (
        rb(n, [P, 512]) for n in ("y_sq", "y_in", "y_tanh", "c_in", "q_inv", "decay_a", "u_in", "states", "gr_tanh",
                                  "gc_tanh", "merged"))
    rx, conv3, r_tanh, tau, i_tanh, root_tau = (
        rb(n, [P, 2, 256]) for n in ("rx", "conv3", "r_tanh", "tau", "i_tanh", "root_tau"))
    rx_hi, rx_lo = rb("rx_hi", [P, 512], F32R), rb("rx_lo", [P, 512], F32R)
    mT_hi, mT_lo = rb("mT_hi", [P, KD, 2 * P], F32R), rb("mT_lo", [P, KD, 2 * P], F32R)
    recurrent_memory.close()

    expert_memory = ExitStack()

    def eb(name, shape, dt=F32):
        return expert_memory.enter_context(nc.sbuf_tensor(name, shape, dt))

    xs_hi, xs_lo = (eb(n, [P, T, D], F32R) for n in ("xs_hi", "xs_lo"))
    slot_of = eb("slot_of", [P, T, GROUPS * P], F32R)
    token_of = eb("token_of", [P, GROUPS, T * P], F32R)
    token_now = eb("token_now", [P, T * P], F32R)
    xg_hi, xg_lo = (eb(n, [P, KD, P], F32R) for n in ("xg_hi", "xg_lo"))
    later_hi, later_lo = (eb(n, [P, KD, (GROUPS - 1) * P], F32R) for n in ("later_hi", "later_lo"))
    y_hi, y_lo = (eb(n, [P, 2, 512], F32R) for n in ("y_hi", "y_lo"))
    ones = eb("ones", [P, P])
    rank = eb("rank", [P, T + 1, GROUPS])
    over_t, over_n, over_i = eb("over_t", [P, T * GROUPS]), eb("over_n", [P, T]), eb("over_i", [P, 2], I32)
    token_gates = eb("token_gates", [P, T, PER_GROUP])
    slot_gates = eb("slot_gates", [P, EXPERTS])
    expert_memory.close()

    embed, ple_gate = sb("embed", [P, T, D]), sb("ple_gate", [P, T, D])
    fin_g = sb("fin_g", [P, D])
    p_in = sb("p_in", [P, T, 256])

    def columns(w, c0, n, h):
        return w.rearrange("(p k) n -> p k n", k=KD)[:, 4 * h:4 * h + 4, c0:c0 + n], 4 * n

    w_in, w_kv = a["w_in"][0], a["cross_w_kv"][0]
    before = []
    for c in range(4):
        before += [columns(w_kv, 512 * c, 512, h) for h in range(2)]
    U_LAT = len(before)
    before += [columns(w_in, 0, 448, h) for h in range(2)]
    U_RQ = len(before)
    for c in range(3):
        before += [columns(w_in, 448 + 512 * c, 512, h) for h in range(2)]
    U_RK, U_RV, U_UQ = U_RQ + 2, U_RQ + 4, U_RQ + 6
    before.append((a["mla_w_uq"][0].rearrange("(p k) n -> p (k n)", k=2), 1536))
    before.append((a["mla_w_ukv"][0], 1024))
    U_UKV, U_RG = U_UQ + 1, U_UQ + 2
    before += [columns(w_in, 448 + 512 * 3, 512, h) for h in range(2)]
    U_OUT = len(before)
    U_CQ, U_CO = U_OUT + 4, U_OUT + 8
    for w in ("w_out", "cross_w_q", "cross_w_o"):
        for c in range(2):
            before += [columns(a[w][0], 512 * c, 512, h) for h in range(2)]
    U_MOE = len(before)
    U_HEADS = U_MOE + 3 * EXPERTS
    HEAD_GROUPS = (0, 1, 3, 4, None, 2, None, 5, 6)
    RX, GELU, C_CONV, X_CONV, RG_R, B_CONV, RG_I, G_R, G_C = range(9)
    UNITS_HEAD = len(HEAD_GROUPS)
    U_OUT2 = U_HEADS + UNITS_HEAD * HEADS
    U_FFN = U_OUT2 + 4
    U_PLE = U_FFN + 3 * STEPS_FFN
    U_END = U_PLE + 5
    middle = []
    for h in range(2):
        for c in range(2):
            middle.append((a["w_out_2"][0].rearrange("(k p) n -> p k n", k=KD)[:, 4 * h:4 * h + 4, 512 * c:512 * c + 512], 2048))
    last = [(a["w_ple_2"][0].rearrange("(p k) n -> p (k n)", k=2), 2048)]
    for c in range(2):
        last += [columns(a["w_ple_gate_2"][0], 512 * c, 512, h) for h in range(2)]

    def cols_of(u):
        if u < U_MOE:
            return before[u][1]
        return 2048

    def count(u0, per=0, i=0):
        return i * per + u0 if per else u0

    def slot_uses(u0, per=0, i=0):
        return i * (16 * per // RING) + 16 * (u0 // RING + 1) if per else 16 * (u0 // RING + 1)

    class Stream:
        def __init__(self, prefix):
            self.landed = [sem(f"{prefix}weights_landed{s}") for s in range(RING)]
            self.hi_ready, self.lo_ready = sem(prefix + "w_hi_ready"), sem(prefix + "w_lo_ready")
            self.half_ready, self.unit_done = sem(prefix + "w_half_ready"), sem(prefix + "unit_done")

    main, over = Stream(""), Stream("over_")
    hi_ready, lo_ready, unit_done = main.hi_ready, main.lo_ready, main.unit_done

    def load_unit(sp, src, cols, u0, per=0, i=0, st=main):
        if u0 >= RING or per:
            sp.wait_ge(st.hi_ready, count(u0 - RING + 1, per, i))
            sp.wait_ge(st.lo_ready, count(u0 - RING + 1, per, i))
        s = u0 % RING
        dst = stage[:, s, 0:cols]
        if len(src.shape) == 3:
            dst = dst.rearrange("p (k n) -> p k n", k=src.shape[1])
        sp.dma_start(dst, src).then_inc(st.landed[s], 16)

    def split_hi(act, cols, u0, per=0, i=0, st=main):
        s = u0 % RING
        act.wait_ge(st.landed[s], slot_uses(u0, per, i))
        if u0 >= RING:
            act.wait_ge(st.unit_done, count(u0 - RING + 1, per, i))
        half = cols // 2
        nc.scalar.activation(w_hi[:, s, 0:half], stage[:, s, 0:half], ACT.Copy).then_inc(st.half_ready, 1)
        nc.scalar.activation(w_hi[:, s, half:cols], stage[:, s, half:cols], ACT.Copy).then_inc(st.hi_ready, 1)

    def split_lo(dve, cols, u0, per=0, i=0, st=main):
        s = u0 % RING
        half = cols // 2
        dve.wait_ge(st.half_ready, count(u0 + 1, per, i))
        nc.vector.tensor_tensor(w_lo[:, s, 0:half], stage[:, s, 0:half], w_hi[:, s, 0:half].bitcast(F32), ALU.subtract)
        dve.wait_ge(st.hi_ready, count(u0 + 1, per, i))
        nc.vector.tensor_tensor(w_lo[:, s, half:cols], stage[:, s, half:cols], w_hi[:, s, half:cols].bitcast(F32),
                                ALU.subtract).then_inc(st.lo_ready, 1)

    products = ([f"mem{n}" for n in range(4)] + ["vec"] + [f"kc{n}" for n in range(4)]
                + [f"attn{n}" for n in range(4)]
                + ["cq", "ckv", "rq0", "rq1", "rk0", "rk1", "rs0", "rs1", "rs2", "ro0", "ro1"]
                + [f"{w}{n}" for w in ("qn", "qr", "kn", "kr") for n in (0, 1)]
                + ["s0", "s1", "s2", "pT0", "pT1", "pT2", "o0", "o1"]
                + [f"cat{n}" for n in range(4)] + [f"crossq{n}" for n in range(4)]
                + [f"{w}{n}" for w in ("qc", "cs", "cp", "co") for n in range(4)]
                + [f"catc{n}" for n in range(4)] + [f"moe{n}" for n in range(4)] + ["router", "logits", "rank"]
                + [f"mix{n}" for n in range(4)] + [f"ffn{n}" for n in range(4)]
                + ["pT"] + [f"ple{n}" for n in range(4)])
    where = {name: (4 + n % 4, n // 4) for n, name in enumerate(products)}
    filled = [sem(f"bank{b}_filled") for b in range(4, 8)]
    freed = [sem(f"bank{b}_freed") for b in range(4, 8)]

    def to_fill(pe, name):
        b, g = where[name]
        if g:
            pe.wait_ge(freed[b - 4], g)
        return bank[b]

    def fills(ins, name):
        ins.then_inc(filled[where[name][0] - 4], 1)

    def product(eng, name):
        b, g = where[name]
        eng.wait_ge(filled[b - 4], g + 1)
        return bank[b]

    def frees(ins, name):
        ins.then_inc(freed[where[name][0] - 4], 1)

    def been_read(eng, name):
        b, g = where[name]
        eng.wait_ge(freed[b - 4], g + 1)

    def row(v):
        return v.rearrange("(o n) -> o n", o=1)

    first_loads = [(ident, a["const"][:, 0:P]),
                   (norm_g[:, MEM_G], a["mem_norm_g"][0].rearrange("(p k) -> p k", k=KD))]
    small_loads = [(const[:, P:], a["const"][:, P:])]
    for n, g in enumerate(("mem_norm_g", "attn_norm_g", "cross_norm_g", "moe_norm_g", "g_mix_2", "g_ffn_2", "g_ple_2")):
        if n != MEM_G:
            small_loads.append((norm_g[:, n], a[g][0].rearrange("(p k) -> p k", k=KD)))
    small_loads += [
        (vec_in[0:4 * KD], a["conv4_w_2"][0].rearrange("w (k p) -> (w k) p", p=P)),
        (vec_in[4 * KD:7 * KD], a["conv3_w_2"][0].rearrange("w (k p) -> (w k) p", p=P)),
        (vec_in[7 * KD:8 * KD], a["conv4_b_2"][0].rearrange("(k p) -> k p", p=P)),
        (vec_in[8 * KD:9 * KD], a["b_rg_r_2"][0].rearrange("h (k p) -> (h k) p", p=P)),
        (vec_in[9 * KD:10 * KD], a["b_rg_i_2"][0].rearrange("h (k p) -> (h k) p", p=P)),
        (vec_in[10 * KD:11 * KD], a["lru_lambda_2"][0].rearrange("(k p) -> k p", p=P)),
        (qn_g[:], a["mla_q_norm_g"][0].rearrange("(p k) -> p k", k=2)),
        (kvn_g[:], a["mla_kv_norm_g"][0].rearrange("(p k) -> p k", k=1)),
        (gn_g[:], a["ret_gn_g"].to_broadcast([P, 512])),
        (r_bias[:, 0:GROUPS], a["router_b_group"].to_broadcast([P, GROUPS])),
        (r_bias[:, GROUPS:], a["router_b_expert"].to_broadcast([P, EXPERTS])),
        (r_w[:, :, 0:GROUPS], a["router_w_group"][0].rearrange("(p k) n -> p k n", k=KD)),
        (r_w[:, :, GROUPS:], a["router_w_expert"][0].rearrange("(p k) n -> p k n", k=KD)),
    ]
    for n, g in enumerate(("mla_q_qk_g", "mla_k_qk_g")):
        small_loads.append((nope_g[:, n:n + 1], a[g][0, 0:NOPE].rearrange("(p k) -> p k", k=1)))
        small_loads.append((rope_g[:, n], a[g][:, NOPE:QK].to_broadcast([P, ROPE])))
    for n, g in enumerate(("cross_q_qk_g", "cross_k_qk_g")):
        for k in range(2):
            small_loads.append((cqk_g[:, n, k:k + 1], a[g][0, P * k:P * k + P].rearrange("(p k) -> p k", k=1)))
    for t in range(T):
        small_loads.append((pos_i[:, t:t + 1], a["positions"][0, P * t:P * t + P].rearrange("(p k) -> p k", k=1)))

    chunk_freed = [sem("pair0_freed"), sem("pair1_freed")]
    (C_K, C_V, C_LAT, C_RQ, C_RK, C_RV, C_UQ, C_UKV, C_RG, C_OUT, C_CQ, C_CO, C_OUT2, C_PLE, C_GATE) = (
        0, 2, 4, 5, 6, 7, 8, 10, 12, 13, 15, 17, 19, 21, 23)

    def pair(c):
        return bank[2 * (c % 2):2 * (c % 2) + 2]

    signalled = [c for c in range(C_GATE) if not (C_OUT <= c < C_CQ or C_CO <= c < C_PLE)]

    def chunk_read(eng, c):
        eng.wait_ge(chunk_freed[c % 2], sum(d % 2 == c % 2 for d in signalled if d <= c))

    def flat3(v):
        return v.rearrange("p k t -> p (k t)")

    NORMS = ("mem", "attn", "crossq", "moe", "mix", "ffn", "ple", "final")
    TURNED = ("mem", "attn", "cat", "crossq", "catc", "moe", "mix", "ffn", "ple")

    def high_ready(eng, name, n):
        eng.wait_ge(sem("xT_hi"), 4 * TURNED.index(name) + n)

    def copy_half(eng, name, j, dst, scale):
        b = product(eng, name)
        return nc.scalar.activation(dst, b[:, 256 * j:256 * j + 256], ACT.Copy, scale=scale)

    def up_done(base, e):
        return base + 2 if isinstance(e, int) and e == 0 else e * 3 + (base + 1)

    def expert_steps(eng, groups, step, tail):
        step(0, 0)
        step(0, 1)
        if groups > 1:
            with eng.Fori(0, groups - 1) as g:
                for j in range(2, PER_GROUP + 2):
                    step(g, j)
        for j in range(2, PER_GROUP - 1):
            step(groups - 1, j)
        tail(groups - 1)

    LAST = PER_GROUP - 1
    PER_TURN = 3 * PER_GROUP

    def eighths(g, n):
        return g * PER_GROUP + n

    def gate_unit(base, j):
        return base + (3 * j - 1 if j else 0)

    def up_unit(base, j):
        return base + (3 * j if j else 1)

    def last_down(base, groups):
        return base + 3 * PER_GROUP * groups - 1

    def part_bank(k):
        return bank[k % 6]

    def overflow(eng):
        eng.wait_ge(sem("over_known"), 1)
        return eng.value_load(over_i[0:1, 0:1], min_val=0, max_val=1)

    def routing(dve, then):
        tt, ts, stt = nc.vector.tensor_tensor, nc.vector.tensor_scalar, nc.vector.scalar_tensor_tensor

        def scratch(n, width):
            return route[:, n, 0:T * width].rearrange("p (t e) -> p t e", t=T)

        def over(v, n):
            return v.to_broadcast([P, T, n])

        def largest(dst, src):
            then(nc.vector.tensor_reduce(dst.rearrange("p t o -> p (t o)"), src, AX, ALU.max))

        def total(dst, src):
            then(nc.vector.tensor_reduce(dst.rearrange("p t o -> p (t o)"), src, AX, ALU.add))

        def first_of_largest(dst, src, best, n, signal=None):
            weight = first_weight[:, 0:n].unsqueeze(1).to_broadcast([P, T, n])
            largest(best, src)
            then(tt(dst, src, over(best, n), ALU.is_equal))
            then(tt(dst, dst, weight, ALU.mult))
            largest(best, dst)
            if signal:
                tt(dst, dst, over(best, n), ALU.is_equal).then_inc(sem(signal), 1)
                dve.wait_ge(sem(signal), 1)
            else:
                then(tt(dst, dst, over(best, n), ALU.is_equal))

        def pick(dst, src, wide):
            then(tt(wide, src, group_hot.unsqueeze(3).to_broadcast([P, T, GROUPS, PER_GROUP]), ALU.mult))
            then(nc.vector.tensor_reduce(dst, wide.rearrange("p t g e -> p t e g"), AX, ALU.add))

        been_read(dve, "logits")
        g_logit = logits[:, :, 0:GROUPS]
        e_logit = logits[:, :, GROUPS:].rearrange("p t (g e) -> p t g e", g=GROUPS)
        best = scratch(0, 1)
        biased, group_hot = scratch(1, GROUPS), scratch(2, GROUPS)
        largest(best, g_logit)
        then(tt(diffs[:, :, 0:GROUPS], g_logit, over(best, GROUPS), ALU.subtract))
        then(tt(biased, g_logit, r_bias[:, 0:GROUPS].unsqueeze(1).to_broadcast([P, T, GROUPS]), ALU.add))
        first_of_largest(group_hot, biased, best, GROUPS, "group_chosen")
        frees(nc.vector.tensor_copy(rank[:].rearrange("p t g -> p (t g)"), product(dve, "rank")[:, 0:(T + 1) * GROUPS]), "rank")
        been_read(dve, "rank")
        for t in range(T):
            for g in range(GROUPS):
                ts(slot_of[:, t, P * g:P * g + P], slot_numbers, rank[:, t, g:g + 1], group_hot[:, t, g:g + 1],
                   ALU.is_equal, ALU.mult).then_inc(sem("slots_known"), 1)
        wide_ = route[:, 3].rearrange("p (t g e) -> p t g e", t=T, g=GROUPS)
        mine, bias = scratch(4, PER_GROUP), scratch(5, PER_GROUP)
        pick(mine, e_logit, wide_)
        pick(bias, r_bias[:, GROUPS:].rearrange("p (g e) -> p g e", g=GROUPS).unsqueeze(1).to_broadcast([P, T, GROUPS, PER_GROUP]), wide_)
        largest(best, mine)
        tt(diffs[:, :, GROUPS:], mine, over(best, PER_GROUP), ALU.subtract).then_inc(sem("route_diffs"), 1)
        dve.wait_ge(sem("route_diffs"), 1)
        then(tt(bias, bias, mine, ALU.add))
        hot1, hot2 = scratch(6, PER_GROUP), scratch(7, PER_GROUP)
        first_of_largest(hot1, bias, best, PER_GROUP)
        then(stt(bias, hot1, -3e38, bias, ALU.mult, ALU.add))
        first_of_largest(hot2, bias, best, PER_GROUP)
        then(tt(hot1, hot1, hot2, ALU.add))
        counts = over_t[:, 0:GROUPS]
        then(ts(counts, rank[:, T], P + 0.5, None, ALU.is_gt))
        then(nc.vector.tensor_reduce(over_n[:, 0:1], counts, AX, ALU.add))
        then(tt(counts, counts, slot_numbers[:, 0:GROUPS], ALU.mult))
        then(nc.vector.tensor_reduce(over_n[:, 1:2], counts, AX, ALU.add))
        then(ts(over_n[:, 1:2], over_n[:, 1:2], float(PER_GROUP), None, ALU.mult))
        nc.vector.tensor_copy(over_i[:], over_n[:]).then_inc(sem("over_known"), 1)
        dve.wait_ge(sem("route_exps"), 1)
        ge, ee = exps[:, :, 0:GROUPS], exps[:, :, GROUPS:]
        total(best, ge)
        then(nc.vector.reciprocal(best, best))
        then(tt(ge, ge, over(best, GROUPS), ALU.mult))
        then(tt(ge, ge, group_hot, ALU.mult))
        g_weight = scratch(8, 1)
        total(g_weight, ge)
        total(best, ee)
        then(nc.vector.reciprocal(best, best))
        then(tt(ee, ee, over(best, PER_GROUP), ALU.mult))
        then(tt(ee, ee, hot1, ALU.mult))
        total(best, ee)
        then(nc.vector.reciprocal(best, best))
        then(tt(ee, ee, over(best, PER_GROUP), ALU.mult))
        then(tt(ee, ee, over(g_weight, PER_GROUP), ALU.mult))
        ts(token_gates[:], ee, 0.5, None, ALU.mult).then_inc(sem("token_gates"), 1)

    block = ctx.enter_context(nc.Block())

    @block.sync
    def _(sp):
        for t in range(T):
            sp.dma_start(xs[:, t], a["mem"][0, P * t:P * t + P]).then_inc(sem(f"mem_loaded{t}"), 16)
        load_unit(sp, *before[0], 0)
        load_unit(sp, *before[1], 1)
        sp.dma_start(x[:], a["x"][0].rearrange("(t p) d -> p t d", p=P)).then_inc(sem("x_loaded"), 16)
        for u in range(2, U_MOE):
            load_unit(sp, *before[u], u)

        def swiglu_loads(gate_of, up_of, down_of, base, steps, st=main):
            def step(i, per=3):
                n = 0 if per else 3 * i
                load_unit(sp, gate_of(i + 1), 2048, base + n + 2, per, i, st)
                load_unit(sp, up_of(i + 1), 2048, base + n + 3, per, i, st)
                load_unit(sp, down_of(i), 2048, base + n + 4, per, i, st)

            load_unit(sp, gate_of(0), 2048, base, st=st)
            load_unit(sp, up_of(0), 2048, base + 1, st=st)
            step(0, per=0)
            with sp.Fori(1, steps - 1) as i:
                step(i)
            load_unit(sp, down_of(steps - 1), 2048, base + 3 * steps - 1, st=st)

        def expert(w, k):
            rows = a[w][0].rearrange("e (p k) n -> e p (k n)", k=k)
            return lambda e: rows[bass.ds(e, 1)].rearrange("e p n -> p (e n)")

        gate_w, up_w, down_w = expert("expert_w_gate", KD), expert("expert_w_up", KD), expert("expert_w_down", 2)
        swiglu_loads(gate_w, up_w, down_w, U_MOE, EXPERTS)
        with sp.If(overflow(sp) > 0):
            first_expert = sp.value_load(over_i[0:1, 1:2], min_val=0, max_val=EXPERTS - PER_GROUP)
            sp.wait_ge(hi_ready, U_HEADS)
            sp.wait_ge(lo_ready, U_HEADS)

            def of_group(w):
                return lambda e: w(first_expert + e)

            swiglu_loads(of_group(gate_w), of_group(up_w), of_group(down_w), 0, PER_GROUP, over)
            sp.wait_ge(over.lo_ready, PER_TURN)

        w_in2 = a["w_in_2"][0].rearrange("(p k) n -> p k n", k=KD)
        rg = [a[w][0].rearrange("h (k p) n -> h p k n", k=2) for w in ("w_rg_r_2", "w_rg_i_2")]
        with sp.Fori(0, HEADS) as h:
            for j, group in enumerate(HEAD_GROUPS):
                if group is None:
                    src = rg[j != RG_R][bass.ds(h, 1)].rearrange("h p k n -> p (h k) n")
                    load_unit(sp, src, 512, U_HEADS + j, UNITS_HEAD, h)
                else:
                    load_unit(sp, w_in2[:, :, bass.ds(h * 256 + group * D, 256)], 2048, U_HEADS + j, UNITS_HEAD, h)
        for n, unit in enumerate(middle):
            load_unit(sp, *unit, U_OUT2 + n)

        gu2 = a["w_gate_up_2"][0].rearrange("(p k) n -> p k n", k=KD)
        down2 = a["w_down_2"][0].rearrange("(c p k) n -> c p (k n)", k=2, p=P)
        swiglu_loads(lambda c: gu2[:, :, bass.ds(c * FF, FF)], lambda c: gu2[:, :, bass.ds(c * FF + D_FF, FF)],
                     lambda c: down2[bass.ds(c, 1)].rearrange("c p n -> p (c n)"), U_FFN, STEPS_FFN)
        for n, unit in enumerate(last):
            load_unit(sp, *unit, U_PLE + n)
        for n in range(4):
            t, at = n // 2, slice(512 * (n % 2), 512 * (n % 2) + 512)
            sp.wait_ge(sem("result"), n + 1)
            sp.dma_start(out[0].rearrange("(t p) d -> p t d", p=P)[:, t, at], embed[:, t, at]).then_inc(sem("stored"), 16)
        sp.wait_ge(sem("stored"), 16 * 4)

    @block.gpsimd
    def _(pool):
        nc.gpsimd.memset(one_col[:], 1.0).then_inc(sem("one_set"), 1)
        pool.wait_ge(sem("mem_loaded1"), 16)
        for dst, src in small_loads:
            pool.dma_start(dst, src).then_inc(sem("constants_loaded"), 16)
        pool.wait_ge(sem("x_cross"), 2)
        nc.gpsimd.memset(ones[:], 1.0).then_inc(sem("ones_set"), 1)
        pool.wait_ge(sem("x_rnn"), 2)
        pool.dma_start(fin_g[:], row(a["g_final_2"]).to_broadcast([P, D])).then_inc(sem("last_loaded"), 16)
        pool.dma_start(p_in[:], a["p_2"][0, 0].rearrange("(t p) n -> p t n", p=P)).then_inc(sem("last_loaded"), 16)

    @block.scalar
    def _(act):
        for dst, src in first_loads:
            act.dma_start(dst, src).then_inc(sem("first_loaded"), 16)

        chain = [0]

        def then(ins):
            chain[0] += 1
            ins.then_inc(sem("act_chain"), 1)
            act.wait_ge(sem("act_chain"), chain[0])

        split = [0]

        def splits_to(u):
            while split[0] < u:
                split_hi(act, cols_of(split[0]), split[0])
                split[0] += 1

        def root(dst, src, inverse_ready, n=1):
            act.wait_ge(sem(inverse_ready), n)
            return nc.scalar.activation(dst, src, ACT.Sqrt)

        def warm_up(func):
            then(nc.scalar.activation(warm[:], one_col[:], func))

        def squares(src, junk, ready):
            for s_, n in ready:
                act.wait_ge(sem(s_), n)
            nc.scalar.activation(junk[:, 0], src[:, 0], ACT.Square, accum_out=sums[:, 0:1]).then_inc(sem("norm_sums"), 1)

        def roots(name):
            n = NORMS.index(name) + 1
            root(rstd[:], inverse[:], "norm_inverse", n).then_inc(sem("norm_rstd"), 1)
            act.wait_ge(sem("norm_rstd"), n)

        def stats(src, junk, ready, name):
            warm_up(ACT.Sqrt)
            squares(src, junk, ready)
            roots(name)

        def high_parts(name, gain, pairs=range(4)):
            for n in pairs:
                b = product(act, f"{name}{n}")
                if gain is None:
                    ins = nc.scalar.activation(xT_hi[:, 2 * n:2 * n + 2].rearrange("p k t -> p (k t)"), b[:, :], ACT.Copy)
                else:
                    for j in range(2):
                        k = 2 * n + j
                        ins = nc.scalar.activation(xT_hi[:, k], b[:, 256 * j:256 * j + 256], ACT.Copy, scale=norm_g[:, gain, k:k + 1])
                ins.then_inc(sem("xT_hi"), 1)

        def norm(src, ready, name, gain):
            squares(src, xs, ready)
            high_parts(name, gain)
            roots(name)

        def head_squares(src_of, n, width, name, junk):
            for m in range(n):
                to = junk[:, width * (m % 8):width * (m % 8) + width]
                ins = nc.scalar.activation(to, src_of(m), ACT.Square, accum_out=head_sums[:, m:m + 1])
                if m == 7 and n > 8:
                    then(ins)
            ins.then_inc(sem(name + "_sums"), 1)

        def copy_to(dst, name, rows=P, **kw):
            b = product(act, name)
            n = int(np.prod(dst.shape[1:]))
            src = b[0:rows, 0:n]
            if len(dst.shape) == 3:
                src = src.rearrange("p (k n) -> p k n", k=dst.shape[1])
            return nc.scalar.activation(dst, src, ACT.Copy, **kw)

        act.wait_ge(sem("one_set"), 1)
        warm_up(ACT.Sqrt)
        squares(xs, k_cross, [("mem_loaded0", 16)])
        act.wait_ge(sem("first_loaded"), 16 * len(first_loads))
        roots("mem")
        high_parts("mem", MEM_G, range(2))
        splits_to(1)
        high_parts("mem", MEM_G, range(2, 4))
        splits_to(2)

        def tables():
            act.wait_ge(sem("constants_loaded"), 16 * len(small_loads))
            frees(copy_to(vec[:], "vec"), "vec")
            act.wait_ge(sem("angles"), 1)
            nc.scalar.activation(trig[:, 1].rearrange("p t n -> p (t n)"), angle[:, 0], ACT.Sin)
            nc.scalar.activation(angle[:, 1], angle[:, 0], ACT.Abs).then_inc(sem("angles_abs"), 1)
            act.wait_ge(sem("angles_turned"), 1)
            nc.scalar.activation(trig[:, 0].rearrange("p t n -> p (t n)"), angle[:, 2], ACT.Sin).then_inc(sem("trig"), 1)
            been_read(act, "vec")
            then(nc.scalar.activation(lam_t[:, 0], lam, ACT.Abs))
            nc.scalar.activation(lam_t[:, 1], lam_t[:, 0], ACT.Exp, scale=-1.0).then_inc(sem("lambda_exp"), 1)
            nc.scalar.activation(r_hi[:], r_w[:], ACT.Copy).then_inc(sem("router_hi"), 1)

        for c in range(2):
            splits_to(2 * c + 4)
            act.wait_ge(unit_done, 2 * c + 2)
            for t in range(T):
                ins = nc.scalar.activation(k_cross[:, t, 512 * c:512 * c + 512], pair(C_K + c)[t][:, :], ACT.Copy,
                                           scale=rstd[:, t:t + 1])
            ins.then_inc(chunk_freed[(C_K + c) % 2], 1)
        chunk_read(act, C_K)
        chunk_read(act, C_K + 1)
        head_squares(lambda m: k_cross[:, m // 4, 256 * (m % 4):256 * (m % 4) + 256], 8, 256, "kc", flat3(xs[:]))
        root(head_rstd[:, 0:8], head_inv[:, 0:8], "kc_inverse").then_inc(sem("kc_rstd"), 1)
        for c in range(2):
            splits_to(2 * c + 8)
            act.wait_ge(unit_done, 2 * c + 6)
            for t in range(T):
                ins = nc.scalar.activation(v_cross[:, t, 512 * c:512 * c + 512], pair(C_V + c)[t][:, :], ACT.Copy,
                                           scale=rstd[:, t:t + 1])
            ins.then_inc(chunk_freed[(C_V + c) % 2], 1)
            if c == 0:
                tables()
                for n in range(4):
                    for j in range(2):
                        ins = copy_half(act, f"kc{n}", j, k_crossT[:, 2 * n + j], cqk_g[:, 1, j:j + 1])
                    frees(ins, f"kc{n}")
                squares(x, xs, [("x_loaded", 16)])
        splits_to(U_LAT + 2)
        high_parts("attn", ATTN_G)
        chunk_read(act, C_V + 1)
        roots("attn")

        splits_to(U_LAT + 4)
        act.wait_ge(unit_done, U_LAT + 2)
        for t in range(T):
            ins = nc.scalar.activation(latent[:, t], pair(C_LAT)[t][:, 0:448], ACT.Copy, scale=rstd[:, t:t + 1])
        ins.then_inc(chunk_freed[C_LAT % 2], 1)
        chunk_read(act, C_LAT)
        for m in range(4):
            src = latent[:, m % 2, 0:256] if m < 2 else latent[:, m % 2, 256:384]
            ins = nc.scalar.activation(hidden[:, 0, 0:src.shape[1]], src, ACT.Square, accum_out=lat_sums[:, m:m + 1])
            if m < 3:
                then(ins)
        ins.then_inc(sem("lat_sums"), 1)
        root(lat_rstd[:], lat_inv[:], "lat_inverse").then_inc(sem("lat_rstd"), 1)

        def wide_copy(c, u, dst, name=None):
            act.wait_ge(unit_done, u + 1)
            for t in range(T):
                ins = nc.scalar.activation(dst[:, t], pair(c)[t][:, :], ACT.Copy, scale=rstd[:, t:t + 1])
            ins.then_inc(chunk_freed[c % 2], 1)

        splits_to(U_RK + 2)
        wide_copy(C_RQ, U_RQ + 1, r_q.rearrange("p (t n) -> p t n", t=T))
        for k in range(2):
            ins = copy_half(act, "cq", k, cT_hi[:, k], qn_g[:, k:k + 1])
        ins.then_inc(sem("cT_hi"), 1)
        copy_half(act, "ckv", 0, cT_hi[:, 2], kvn_g[:, 0:1]).then_inc(sem("cT_hi"), 1)
        splits_to(U_RV + 2)
        wide_copy(C_RK, U_RK + 1, r_k.rearrange("p (t n) -> p t n", t=T))
        splits_to(U_UKV + 1)
        wide_copy(C_RV, U_RV + 1, r_v)
        splits_to(U_RG + 1)
        act.wait_ge(unit_done, U_UQ + 1)
        for c in range(2):
            for t in range(T):
                ins = nc.scalar.activation(q_mla[:, t, 2 * c:2 * c + 2].rearrange("p h d -> p (h d)"),
                                           pair(C_UQ + c)[t][:, 0:384], ACT.Copy)
            ins.then_inc(chunk_freed[(C_UQ + c) % 2], 1)
        for n in range(2):
            frees(copy_to(r_qT[:, 2 * n:2 * n + 2], f"rq{n}"), f"rq{n}")
        for n in range(2):
            frees(copy_to(r_kT[:, 2 * n:2 * n + 2], f"rk{n}"), f"rk{n}")
        splits_to(U_RG + 2)
        act.wait_ge(unit_done, U_UKV + 1)
        for c in range(2):
            for t in range(T):
                src = pair(C_UKV + c)[t][:, :].rearrange("p (h w d) -> p h w d", h=2, w=2)
                nc.scalar.activation(k_mla[:, t, 2 * c:2 * c + 2, 0:NOPE], src[:, :, 0], ACT.Copy)
                ins = nc.scalar.activation(v_mla[:, t, 2 * c:2 * c + 2], src[:, :, 1], ACT.Copy)
            ins.then_inc(chunk_freed[(C_UKV + c) % 2], 1)
        chunk_read(act, C_UKV)
        chunk_read(act, C_UKV + 1)
        act.wait_ge(sem("k_pe_placed"), 1)
        head_squares(lambda m: (q_mla if m < 8 else k_mla)[:, m // 4 % 2, m % 4], 16, QK, "qk", turned[:, 2048:])
        root(head_rstd[:], head_inv[:], "qk_inverse").then_inc(sem("qk_rstd"), 1)
        splits_to(U_OUT + 2)

        def turned_copies(w, dst, positions=False):
            for n in range(2):
                name = "qk"[w] + "nr"[positions] + str(n)
                if positions:
                    ins = copy_to(dst[0:ROPE, 2 * n:2 * n + 2], name, rows=ROPE)
                else:
                    ins = copy_to(dst[:, 2 * n:2 * n + 2], name, scale=nope_g[:, w:w + 1])
                frees(ins, name)

        turned_copies(0, qT_n)
        root(gn_rstd[:], gn_inv[:], "gn_inverse").then_inc(sem("gn_rstd"), 1)
        act.wait_ge(sem("norm_half"), NORMS.index("attn") + 1)
        act.wait_ge(unit_done, U_RG + 2)
        for t in range(T):
            nc.scalar.activation(r_gate[:, t], pair(C_RG)[t][:, :], ACT.Tanh, scale=half_rstd[:, t:t + 1]).then_inc(sem("rg_tanh"), 1)
        turned_copies(0, qT_r, positions=True)
        turned_copies(1, kT_n)
        turned_copies(1, kT_r, positions=True)
        for m in range(8):
            act.wait_ge(sem("masked"), 1 if m < 4 else m // 2)
            part_ = scores[:, 128 * m:128 * m + 128] if m < 4 else scores[:, 512 + 256 * (m - 4):768 + 256 * (m - 4)]
            nc.scalar.activation(part_, part_, ACT.Exp, bias=neg_top[:, m:m + 1], scale=q_scale[:, m:m + 1],
                                 accum_out=exp_sum[:, m:m + 1]).then_inc(sem("exped"), 1)
        for n in range(3):
            frees(copy_to(probsT[:, 512 * n:512 * n + 512], f"pT{n}"), f"pT{n}")
        high_parts("cat", None)
        splits_to(U_CQ + 2)

        norm(x, [("x_attn", 2)], "crossq", CROSS_G)
        for c in range(2):
            splits_to(U_CQ + 2 * c + 4)
            wide_copy(C_CQ + c, U_CQ + 2 * c + 1, q_cross[:, :, 512 * c:512 * c + 512])
            chunk_read(act, C_CQ + c)
            for t in range(T):
                for h in (2 * c, 2 * c + 1):
                    ins = nc.scalar.activation(xs[:, t, 256 * h:256 * h + 256], q_cross[:, t, 256 * h:256 * h + 256], ACT.Square,
                                               accum_out=head_sums[:, 4 * t + h:4 * t + h + 1])
        ins.then_inc(sem("qc_sums"), 1)
        for n in (0, 2):
            for j in range(2):
                ins = copy_half(act, f"qc{n}", j, q_crossT[:, 2 * n + j], cqk_g[:, 0, j:j + 1])
            frees(ins, f"qc{n}")
        root(head_rstd[:, 0:8], head_inv[:, 0:8], "qc_inverse").then_inc(sem("qc_rstd"), 1)
        warm_up(ACT.Exp)
        for n in range(4):
            t, pair_of = n // 2, n % 2
            act.wait_ge(sem("cross_top"), n + 1)
            b = bank[where[f"cs{n}"][0]]
            for j in range(2):
                m = 2 * n + j
                ins = nc.scalar.activation(c_scores[:, t, 2 * pair_of + j], b[:, 256 * j:256 * j + 256], ACT.Exp,
                                           bias=neg_top[:, m:m + 1], scale=q_scale[:, m:m + 1], accum_out=exp_sum[:, m:m + 1])
            frees(ins, f"cs{n}")
        for n in range(4):
            frees(copy_to(c_probsT[:, n // 2, 2 * (n % 2):2 * (n % 2) + 2], f"cp{n}"), f"cp{n}")
        high_parts("catc", None)
        splits_to(U_MOE + 2)
        norm(x, [("x_cross", 2)], "moe", MOE_G)
        for t in range(T):
            nc.scalar.activation(xs_hi[:, t], x[:, t], ACT.Copy, scale=rstd[:, t:t + 1]).then_inc(sem("xs_hi"), 1)
        frees(nc.scalar.activation(logitsT, product(act, "router")[0:CHOICES, 0:T * P], ACT.Copy), "router")
        b = product(act, "logits")
        for t in range(T):
            ins = nc.scalar.activation(logits[:, t], b[:, CHOICES * t:CHOICES * t + CHOICES], ACT.Copy, scale=rstd[:, t:t + 1])
        frees(ins, "logits")
        act.wait_ge(sem("route_diffs"), 1)
        nc.scalar.activation(exps[:], diffs[:], ACT.Exp).then_inc(sem("route_exps"), 1)

        def swiglu(name, base, steps, scale_of):
            def tanhs(e):
                act.wait_ge(unit_done, up_done(base, e))
                for t in range(T):
                    nc.scalar.activation(silu_t[:, t], bank[4 + t][:, 0:FF], ACT.Tanh, scale=scale_of(t)).then_inc(sem(name + "_tanh"), 1)

            def high(e):
                act.wait_ge(sem(name + "_turned"), e + 1)
                nc.scalar.activation(aT_hi[:].rearrange("p k t -> p (k t)"), bank[6][:, :], ACT.Copy).then_inc(sem(name + "_aT_hi"), 1)

            def step(i, first=False):
                if not first:
                    split_hi(act, SLOT, base + 1, 3, i)
                split_hi(act, SLOT, base + 2, 3, i)
                tanhs(i)
                split_hi(act, SLOT, base + 3, 3, i)
                high(i)

            step(0, first=True)
            with act.Fori(1, steps - 1) as i:
                step(i)
            split_hi(act, SLOT, base + 1 + 3 * (steps - 1))
            split_hi(act, SLOT, base + 3 * steps - 1)
            tanhs(steps - 1)
            high(steps - 1)

        def experts(name, st, base, groups, before_sums=None):
            for k in range(KD):
                act.wait_ge(sem(name + "_gathered"), k + 1)
                gain = norm_g[:, MOE_G, k:k + 1]
                ins = nc.scalar.activation(xg_hi[:, k], part_bank(k)[:, 0:P], ACT.Copy, scale=gain)
                if groups > 1:
                    ins = nc.scalar.activation(later_hi[:, k], part_bank(k)[:, P:P * groups], ACT.Copy, scale=gain)
                ins.then_inc(sem(name + "_xg_hi"), 1)
            act.wait_ge(sem(name + "_gates"), 1)
            nc.scalar.activation(slot_gates[:, 0:PER_GROUP * groups], bank[7][:, 0:PER_GROUP * groups],
                                 ACT.Copy).then_inc(sem(name + "_slot_gates"), 1)

            def tanh_high(g, j, next_up):
                act.wait_ge(st.unit_done, g * PER_TURN + (up_unit(base, j) + 1))
                nc.scalar.activation(silu_t[:, 0], bank[6][:, 0:FF], ACT.Tanh, scale=0.5).then_inc(sem(name + "_tanh"), 1)
                if j == LAST and next_up:
                    nc.scalar.activation(xg_hi[:], later_hi[:, :, bass.ds(g * P, P)].bitcast(F32),
                                         ACT.Copy).then_inc(sem(name + "_moved"), 1)
                if next_up:
                    split_hi(act, SLOT, up_unit(base, j + 1), PER_TURN, g, st)
                act.wait_ge(sem(name + "_turned"), eighths(g, j + 1))
                nc.scalar.activation(flat3(aT_hi[:])[:, 0:FF], bank[7][:, 0:FF], ACT.Copy).then_inc(sem(name + "_aT_hi"), 1)

            def sums(g, done):
                act.wait_ge(st.unit_done, done)
                for c in range(2):
                    nc.scalar.activation(y_hi[:, c], bank[4 + c][:, :], ACT.Copy).then_inc(sem(name + "_y_hi"), 1)

            def step(g, j):
                if j:
                    split_hi(act, SLOT, up_unit(base, j) + 1, PER_TURN, g, st)
                split_hi(act, SLOT, gate_unit(base, j + 1), PER_TURN, g, st)
                tanh_high(g, j, True)
                if j == 0:
                    for n in range((groups + 1) // 2):
                        act.wait_ge(sem(name + "_sel_turned"), n + 1)
                        w = min(groups, 2)
                        nc.scalar.activation(token_of[:, 2 * n:2 * n + w].rearrange("p g t -> p (g t)"), bank[2 + n][:, 0:256 * w],
                                             ACT.Copy).then_inc(sem(name + "_banks_free"), 1)
                if j == 4:
                    act.wait_ge(sem(name + "_banks_free"), (groups + 1) // 2)
                    nc.scalar.activation(token_now[:], token_of[:, bass.ds(g, 1)].rearrange("p g t -> p (g t)").bitcast(F32),
                                         ACT.Copy).then_inc(sem(name + "_token_now"), 1)
                if j == PER_GROUP:
                    sums(g, g * PER_TURN + (up_unit(base, j) + 2))

            def tail(g):
                split_hi(act, SLOT, up_unit(base, LAST) + 1, PER_TURN, g, st)
                split_hi(act, SLOT, last_down(base, groups), st=st)
                tanh_high(g, LAST, False)
                if before_sums:
                    before_sums()
                sums(g, last_down(base, groups) + 1)

            expert_steps(act, groups, step, tail)

        def head_splits():
            for u in (U_HEADS, U_HEADS + 1):
                split_hi(act, SLOT, u)

        over_flag = []

        def early_head_splits():
            over_flag.append(overflow(act))
            with act.If(over_flag[0] < 1):
                head_splits()

        experts("moe", main, U_MOE, GROUPS, early_head_splits)
        with act.If(over_flag[0] > 0):
            act.wait_ge(unit_done, U_HEADS)
            for u in range(2):
                split_hi(act, SLOT, u, st=over)
            experts("over", over, 0, 1)
            act.wait_ge(sem("x_over"), 4)
            head_splits()
        stats(x, xs, [("x_moe", 4)], "mix")
        nc.scalar.activation(xs[:, 0], x[:, 0], ACT.Copy, scale=rstd[:, 0:1]).then_inc(sem("mix_scaled"), 1)
        high_parts("mix", MIX_G)

        with act.Fori(0, HEADS) as h:
            def unit(j):
                split_hi(act, 512 if j in (RG_R, RG_I) else SLOT, U_HEADS + j, UNITS_HEAD, h)

            def done(j):
                act.wait_ge(unit_done, h * UNITS_HEAD + (U_HEADS + j + 1))

            def blocks(b):
                return b[:, :].rearrange("p (f t) -> p f t", f=2)

            unit(C_CONV)
            done(RX)
            nc.scalar.activation(xpad[:, :, 3:259], blocks(bank[0]), ACT.Copy).then_inc(sem("rx_copied"), 1)
            unit(X_CONV)
            act.wait_ge(sem("conv4_done"), h + 1)
            nc.scalar.activation(rx_hi[:], rx[:].rearrange("p f t -> p (f t)"), ACT.Copy).then_inc(sem("rx_hi"), 1)
            done(GELU)
            nc.scalar.activation(y_sq[:], bank[1][:, :], ACT.Square)
            nc.scalar.activation(y_in[:], bank[1][:, :], ACT.Copy).then_inc(sem("y_copied"), 1)
            unit(RG_R)
            act.wait_ge(sem("gelu_inner"), h + 1)
            nc.scalar.activation(y_tanh[:], y_sq[:], ACT.Tanh, scale=float(np.sqrt(2 / np.pi))).then_inc(sem("gelu_tanh"), 1)
            done(C_CONV)
            nc.scalar.activation(c_in[:], bank[2][:, :], ACT.Copy).then_inc(sem("c_copied"), 1)
            unit(B_CONV)
            unit(RG_I)
            done(RG_R)
            for f in range(2):
                nc.scalar.activation(r_tanh[:, f], blocks(bank[7])[:, f], ACT.Tanh, scale=0.5,
                                     bias=half_br[:, bass.ds(h * 2 + f, 1)]).then_inc(sem("r_tanh"), 1)
            unit(G_R)
            act.wait_ge(sem("r_tanh"), h * 2 + 2)
            for f in range(2):
                nc.scalar.activation(tau[:, f], r_tanh[:, f], ACT.Tanh, scale=softplus2[:, bass.ds(h * 2 + f, 1)],
                                     bias=softplus2[:, bass.ds(h * 2 + f, 1)]).then_inc(sem("tau"), 1)
            unit(G_C)
            done(RG_I)
            for f in range(2):
                nc.scalar.activation(i_tanh[:, f], blocks(bank[0])[:, f], ACT.Tanh, scale=0.5,
                                     bias=half_bi[:, bass.ds(h * 2 + f, 1)]).then_inc(sem("i_tanh"), 1)
            act.wait_ge(sem("tau"), h * 2 + 2)
            nc.scalar.activation(root_tau[:], tau[:], ACT.Sqrt).then_inc(sem("root_tau"), 1)
            split_hi(act, SLOT, U_HEADS + 9, UNITS_HEAD, h)
            done(G_R)
            nc.scalar.activation(gr_tanh[:], bank[5][:, :], ACT.Tanh, scale=0.5).then_inc(sem("gr_tanh"), 1)
            split_hi(act, SLOT, U_HEADS + 10, UNITS_HEAD, h)
            done(G_C)
            nc.scalar.activation(gc_tanh[:], bank[6][:, :], ACT.Tanh, scale=0.5).then_inc(sem("gc_tanh"), 1)
            act.wait_ge(sem("merged"), h + 1)
            nc.scalar.activation(flat3(mT_hi[:])[:, bass.ds(h * 512, 512)], merged[:], ACT.Copy, scale=0.5).then_inc(sem("mT_hi"), 1)

        split[0] = U_OUT2 + 2
        splits_to(U_FFN + 2)
        norm(x, [("x_rnn", 2)], "ffn", FFN_G)
        act.wait_ge(sem("norm_half"), NORMS.index("ffn") + 1)
        swiglu("ffn", U_FFN, STEPS_FFN, lambda t: half_rstd[:, t:t + 1])
        split[0] = U_PLE
        splits_to(U_PLE + 2)
        copy_to(aT_hi[:], "pT").then_inc(sem("pT_hi"), 1)
        norm(x, [("x_ffn", 4)], "ple", PLE_G)
        act.wait_ge(sem("norm_half"), NORMS.index("ple") + 1)
        act.wait_ge(unit_done, U_PLE + 1)
        for c in range(2):
            for t in range(T):
                ins = nc.scalar.activation(embed[:, t, 512 * c:512 * c + 512], pair(C_PLE + c)[t][:, :], ACT.Copy)
            ins.then_inc(chunk_freed[(C_PLE + c) % 2], 1)
        for c in range(2):
            splits_to(min(U_END, U_PLE + 2 * c + 5))
            act.wait_ge(unit_done, U_PLE + 2 * c + 3)
            for t in range(T):
                nc.scalar.activation(ple_gate[:, t, 512 * c:512 * c + 512], pair(C_GATE + c)[t][:, :], ACT.Tanh,
                                     scale=half_rstd[:, t:t + 1]).then_inc(sem("ple_tanh"), 1)
        stats(x, xs, [("x_ple", 3)], "final")

    @block.vector
    def _(dve):
        chain = [0]

        def then(ins):
            chain[0] += 1
            ins.then_inc(sem("dve_chain"), 1)
            dve.wait_ge(sem("dve_chain"), chain[0])

        split = [0]

        def splits_to(u):
            while split[0] < u:
                split_lo(dve, cols_of(split[0]), split[0])
                split[0] += 1

        tt, ts, stt = nc.vector.tensor_tensor, nc.vector.tensor_scalar, nc.vector.scalar_tensor_tensor

        def inverse_of(dst, src, width, ready, n, signal):
            dve.wait_ge(sem(ready), n)
            then(ts(dst, src, 1.0 / width, EPS, ALU.mult, ALU.add))
            nc.vector.reciprocal(dst, dst).then_inc(sem(signal), 1)

        def low_half(name, j, lo, hi, gain):
            b = bank[where[name][0]]
            return stt(lo, b[:, 256 * j:256 * j + 256], gain, hi.bitcast(F32), ALU.mult, ALU.subtract)

        def low_parts(name, gain, pairs=range(4)):
            for n in pairs:
                high_ready(dve, name, n + 1)
                b = bank[where[f"{name}{n}"][0]]
                if gain is None:
                    ins = tt(flat3(xT_lo[:, 2 * n:2 * n + 2]), b[:, :], flat3(xT_hi[:, 2 * n:2 * n + 2]).bitcast(F32), ALU.subtract)
                else:
                    for j in range(2):
                        k = 2 * n + j
                        ins = low_half(f"{name}{n}", j, xT_lo[:, k], xT_hi[:, k], norm_g[:, gain, k:k + 1])
                frees(ins, f"{name}{n}")

        def stats(src, junk, ready, name):
            for s_, n in ready:
                dve.wait_ge(sem(s_), n)
            then(nc.vector.tensor_tensor_reduce(junk[:, 1], src[:, 1], src[:, 1], 1.0, 0.0, ALU.mult, ALU.add, sums[:, 1:2]))
            inverse_of(inverse[:], sums[:], D, "norm_sums", NORMS.index(name) + 1, "norm_inverse")

        def halves(name):
            dve.wait_ge(sem("norm_rstd"), NORMS.index(name) + 1)
            ts(half_rstd[:], rstd[:], 0.5, None, ALU.mult).then_inc(sem("norm_half"), 1)

        def norm(ready, name, gain):
            stats(x, xs, ready, name)
            low_parts(name, gain)
            halves(name)

        def rope(src, dst, lo, hi, ta, tb):
            n = hi - lo
            cos, sin = (trig[:, w, :, lo:hi].unsqueeze(2).to_broadcast([P, T, HEADS, n]) for w in (0, 1))
            x1, x2 = src[:, :, :, 0:n], src[:, :, :, n:2 * n]
            tt(dst[:, :, :, 0:n], x1, cos, ALU.mult)
            tt(ta, x2, sin, ALU.mult)
            tt(dst[:, :, :, n:2 * n], x2, cos, ALU.mult)
            then(tt(tb, x1, sin, ALU.mult))
            tt(dst[:, :, :, 0:n], dst[:, :, :, 0:n], ta, ALU.subtract)
            return tt(dst[:, :, :, n:2 * n], dst[:, :, :, n:2 * n], tb, ALU.add)

        def heads4(v, d):
            return v.rearrange("p (t h d) -> p t h d", t=T, d=d)

        tmp_a, tmp_b = silu_t[:].rearrange("p t f -> p (t f)"), silu_g[:].rearrange("p t f -> p (t f)")

        stats(xs, k_cross, [("mem_loaded1", 16)], "mem")
        dve.wait_ge(sem("first_loaded"), 16 * len(first_loads))
        low_parts("mem", MEM_G, range(2))
        splits_to(1)
        low_parts("mem", MEM_G, range(2, 4))
        halves("mem")
        splits_to(2)
        splits_to(6)
        inverse_of(head_inv[:, 0:8], head_sums[:, 0:8], CROSS, "kc_sums", 1, "kc_inverse")
        dve.wait_ge(sem("kc_rstd"), 1)
        for m in range(8):
            part_ = k_cross[:, m // 4, 256 * (m % 4):256 * (m % 4) + 256]
            ins = ts(part_, part_, head_rstd[:, m:m + 1], None, ALU.mult)
        ins.then_inc(sem("kc_scaled"), 1)
        dve.wait_ge(sem("constants_loaded"), 16 * len(small_loads))
        then(nc.vector.tensor_copy(pos_f[:], pos_i[:]))
        for t in range(T):
            ins = ts(angle[:, 0, 96 * t:96 * t + 96], inv_freq, pos_f[:, t:t + 1], None, ALU.mult)
        then(ins)
        then(ts(angle[:, 3], angle[:, 0], float(np.float32(1 / (2 * np.pi))), MAGIC, ALU.mult, ALU.add))
        then(ts(angle[:, 3], angle[:, 3], MAGIC, None, ALU.subtract))
        for piece in two_pi_parts():
            then(stt(angle[:, 0], angle[:, 3], -piece, angle[:, 0], ALU.mult, ALU.add))
        ts(angle[:, 0], angle[:, 0], PI_BELOW, -PI_BELOW, ALU.min, ALU.max).then_inc(sem("angles"), 1)
        splits_to(U_LAT)
        dve.wait_ge(sem("angles_abs"), 1)
        ts(angle[:, 2], angle[:, 1], -1.0, float(np.float32(np.pi / 2)), ALU.mult, ALU.add).then_inc(sem("angles_turned"), 1)
        stats(x, xs, [("x_loaded", 16)], "attn")
        splits_to(U_LAT + 1)
        splits_to(U_LAT + 2)
        low_parts("attn", ATTN_G)
        halves("attn")

        splits_to(U_LAT + 4)
        dve.wait_ge(sem("lat_sums"), 1)
        ts(lat_inv[:, 0:2], lat_sums[:, 0:2], 1.0 / 256, EPS, ALU.mult, ALU.add)
        then(ts(lat_inv[:, 2:4], lat_sums[:, 2:4], 1.0 / 128, EPS, ALU.mult, ALU.add))
        nc.vector.reciprocal(lat_inv[:], lat_inv[:]).then_inc(sem("lat_inverse"), 1)
        dve.wait_ge(sem("lat_rstd"), 1)
        for t in range(T):
            ts(latent[:, t, 0:256], latent[:, t, 0:256], lat_rstd[:, t:t + 1], None, ALU.mult)
            ins = ts(latent[:, t, 256:384], latent[:, t, 256:384], lat_rstd[:, 2 + t:3 + t], None, ALU.mult)
        ins.then_inc(sem("lat_scaled"), 1)
        splits_to(U_RK + 2)
        dve.wait_ge(sem("cT_hi"), 1)
        for k in range(2):
            ins = low_half("cq", k, cT_lo[:, k], cT_hi[:, k], qn_g[:, k:k + 1])
        frees(ins, "cq")
        dve.wait_ge(sem("cT_hi"), 2)
        frees(low_half("ckv", 0, cT_lo[:, 2], cT_hi[:, 2], kvn_g[:, 0:1]), "ckv")
        dve.wait_ge(sem("trig"), 1)
        chunk_read(dve, C_RQ)
        rope(heads4(r_q, 128), heads4(rot_q, 128), 32, 96, heads4(tmp_a, 64), heads4(tmp_b, 64)).then_inc(sem("rot_ready"), 1)
        dve.wait_ge(sem("rot_ready"), 1)
        splits_to(U_RV + 2)
        chunk_read(dve, C_RK)
        rope(heads4(r_k, 128), heads4(rot_k, 128), 32, 96, heads4(tmp_a, 64), heads4(tmp_b, 64)).then_inc(sem("rot_ready"), 1)
        dve.wait_ge(sem("rot_ready"), 2)
        splits_to(U_RG + 1)
        nc.vector.tensor_copy(k_mla[:, :, :, NOPE:QK], latent[:, :, 384:448].unsqueeze(2).to_broadcast([P, T, HEADS, ROPE]))\
            .then_inc(sem("k_pe_placed"), 1)
        splits_to(U_RG + 2)
        for n in range(2):
            b = product(dve, f"rs{n}")
            frees(tt(r_s0[:, 2 * n:2 * n + 2], b[:, :].rearrange("p (h q) -> p h q", h=2), decay[:, 2 * n:2 * n + 2], ALU.mult), f"rs{n}")
        b = product(dve, "rs2")
        frees(tt(r_s1, b[:, :].rearrange("p (h q) -> p h q", h=HEADS), decay[:, :, 0:P], ALU.mult), "rs2")
        chunk_read(dve, C_UQ)
        chunk_read(dve, C_UQ + 1)
        gained = heads4(flat3(hidden[:]), ROPE)
        for w, v in enumerate((q_mla, k_mla)):
            gain = rope_g[:, w].unsqueeze(1).unsqueeze(1).to_broadcast([P, T, HEADS, ROPE])
            then(tt(gained, v[:, :, :, NOPE:QK], gain, ALU.mult))
            rope(gained, qk_r[w], 0, 32, heads4(tmp_a[:, 0:256], 32), heads4(tmp_b[:, 0:256], 32)).then_inc(sem("qk_turned"), 1)
            dve.wait_ge(sem("qk_turned"), w + 1)
        inverse_of(head_inv[:], head_sums[:], QK, "qk_sums", 1, "qk_inverse")
        dve.wait_ge(sem("qk_rstd"), 1)
        ts(q_scale[:], head_rstd[:, 0:8], QK ** -0.5, None, ALU.mult)
        k_rstd = head_rstd[:, 8:16].rearrange("p (t h) -> p t h", t=T).unsqueeze(3)
        tt(k_mla[:, :, :, 0:NOPE], k_mla[:, :, :, 0:NOPE], k_rstd.to_broadcast([P, T, HEADS, NOPE]), ALU.mult)
        tt(qk_r[1], qk_r[1], k_rstd.to_broadcast([P, T, HEADS, ROPE]), ALU.mult).then_inc(sem("qk_turned"), 1)
        for t in range(T):
            b = product(dve, f"ro{t}")
            for h in range(HEADS):
                ins = nc.vector.bn_stats(gn_stats[:, 4 * t + h], b[:, 128 * h:128 * h + 128])
        then(ins)
        for m in range(T * HEADS):
            ins = nc.vector.bn_aggr(gn_mv[:, m], gn_stats[:, m])
        then(ins)
        then(ts(gn_inv[:], gn_mv[:, :, 1], EPS, None, ALU.add))
        nc.vector.reciprocal(gn_inv[:], gn_inv[:]).then_inc(sem("gn_inverse"), 1)
        dve.wait_ge(sem("gn_rstd"), 1)
        for t in range(T):
            b = bank[where[f"ro{t}"][0]]
            for h in range(HEADS):
                m = 4 * t + h
                ins = ts(xs[:, t, 512 + 128 * h:640 + 128 * h], b[:, 128 * h:128 * h + 128], gn_mv[:, m, 0:1],
                         gn_rstd[:, m:m + 1], ALU.subtract, ALU.mult)
            frees(ins, f"ro{t}")
        been_read(dve, "ro1")
        for t in range(T):
            stt(xs[:, t, 512:1024], xs[:, t, 512:1024], half_rstd[:, t:t + 1], gn_g[:], ALU.mult, ALU.mult).then_inc(sem("gn_gained"), 1)
        for t in range(T):
            dve.wait_ge(sem("rg_tanh"), t + 1)
            ins = stt(r_gate[:, t], r_gate[:, t], 1.0, pair(C_RG)[t][:, :], ALU.add, ALU.mult)
        ins.then_inc(chunk_freed[C_RG % 2], 1)
        chunk_read(dve, C_RG)
        for t in range(T):
            tt(xs[:, t, 512:1024], xs[:, t, 512:1024], r_gate[:, t], ALU.mult).then_inc(sem("cat_scaled"), 1)
        splits_to(U_OUT + 2)
        for n in range(3):
            b, at = product(dve, f"s{n}"), 0 if n == 0 else 2 + 2 * n
            heads, keys = (HEADS, P) if n == 0 else (2, 2 * P)
            part_ = scores[:, 512 * n:512 * n + 512].rearrange("p (h k) -> p h k", h=heads)
            frees(tt(part_, b[:, :].rearrange("p (h k) -> p h k", h=heads),
                     mask[:, 2 * P - keys:].unsqueeze(1).to_broadcast([P, heads, keys]), ALU.add), f"s{n}")
            been_read(dve, f"s{n}")
            then(nc.vector.tensor_reduce(top[:, at:at + heads], part_, AX, ALU.max))
            stt(neg_top[:, at:at + heads], top[:, at:at + heads], -1.0, q_scale[:, at:at + heads], ALU.mult, ALU.mult)\
                .then_inc(sem("masked"), 1)
        dve.wait_ge(sem("exped"), 8)
        then(nc.vector.reciprocal(exp_inv[:, 0:8], exp_sum[:, 0:8]))
        for t in range(T):
            b = product(dve, f"o{t}")
            ins = tt(xs[:, t, 0:512].rearrange("p (h d) -> p h d", h=HEADS), b[:, :].rearrange("p (h d) -> p h d", h=HEADS),
                     exp_inv[:, 4 * t:4 * t + 4].unsqueeze(2).to_broadcast([P, HEADS, P]), ALU.mult)
            frees(ins, f"o{t}")
        low_parts("cat", None)

        def add_chunk(c, chunk, last_unit, signal):
            dve.wait_ge(unit_done, last_unit + 1)
            for t in range(T):
                dst = x[:, t, 512 * c:512 * c + 512]
                ins = tt(dst, dst, pair(chunk + c)[t][:, :], ALU.add)
            ins.then_inc(sem(signal), 1)

        splits_to(U_CQ + 1)
        add_chunk(0, C_OUT, U_OUT + 1, "x_attn")
        splits_to(U_CQ + 2)
        add_chunk(1, C_OUT, U_OUT + 3, "x_attn")
        norm([("x_attn", 2)], "crossq", CROSS_G)
        dve.wait_ge(sem("router_hi"), 1)
        tt(r_lo[:], r_w[:], r_hi[:].bitcast(F32), ALU.subtract).then_inc(sem("router_lo"), 1)
        splits_to(U_CQ + 6)
        inverse_of(head_inv[:, 0:8], head_sums[:, 0:8], CROSS, "qc_sums", 1, "qc_inverse")
        for n in (1, 3):
            b = product(dve, f"qc{n}")
            for j in range(2):
                ins = ts(q_crossT[:, 2 * n + j], b[:, 256 * j:256 * j + 256], cqk_g[:, 0, j:j + 1], None, ALU.mult)
            frees(ins, f"qc{n}")
        dve.wait_ge(sem("qc_rstd"), 1)
        then(ts(q_scale[:], head_rstd[:, 0:8], CROSS ** -0.5, None, ALU.mult))
        for n in range(4):
            b = product(dve, f"cs{n}")
            then(nc.vector.tensor_reduce(top[:, 2 * n:2 * n + 2], b[:, :].rearrange("p (h k) -> p h k", h=2), AX, ALU.max))
            stt(neg_top[:, 2 * n:2 * n + 2], top[:, 2 * n:2 * n + 2], -1.0, q_scale[:, 2 * n:2 * n + 2],
                ALU.mult, ALU.mult).then_inc(sem("cross_top"), 1)
        for n in range(4):
            been_read(dve, f"cs{n}")
        then(nc.vector.reciprocal(exp_inv[:, 0:8], exp_sum[:, 0:8]))
        for n in range(4):
            t, pair_of = n // 2, n % 2
            b = product(dve, f"co{n}")
            ins = tt(xs[:, t, 512 * pair_of:512 * pair_of + 512].rearrange("p (h d) -> p h d", h=2),
                     b[:, :].rearrange("p (h d) -> p h d", h=2),
                     exp_inv[:, 2 * n:2 * n + 2].unsqueeze(2).to_broadcast([P, 2, CROSS]), ALU.mult)
            frees(ins, f"co{n}")
        low_parts("catc", None)
        splits_to(U_MOE + 1)
        add_chunk(0, C_CO, U_CO + 1, "x_cross")
        dve.wait_ge(sem("lambda_exp"), 1)
        y, z, w, s = (lam_t[:, n] for n in (1, 2, 3, 4))
        then(ts(z, y, 2.0, None, ALU.add))
        then(nc.vector.reciprocal(z, z))
        then(tt(z, z, y, ALU.mult))
        then(tt(w, z, z, ALU.mult))
        then(ts(s, w, 1.0 / 19, None, ALU.mult))
        for n in range(8, 0, -1):
            then(stt(s, s, 1.0 / (2 * n + 1), w, ALU.add, ALU.mult))
        then(stt(s, s, 1.0, z, ALU.add, ALU.mult))
        then(ts(softplus2[:], lam, -1.0, 0.0, ALU.mult, ALU.max))
        then(stt(softplus2[:], s, 2.0, softplus2[:], ALU.mult, ALU.add))
        then(ts(softplus2[:], softplus2[:], 2.0, None, ALU.mult))
        ts(half_br, half_br, 0.5, None, ALU.mult)
        then(ts(half_bi, half_bi, 0.5, None, ALU.mult))
        splits_to(U_MOE + 2)
        add_chunk(1, C_CO, U_CO + 3, "x_cross")
        norm([("x_cross", 2)], "moe", MOE_G)
        for t in range(T):
            dve.wait_ge(sem("xs_hi"), t + 1)
            stt(xs_lo[:, t], x[:, t], rstd[:, t:t + 1], xs_hi[:, t].bitcast(F32), ALU.mult, ALU.subtract).then_inc(sem("xs_lo"), 1)
        routing(dve, then)

        def swiglu(name, base, steps, gate_of):
            def hiddens(e):
                for t in range(T):
                    dve.wait_ge(sem(name + "_tanh"), e * 2 + (t + 1))
                    stt(silu_g[:, t], silu_t[:, t], 1.0, bank[4 + t][:, 0:FF], ALU.add, ALU.mult).then_inc(sem(name + "_silu"), 1)
                for t in range(T):
                    dve.wait_ge(sem(name + "_silu"), e * 2 + (t + 1))
                    stt(hidden[:, t], bank[4 + t][:, FF:2 * FF], gate_of(t, e), silu_g[:, t], ALU.mult, ALU.mult)\
                        .then_inc(sem(name + "_hidden"), 1)

            def low(e):
                dve.wait_ge(sem(name + "_aT_hi"), e + 1)
                tt(flat3(aT_lo[:]), bank[6][:, :], flat3(aT_hi[:]).bitcast(F32), ALU.subtract).then_inc(sem(name + "_aT_lo"), 1)

            def step(i, first=False):
                if not first:
                    split_lo(dve, SLOT, base + 1, 3, i)
                split_lo(dve, SLOT, base + 2, 3, i)
                hiddens(i)
                split_lo(dve, SLOT, base + 3, 3, i)
                low(i)

            step(0, first=True)
            with dve.Fori(1, steps - 1) as i:
                step(i)
            split_lo(dve, SLOT, base + 1 + 3 * (steps - 1))
            hiddens(steps - 1)
            split_lo(dve, SLOT, base + 3 * steps - 1)
            low(steps - 1)

        def add_down(last_unit, signal):
            dve.wait_ge(unit_done, last_unit + 1)
            for n in range(4):
                dst = x[:, n % 2, 512 * (n // 2):512 * (n // 2) + 512]
                tt(dst, dst, bank[n][:, :], ALU.add).then_inc(sem(signal), 1)

        def experts(name, st, base, groups, signal, before_sums=None):
            for k in range(KD):
                dve.wait_ge(sem(name + "_xg_hi"), k + 1)
                gain = norm_g[:, MOE_G, k:k + 1]
                ins = stt(xg_lo[:, k], part_bank(k)[:, 0:P], gain, xg_hi[:, k].bitcast(F32), ALU.mult, ALU.subtract)
                if groups > 1:
                    ins = stt(later_lo[:, k], part_bank(k)[:, P:P * groups], gain, later_hi[:, k].bitcast(F32),
                              ALU.mult, ALU.subtract)
                ins.then_inc(sem(name + "_xg_lo"), 1)
            dve.wait_ge(sem(name + "_slot_gates"), 1)

            def hidden_low(g, j, next_up, last_down_unit=None):
                dve.wait_ge(sem(name + "_tanh"), eighths(g, j + 1))
                stt(silu_g[:, 0], silu_t[:, 0], 1.0, bank[6][:, 0:FF], ALU.add, ALU.mult).then_inc(sem(name + "_silu"), 1)
                dve.wait_ge(sem(name + "_silu"), eighths(g, j + 1))
                stt(hidden[:, 0], bank[6][:, FF:2 * FF], slot_gates[:, bass.ds(eighths(g, j), 1)], silu_g[:, 0],
                    ALU.mult, ALU.mult).then_inc(sem(name + "_hidden"), 1)
                if j == LAST and next_up:
                    nc.vector.tensor_copy(xg_lo[:], later_lo[:, :, bass.ds(g * P, P)].bitcast(F32))\
                        .then_inc(sem(name + "_moved"), 1)
                if next_up:
                    split_lo(dve, SLOT, up_unit(base, j + 1), PER_TURN, g, st)
                if last_down_unit is not None:
                    split_lo(dve, SLOT, last_down_unit, st=st)
                dve.wait_ge(sem(name + "_aT_hi"), eighths(g, j + 1))
                tt(flat3(aT_lo[:])[:, 0:FF], bank[7][:, 0:FF], flat3(aT_hi[:])[:, 0:FF].bitcast(F32),
                   ALU.subtract).then_inc(sem(name + "_aT_lo"), 1)

            def sums(g):
                for c in range(2):
                    dve.wait_ge(sem(name + "_y_hi"), g * 2 + (c + 1))
                    tt(y_lo[:, c], bank[4 + c][:, :], y_hi[:, c].bitcast(F32), ALU.subtract).then_inc(sem(name + "_y_lo"), 1)

            def add(g, to=None):
                dve.wait_ge(sem(name + "_banks_free"), g * 4 + (groups + 1) // 2)
                for n in range(4):
                    dve.wait_ge(sem(name + "_returned"), g * 4 + (n + 1))
                    dst = x[:, n % 2, 512 * (n // 2):512 * (n // 2) + 512]
                    tt(dst, dst, bank[n][:, :], ALU.add).then_inc(sem(to or name + "_banks_free"), 1)

            def step(g, j):
                if j:
                    split_lo(dve, SLOT, up_unit(base, j) + 1, PER_TURN, g, st)
                split_lo(dve, SLOT, gate_unit(base, j + 1), PER_TURN, g, st)
                hidden_low(g, j, True)
                if j == PER_GROUP:
                    sums(g)
                if j == PER_GROUP + 1:
                    add(g)

            def tail(g):
                split_lo(dve, SLOT, up_unit(base, LAST) + 1, PER_TURN, g, st)
                hidden_low(g, LAST, False, last_down(base, groups))
                if before_sums:
                    before_sums()
                sums(g)
                add(g, signal)

            expert_steps(dve, groups, step, tail)

        def head_splits():
            split_lo(dve, SLOT, U_HEADS)

        over_flag = []

        def early_head_splits():
            over_flag.append(overflow(dve))
            with dve.If(over_flag[0] < 1):
                head_splits()

        experts("moe", main, U_MOE, GROUPS, "x_moe", early_head_splits)
        with dve.If(over_flag[0] > 0):
            dve.wait_ge(sem("x_moe"), 4)
            group_hot = route[:, 2, 0:T * GROUPS]
            tt(over_t[:], rank[:, 0:T].rearrange("p t g -> p (t g)"), group_hot, ALU.mult).then_inc(sem("over_chain"), 1)
            dve.wait_ge(sem("over_chain"), 1)
            nc.vector.tensor_reduce(over_n[:], over_t[:].rearrange("p (t g) -> p t g", t=T), AX, ALU.add).then_inc(sem("over_chain"), 1)
            dve.wait_ge(sem("over_chain"), 2)
            ts(over_n[:], over_n[:], float(P), None, ALU.subtract).then_inc(sem("over_chain"), 1)
            dve.wait_ge(sem("over_chain"), 3)
            for t in range(T):
                ts(slot_of[:, t, 0:P], slot_numbers, over_n[:, t:t + 1], None, ALU.is_equal).then_inc(sem("over_slots"), 1)
            for u in range(2):
                split_lo(dve, SLOT, u, st=over)
            experts("over", over, 0, 1, "x_over")
            dve.wait_ge(sem("x_over"), 4)
            head_splits()
        stats(x, xs, [("x_moe", 4)], "mix")
        halves("mix")
        ts(xs[:, 1], x[:, 1], rstd[:, 1:2], None, ALU.mult).then_inc(sem("mix_scaled"), 1)
        split_lo(dve, SLOT, U_HEADS + 1)
        low_parts("mix", MIX_G)
        nc.vector.memset(xpad[:, :, 0:3], 0.0)
        nc.vector.memset(cpad[:, :, 0:2], 0.0).then_inc(sem("padded"), 1)
        dve.wait_ge(sem("padded"), 1)

        with dve.Fori(0, HEADS) as h:
            links = [0]

            def link(ins):
                links[0] += 1
                ins.then_inc(sem("head_chain"), 1)
                dve.wait_ge(sem("head_chain"), h * HEAD_LINKS + links[0])

            def unit(j):
                split_lo(dve, 512 if j in (RG_R, RG_I) else SLOT, U_HEADS + j, UNITS_HEAD, h)

            def done(j):
                dve.wait_ge(unit_done, h * UNITS_HEAD + (U_HEADS + j + 1))

            def col(v, tap, f):
                return v[:, bass.ds(h * 2 + (tap * KD + f), 1)]

            unit(C_CONV)
            dve.wait_ge(sem("rx_copied"), h + 1)
            for f in range(2):
                ins = ts(rx[:, f], xpad[:, f, 0:256], col(conv4_w, 0, f), col(conv4_b, 0, f), ALU.mult, ALU.add)
            for tap in range(1, 4):
                link(ins)
                for f in range(2):
                    ins = stt(rx[:, f], xpad[:, f, tap:tap + 256], col(conv4_w, tap, f), rx[:, f], ALU.mult, ALU.add)
            ins.then_inc(sem("conv4_done"), 1)
            unit(X_CONV)
            dve.wait_ge(sem("rx_hi"), h + 1)
            tt(rx_lo[:], rx[:].rearrange("p f t -> p (f t)"), rx_hi[:].bitcast(F32), ALU.subtract).then_inc(sem("rx_lo"), 1)
            dve.wait_ge(sem("y_copied"), h + 1)
            link(ts(y_sq[:], y_sq[:], 0.044715, 1.0, ALU.mult, ALU.add))
            tt(y_sq[:], y_sq[:], y_in[:], ALU.mult).then_inc(sem("gelu_inner"), 1)
            unit(RG_R)
            dve.wait_ge(sem("gelu_tanh"), h + 1)
            link(stt(y_in[:], y_tanh[:], 1.0, y_in[:], ALU.add, ALU.mult))
            unit(B_CONV)
            dve.wait_ge(sem("c_copied"), h + 1)
            done(X_CONV)
            tt(cpad[:, :, 2:258], bank[3][:, :].rearrange("p (f t) -> p f t", f=2),
               c_in[:].rearrange("p (f t) -> p f t", f=2), ALU.mult).then_inc(sem("cx_read"), 1)
            dve.wait_ge(sem("cx_read"), h + 1)
            for f in range(2):
                ins = ts(conv3[:, f], cpad[:, f, 0:256], col(conv3_w, 0, f), None, ALU.mult)
            for tap in range(1, 3):
                link(ins)
                for f in range(2):
                    ins = stt(conv3[:, f], cpad[:, f, tap:tap + 256], col(conv3_w, tap, f), conv3[:, f], ALU.mult, ALU.add)
            link(ins)
            unit(RG_I)
            unit(G_R)
            dve.wait_ge(sem("tau"), h * 2 + 2)
            tf = tau[:].rearrange("p f t -> p (f t)")
            link(ts(q_inv[:], tf, 1.0, None, ALU.add))
            nc.vector.reciprocal(q_inv[:, 0:256], q_inv[:, 0:256])
            unit(G_C)
            link(nc.vector.reciprocal(q_inv[:, 256:512], q_inv[:, 256:512]))
            ts(decay_a[:], q_inv[:], 2.0, -1.0, ALU.mult, ALU.add)
            split_lo(dve, SLOT, U_HEADS + 9, UNITS_HEAD, h)
            done(B_CONV)
            y_conv = conv3[:].rearrange("p f t -> p (f t)")
            tt(y_conv, bank[4][:, :], y_conv, ALU.mult).then_inc(sem("b_read"), 1)
            dve.wait_ge(sem("i_tanh"), h * 2 + 2)
            stt(u_in[:], i_tanh[:].rearrange("p f t -> p (f t)"), 1.0, rx[:].rearrange("p f t -> p (f t)"), ALU.add, ALU.mult)
            dve.wait_ge(sem("root_tau"), h + 1)
            link(tt(q_inv[:], root_tau[:].rearrange("p f t -> p (f t)"), q_inv[:], ALU.mult))
            link(tt(u_in[:], u_in[:], q_inv[:], ALU.mult))
            for f in range(2):
                ins = nc.vector.tensor_tensor_scan(states[:, 256 * f:256 * f + 256], decay_a[:, 256 * f:256 * f + 256],
                                                   u_in[:, 256 * f:256 * f + 256], 0.0, ALU.mult, ALU.add)
            link(ins)
            link(tt(y_in[:], y_in[:], states[:], ALU.mult))
            dve.wait_ge(sem("gr_tanh"), h + 1)
            stt(y_in[:], gr_tanh[:], 1.0, y_in[:], ALU.add, ALU.mult)
            split_lo(dve, SLOT, U_HEADS + 10, UNITS_HEAD, h)
            dve.wait_ge(sem("gc_tanh"), h + 1)
            link(stt(y_conv, gc_tanh[:], 1.0, y_conv, ALU.add, ALU.mult))
            stt(merged[:], y_in[:], 0.5, y_conv, ALU.mult, ALU.add).then_inc(sem("merged"), 1)
            dve.wait_ge(sem("mT_hi"), h + 1)
            stt(flat3(mT_lo[:])[:, bass.ds(h * 512, 512)], merged[:], 0.5,
                flat3(mT_hi[:])[:, bass.ds(h * 512, 512)].bitcast(F32), ALU.mult, ALU.subtract).then_inc(sem("mT_lo"), 1)
            assert links[0] == HEAD_LINKS, links[0]

        split[0] = U_OUT2 + 2
        splits_to(U_FFN + 1)
        add_chunk(0, C_OUT2, U_OUT2 + 2, "x_rnn")
        splits_to(U_FFN + 2)
        add_chunk(1, C_OUT2, U_OUT2 + 3, "x_rnn")
        norm([("x_rnn", 2)], "ffn", FFN_G)
        dve.wait_ge(sem("norm_half"), NORMS.index("ffn") + 1)
        then(tt(ffn_scale[:], half_rstd[:], rstd[:], ALU.mult))
        swiglu("ffn", U_FFN, STEPS_FFN, lambda t, e: ffn_scale[:, t:t + 1])
        split[0] = U_PLE
        splits_to(U_PLE + 2)
        add_down(U_PLE - 1, "x_ffn")
        dve.wait_ge(sem("pT_hi"), 1)
        frees(tt(flat3(aT_lo[:]), bank[where["pT"][0]][:, :], flat3(aT_hi[:]).bitcast(F32), ALU.subtract), "pT")
        norm([("x_ffn", 4)], "ple", PLE_G)
        for c in range(2):
            splits_to(min(U_END, U_PLE + 2 * c + 5))
            for t in range(T):
                dve.wait_ge(sem("ple_tanh"), 2 * c + t + 1)
                g, e, dst = (v[:, t, 512 * c:512 * c + 512] for v in (ple_gate, embed, x))
                then(stt(g, g, 1.0, e, ALU.add, ALU.mult))
                stt(dst, g, 0.5, dst, ALU.mult, ALU.add).then_inc(sem("x_ple"), 1)
        stats(x, xs, [("x_ple", 4)], "final")
        dve.wait_ge(sem("norm_rstd"), len(NORMS))
        dve.wait_ge(sem("last_loaded"), 32)
        for t in range(T):
            for c in range(2):
                at = slice(512 * c, 512 * c + 512)
                stt(embed[:, t, at], x[:, t, at], rstd[:, t:t + 1], fin_g[:, at], ALU.mult, ALU.mult).then_inc(sem("result"), 1)

    @block.tensor
    def _(pe):
        mm = nc.tensor.matmul

        def three(o, k_hi, k_lo, v_hi, v_lo, start, stop):
            mm(o, k_hi, v_hi, start=start, stop=False)
            mm(o, k_hi, v_lo, start=False, stop=False)
            return mm(o, k_lo, v_hi, start=False, stop=stop)

        def transpose(o, src):
            return nc.tensor.transpose(o, src, ident)

        def chunk_free(c):
            if c >= 2:
                chunk_read(pe, c - 2)

        def wide_unit(u, c, h, cols, th, tl, xt=None):
            s = u % RING
            pe.wait_ge(lo_ready, u + 1)
            for k in range(4):
                if xt is not None and k % 2 == 0:
                    been_read(pe, f"{xt}{2 * h + k // 2}")
                for t in range(T):
                    kk, at = 4 * h + k, cols * k
                    ins = three(pair(c)[t][:, 0:cols], th[:, kk, P * t:P * t + P], tl[:, kk, P * t:P * t + P],
                                w_hi[:, s, at:at + cols], w_lo[:, s, at:at + cols], start=kk == 0, stop=kk == KD - 1)
            ins.then_inc(unit_done, 1)

        def wide(c, u, cols=512, xt=None, th=xT_hi, tl=xT_lo, free=True):
            if free:
                chunk_free(c)
            for h in range(2):
                wide_unit(u + h, c, h, cols, th, tl, xt)

        def turn(name, src, waits):
            for s, n in waits:
                pe.wait_ge(sem(s), n)
            view = src[:].rearrange("p t (q k) -> p t k q", k=KD)
            for n in range(4):
                b = to_fill(pe, f"{name}{n}")
                for j in range(2):
                    for t in range(T):
                        ins = transpose(b[:, 256 * j + P * t:256 * j + P * t + P], view[:, t, 2 * n + j])
                fills(ins, f"{name}{n}")

        def turn_tiles(name, src_of, n=2):
            for i in range(n):
                b = to_fill(pe, f"{name}{i}")
                for j in range(2):
                    for t in range(T):
                        src = src_of(2 * i + j, t)
                        ins = transpose(b[0:src.shape[1], 256 * j + P * t:256 * j + P * t + P], src)
                fills(ins, f"{name}{i}")

        pe.wait_ge(sem("first_loaded"), 16 * len(first_loads))
        turn("mem", xs, [("mem_loaded0", 16), ("mem_loaded1", 16)])
        for c in range(4):
            wide(C_K + c, 2 * c, xt="mem")
            if c == 2:
                pe.wait_ge(sem("constants_loaded"), 16 * len(small_loads))
                b = to_fill(pe, "vec")
                fills(nc.tensor.transpose(b[:, 0:VEC_ROWS], vec_in[:], ident[0:VEC_ROWS, 0:VEC_ROWS]), "vec")
                pe.wait_ge(sem("kc_scaled"), 1)
                turn_tiles("kc", lambda j, t: k_cross[:, t, P * j:P * j + P], 4)
        turn("attn", x, [("x_loaded", 16)])
        wide(C_LAT, U_LAT, 448, xt="attn")
        wide(C_RQ, U_RQ)
        pe.wait_ge(sem("lat_scaled"), 1)
        b = to_fill(pe, "cq")
        for k in range(2):
            for t in range(T):
                ins = transpose(b[:, 256 * k + P * t:256 * k + P * t + P],
                                latent[:, t, 0:256].rearrange("p (q k) -> p k q", k=2)[:, k])
        fills(ins, "cq")
        b = to_fill(pe, "ckv")
        for t in range(T):
            ins = transpose(b[:, P * t:P * t + P], latent[:, t, 256:384])
        fills(ins, "ckv")
        wide(C_RK, U_RK)
        wide(C_RV, U_RV)
        been_read(pe, "cq")
        pe.wait_ge(lo_ready, U_UQ + 1)
        s = U_UQ % RING
        for c in range(2):
            chunk_free(C_UQ + c)
            for k in range(2):
                for t in range(T):
                    at = 768 * k + 384 * c
                    ins = three(pair(C_UQ + c)[t][:, 0:384], cT_hi[:, k, P * t:P * t + P], cT_lo[:, k, P * t:P * t + P],
                                w_hi[:, s, at:at + 384], w_lo[:, s, at:at + 384], start=k == 0, stop=k == 1)
        ins.then_inc(unit_done, 1)
        pe.wait_ge(sem("rot_ready"), 2)
        turn_tiles("rq", lambda h, t: rot_q.rearrange("p (t h d) -> p t h d", t=T, h=HEADS)[:, t, h])
        turn_tiles("rk", lambda h, t: rot_k.rearrange("p (t h d) -> p t h d", t=T, h=HEADS)[:, t, h])
        been_read(pe, "ckv")
        pe.wait_ge(lo_ready, U_UKV + 1)
        s = U_UKV % RING
        for c in range(2):
            chunk_free(C_UKV + c)
            for t in range(T):
                ins = three(pair(C_UKV + c)[t][:, :], cT_hi[:, 2, P * t:P * t + P], cT_lo[:, 2, P * t:P * t + P],
                            w_hi[:, s, 512 * c:512 * c + 512], w_lo[:, s, 512 * c:512 * c + 512], start=True, stop=True)
        ins.then_inc(unit_done, 1)
        for n in range(2):
            been_read(pe, f"rq{n}")
            been_read(pe, f"rk{n}")
        for n in range(2):
            b = to_fill(pe, f"rs{n}")
            for j in range(2):
                h = 2 * n + j
                ins = mm(b[:, 256 * j:256 * j + 256], r_kT[:, h, 0:P], r_qT[:, h, :], start=True, stop=True)
            fills(ins, f"rs{n}")
        b = to_fill(pe, "rs2")
        for h in range(HEADS):
            ins = mm(b[:, P * h:P * h + P], r_kT[:, h, P:2 * P], r_qT[:, h, P:2 * P], start=True, stop=True)
        fills(ins, "rs2")
        chunk_free(C_RG)
        wide_unit(U_RG, C_RG, 0, 512, xT_hi, xT_lo)
        for n in range(3):
            been_read(pe, f"rs{n}")
        for t in range(T):
            b = to_fill(pe, f"ro{t}")
            for h in range(HEADS):
                o = b[:, P * h:P * h + P]
                ins = mm(o, r_s0[:, h, P * t:P * t + P], r_v[:, 0, P * h:P * h + P], start=True, stop=t == 0)
                if t:
                    ins = mm(o, r_s1[:, h], r_v[:, 1, P * h:P * h + P], start=False, stop=True)
            fills(ins, f"ro{t}")

        pe.wait_ge(sem("qk_turned"), 1)
        turn_tiles("qn", lambda h, t: q_mla[:, t, h, 0:NOPE])
        wide_unit(U_RG + 1, C_RG, 1, 512, xT_hi, xT_lo)
        turn_tiles("qr", lambda h, t: qk_r[0][:, t, h])
        pe.wait_ge(sem("qk_turned"), 3)
        turn_tiles("kn", lambda h, t: k_mla[:, t, h, 0:NOPE])
        turn_tiles("kr", lambda h, t: qk_r[1][:, t, h])
        for name in ("qn", "qr", "kn", "kr"):
            for n in range(2):
                been_read(pe, f"{name}{n}")

        def score(o, h, q, keys):
            mm(o, qT_n[:, h, q], kT_n[:, h, keys], start=True, stop=False)
            return mm(o, qT_r[0:ROPE, h, q], kT_r[0:ROPE, h, keys], start=False, stop=True)

        b = to_fill(pe, "s0")
        for h in range(HEADS):
            ins = score(b[:, P * h:P * h + P], h, slice(0, P), slice(0, P))
        fills(ins, "s0")
        for n in (1, 2):
            b = to_fill(pe, f"s{n}")
            for j in range(2):
                ins = score(b[:, 256 * j:256 * j + 256], 2 * (n - 1) + j, slice(P, 2 * P), slice(0, 2 * P))
            fills(ins, f"s{n}")
        for n in range(3):
            pe.wait_ge(sem("exped"), 4 + 2 * n)
            b = to_fill(pe, f"pT{n}")
            for j in range(4):
                ins = transpose(b[:, P * j:P * j + P], scores[:, 512 * n + P * j:512 * n + P * j + P])
            fills(ins, f"pT{n}")
        for n in range(3):
            been_read(pe, f"pT{n}")
        for t in range(T):
            b = to_fill(pe, f"o{t}")
            for h in range(HEADS):
                for k in range(t + 1):
                    at = P * h if t == 0 else 512 + 256 * h + P * k
                    ins = mm(b[:, P * h:P * h + P], probsT[:, at:at + P], v_mla[:, k, h], start=k == 0, stop=k == t)
            fills(ins, f"o{t}")
        been_read(pe, "o0")
        been_read(pe, "o1")
        turn("cat", xs, [("cat_scaled", T)])
        for c in range(2):
            wide(C_OUT + c, U_OUT + 2 * c, xt="cat")

        turn("crossq", x, [("x_attn", 2)])
        pe.wait_ge(sem("x_attn"), 2)
        for c in range(2):
            wide(C_CQ + c, U_CQ + 2 * c, xt="crossq", free=False)
        for c in range(2):
            chunk_read(pe, C_CQ + c)
        turn_tiles("qc", lambda j, t: q_cross[:, t, P * j:P * j + P], 4)
        for n in range(4):
            been_read(pe, f"kc{n}")
        for n in range(4):
            if n < 2:
                been_read(pe, f"qc{2 * n}")
                been_read(pe, f"qc{2 * n + 1}")
            t, b = n // 2, to_fill(pe, f"cs{n}")
            for j in range(2):
                h = 2 * (n % 2) + j
                for k in range(2):
                    ins = mm(b[:, 256 * j:256 * j + 256], q_crossT[:, 2 * h + k, P * t:P * t + P], k_crossT[:, 2 * h + k],
                             start=k == 0, stop=k == 1)
            fills(ins, f"cs{n}")
        for n in range(4):
            been_read(pe, f"cs{n}")
            t, b = n // 2, to_fill(pe, f"cp{n}")
            for j in range(2):
                for k in range(2):
                    ins = transpose(b[:, 256 * j + P * k:256 * j + P * k + P], c_scores[:, t, 2 * (n % 2) + j, P * k:P * k + P])
            fills(ins, f"cp{n}")
        for n in range(4):
            been_read(pe, f"cp{n}")
            t, b = n // 2, to_fill(pe, f"co{n}")
            for j in range(2):
                h = 2 * (n % 2) + j
                for k in range(2):
                    ins = mm(b[:, 256 * j:256 * j + 256], c_probsT[:, t, h, P * k:P * k + P],
                             v_cross[:, k, 256 * h:256 * h + 256], start=k == 0, stop=k == 1)
            fills(ins, f"co{n}")
        for n in range(4):
            been_read(pe, f"co{n}")
        turn("catc", xs, [])
        for c in range(2):
            chunk_read(pe, C_CQ + c)
        for c in range(2):
            wide(C_CO + c, U_CO + 2 * c, xt="catc", free=False)

        turn("moe", x, [("x_cross", 2)])
        pe.wait_ge(sem("router_lo"), 1)
        b = to_fill(pe, "router")
        for k in range(KD):
            if k % 2 == 0:
                been_read(pe, f"moe{k // 2}")
            ins = three(b[0:CHOICES, 0:T * P], r_hi[:, k], r_lo[:, k], xT_hi[:, k], xT_lo[:, k], start=k == 0, stop=k == KD - 1)
        fills(ins, "router")
        been_read(pe, "router")
        b = to_fill(pe, "logits")
        for t in range(T):
            ins = nc.tensor.transpose(b[:, CHOICES * t:CHOICES * t + CHOICES], logitsT[:, P * t:P * t + P], ident[0:CHOICES, 0:CHOICES])
        fills(ins, "logits")
        pe.wait_ge(sem("group_chosen"), 1)
        pe.wait_ge(sem("ones_set"), 1)
        b = to_fill(pe, "rank")
        hot = [route[:, 2, GROUPS * t:GROUPS * t + GROUPS] for t in range(T)]
        mm(b[:, 0:GROUPS], earlier, hot[0], start=True, stop=True)
        mm(b[:, GROUPS:2 * GROUPS], earlier, hot[1], start=True, stop=False)
        mm(b[:, GROUPS:2 * GROUPS], ones[:], hot[0], start=False, stop=True)
        mm(b[:, 2 * GROUPS:3 * GROUPS], ones[:], hot[0], start=True, stop=False)
        fills(mm(b[:, 2 * GROUPS:3 * GROUPS], ones[:], hot[1], start=False, stop=True), "rank")
        been_read(pe, "logits")
        been_read(pe, "rank")
        pe.wait_ge(sem("x_cross"), 2)
        pe.wait_ge(sem("xs_lo"), T)

        def experts(name, st, base, groups):
            view_hi, view_lo = (v[:].rearrange("p t (q k) -> p t k q", k=KD) for v in (xs_hi, xs_lo))
            width = P * groups
            for k in range(KD):
                if k >= 6:
                    pe.wait_ge(sem(name + "_xg_lo"), k - 5)
                for t in range(T):
                    mm(part_bank(k)[:, 0:width], view_hi[:, t, k], slot_of[:, t, 0:width], start=t == 0, stop=False)
                    ins = mm(part_bank(k)[:, 0:width], view_lo[:, t, k], slot_of[:, t, 0:width], start=False, stop=t == T - 1)
                ins.then_inc(sem(name + "_gathered"), 1)
            pe.wait_ge(sem("token_gates"), 1)
            for g in range(groups):
                for t in range(T):
                    ins = mm(bank[7][:, PER_GROUP * g:PER_GROUP * g + PER_GROUP], slot_of[:, t, P * g:P * g + P].bitcast(F32),
                             token_gates[:, t], start=t == 0, stop=t == T - 1)
            ins.then_inc(sem(name + "_gates"), 1)

            def columns_of(which, u0, g, first=False):
                pe.wait_ge(st.lo_ready, g * PER_TURN + (u0 + 1))
                s = u0 % RING
                for k in range(KD):
                    if first:
                        pe.wait_ge(sem(name + "_xg_lo"), k + 1)
                    ins = three(bank[6][:, FF * which:FF * which + FF], xg_hi[:, k], xg_lo[:, k],
                                w_hi[:, s, FF * k:FF * k + FF], w_lo[:, s, FF * k:FF * k + FF], start=k == 0, stop=k == KD - 1)
                ins.then_inc(st.unit_done, 1)

            def down(g, j, u0):
                pe.wait_ge(st.lo_ready, g * PER_TURN + (u0 + 1) if u0 != last_down(base, groups) else u0 + 1)
                pe.wait_ge(sem(name + "_aT_lo"), eighths(g, j + 1))
                s = u0 % RING
                for k in range(2):
                    for c in range(2):
                        at = D * k + 512 * c
                        ins = three(bank[4 + c][:, :], flat3(aT_hi[:])[:, P * k:P * k + P], flat3(aT_lo[:])[:, P * k:P * k + P],
                                    w_hi[:, s, at:at + 512], w_lo[:, s, at:at + 512],
                                    start=j % PER_GROUP == 0 and k == 0, stop=j % PER_GROUP == LAST and k == 1)
                ins.then_inc(st.unit_done, 1)

            def turn_hidden(g, j):
                pe.wait_ge(sem(name + "_hidden"), eighths(g, j + 1))
                view = hidden[:, 0].rearrange("p (q k) -> p k q", k=2)
                for k in range(2):
                    ins = transpose(bank[7][:, P * k:P * k + P], view[:, k])
                ins.then_inc(sem(name + "_turned"), 1)

            def bring_back(g):
                pe.wait_ge(sem(name + "_y_lo"), g * 2 + 2)
                pe.wait_ge(sem(name + "_banks_free"), g * 4 + (groups + 1) // 2)
                pe.wait_ge(sem(name + "_token_now"), g + 1)
                for n in range(4):
                    tokens = token_now[:, P * (n % 2):P * (n % 2) + P]
                    mm(bank[n][:, :], tokens, y_hi[:, n // 2], start=True, stop=False)
                    mm(bank[n][:, :], tokens, y_lo[:, n // 2], start=False, stop=True).then_inc(sem(name + "_returned"), 1)

            def gate_up(g, j):
                if j:
                    pe.wait_ge(sem(name + "_hidden"), eighths(g, j))
                if j == PER_GROUP:
                    pe.wait_ge(sem(name + "_moved"), g * 2 + 2)
                columns_of(0, gate_unit(base, j), g, first=j == 0)
                columns_of(1, up_unit(base, j), g)

            def step(g, j):
                gate_up(g, j)
                if j == PER_GROUP + 1:
                    bring_back(g)
                if j:
                    down(g, j - 1, up_unit(base, j) + 1)
                turn_hidden(g, j)
                if j == 0:
                    for n in range(groups):
                        for t in range(T):
                            at = 256 * (n % 2) + P * t
                            ins = transpose(bank[2 + n // 2][:, at:at + P], slot_of[:, t, P * n:P * n + P].bitcast(F32))
                        if n % 2 or groups == 1:
                            ins.then_inc(sem(name + "_sel_turned"), 1)

            def tail(g):
                step(g, LAST)
                down(g, LAST, last_down(base, groups))
                bring_back(g)

            expert_steps(pe, groups, step, tail)

        pe.wait_ge(sem("slots_known"), T * GROUPS)
        experts("moe", main, U_MOE, GROUPS)
        with pe.If(overflow(pe) > 0):
            pe.wait_ge(sem("x_moe"), 4)
            pe.wait_ge(sem("over_slots"), T)
            experts("over", over, 0, 1)

        def swiglu(name, base, steps):
            def columns_of(which, u0, per, i):
                if u0 == base and per == 0:
                    for n in range(4):
                        if where[f"{name}{n}"][0] < 6:
                            been_read(pe, f"{name}{n}")
                pe.wait_ge(lo_ready, count(u0 + 1, per, i))
                s = u0 % RING
                for k in range(KD):
                    if u0 == base and per == 0 and k % 2 == 0:
                        been_read(pe, f"{name}{k // 2}")
                    for t in range(T):
                        ins = three(bank[4 + t][:, FF * which:FF * which + FF], xT_hi[:, k, P * t:P * t + P], xT_lo[:, k, P * t:P * t + P],
                                    w_hi[:, s, FF * k:FF * k + FF], w_lo[:, s, FF * k:FF * k + FF], start=k == 0, stop=k == KD - 1)
                ins.then_inc(unit_done, 1)

            def down(e, u0, per, i, first=False, last_step=False):
                pe.wait_ge(lo_ready, count(u0 + 1, per, i))
                pe.wait_ge(sem(name + "_aT_lo"), e + 1)
                s = u0 % RING
                for k in range(2):
                    for t in range(T):
                        for c in range(2):
                            at = D * k + 512 * c
                            ins = three(bank[2 * c + t][:, :], aT_hi[:, k, P * t:P * t + P], aT_lo[:, k, P * t:P * t + P],
                                        w_hi[:, s, at:at + 512], w_lo[:, s, at:at + 512],
                                        start=first and k == 0, stop=last_step and k == 1)
                ins.then_inc(unit_done, 1)

            def turn_hidden(e):
                pe.wait_ge(sem(name + "_hidden"), e * 2 + 2)
                view = hidden[:].rearrange("p t (q k) -> p t k q", k=2)
                for k in range(2):
                    for t in range(T):
                        ins = transpose(bank[6][:, 256 * k + P * t:256 * k + P * t + P], view[:, t, k])
                ins.then_inc(sem(name + "_turned"), 1)

            columns_of(0, base, 0, 0)
            columns_of(1, base + 1, 0, 0)
            turn_hidden(0)

            def step(i, first=False):
                pe.wait_ge(sem(name + "_hidden"), i * 2)
                columns_of(0, base - 1, 3, i)
                columns_of(1, base, 3, i)
                down(i - 1, base + 1, 3, i, first=first)
                turn_hidden(i)

            step(1, first=True)
            with pe.Fori(2, steps) as i:
                step(i)
            down(steps - 1, base + 3 * steps - 1, 0, 0, last_step=True)

        turn("mix", xs, [("mix_scaled", T)])
        for n in range(4):
            been_read(pe, f"mix{n}")
        pe.wait_ge(sem("x_moe"), 4)
        with pe.Fori(0, HEADS) as h:
            def features(j, b):
                pe.wait_ge(lo_ready, h * UNITS_HEAD + (U_HEADS + j + 1))
                s = (U_HEADS + j) % RING
                for f in range(2):
                    for k in range(KD):
                        at = 256 * k + P * f
                        o = bank[b][:, 256 * f:256 * f + 256]
                        mm(o, w_hi[:, s, at:at + P], xT_hi[:, k, :], start=k == 0, stop=False)
                        mm(o, w_hi[:, s, at:at + P], xT_lo[:, k, :], start=False, stop=False)
                        ins = mm(o, w_lo[:, s, at:at + P], xT_hi[:, k, :], start=False, stop=k == KD - 1)
                ins.then_inc(unit_done, 1)

            def block_diagonal(j, b):
                pe.wait_ge(lo_ready, h * UNITS_HEAD + (U_HEADS + j + 1))
                s = (U_HEADS + j) % RING
                for f in range(2):
                    for k in range(2):
                        at = 256 * k + P * f
                        o = bank[b][:, 256 * f:256 * f + 256]
                        mm(o, w_hi[:, s, at:at + P], rx_hi[:, 256 * k:256 * k + 256], start=k == 0, stop=False)
                        mm(o, w_hi[:, s, at:at + P], rx_lo[:, 256 * k:256 * k + 256], start=False, stop=False)
                        ins = mm(o, w_lo[:, s, at:at + P], rx_hi[:, 256 * k:256 * k + 256], start=False, stop=k == 1)
                ins.then_inc(unit_done, 1)

            for b, j in enumerate((RX, GELU, C_CONV, X_CONV)):
                features(j, b)
            pe.wait_ge(sem("rx_lo"), h + 1)
            block_diagonal(RG_R, 7)
            features(B_CONV, 4)
            pe.wait_ge(sem("rx_copied"), h + 1)
            block_diagonal(RG_I, 0)
            features(G_R, 5)
            features(G_C, 6)

        for half in range(2):
            pe.wait_ge(sem("mT_lo"), 2 * half + 2)
            for c in range(2):
                wide_unit(U_OUT2 + 2 * half + c, C_OUT2 + c, half, 512, mT_hi, mT_lo)
        turn("ffn", x, [("x_rnn", 2)])
        pe.wait_ge(sem("x_rnn"), 2)
        swiglu("ffn", U_FFN, STEPS_FFN)

        pe.wait_ge(sem("last_loaded"), 32)
        b = to_fill(pe, "pT")
        view = p_in[:].rearrange("p t (q k) -> p t k q", k=2)
        for k in range(2):
            for t in range(T):
                ins = transpose(b[:, 256 * k + P * t:256 * k + P * t + P], view[:, t, k])
        fills(ins, "pT")
        turn("ple", x, [("x_ffn", 4)])
        been_read(pe, "pT")
        pe.wait_ge(lo_ready, U_PLE + 1)
        s = U_PLE % RING
        for c in range(2):
            for k in range(2):
                for t in range(T):
                    at = D * k + 512 * c
                    ins = three(pair(C_PLE + c)[t][:, :], aT_hi[:, k, P * t:P * t + P], aT_lo[:, k, P * t:P * t + P],
                                w_hi[:, s, at:at + 512], w_lo[:, s, at:at + 512], start=k == 0, stop=k == 1)
        ins.then_inc(unit_done, 1)
        for c in range(2):
            wide(C_GATE + c, U_PLE + 1 + 2 * c, xt="ple")


_INS = ("x mem positions attn_norm_g w_in mla_q_norm_g mla_w_uq mla_kv_norm_g mla_w_ukv mla_q_qk_g mla_k_qk_g "
        "ret_gn_g w_out cross_norm_g mem_norm_g cross_w_q cross_w_kv cross_q_qk_g cross_k_qk_g cross_w_o moe_norm_g "
        "router_w_group router_b_group router_w_expert router_b_expert expert_w_gate expert_w_up expert_w_down p_2 "
        "g_mix_2 w_in_2 conv4_w_2 conv4_b_2 w_rg_r_2 b_rg_r_2 w_rg_i_2 b_rg_i_2 lru_lambda_2 conv3_w_2 w_out_2 "
        "g_ffn_2 w_gate_up_2 w_down_2 g_ple_2 w_ple_gate_2 w_ple_2 g_final_2").split()


def kernel(**inputs):
    import numpy as _np
    import concourse.bacc as _bacc
    from concourse import mybir as _mybir
    from concourse.bass_utils import run_bass_kernel_spmd as _run

    nc = _bacc.Bacc("TRN2", target_bir_lowering=False, num_devices=1)
    arrays, aps = {}, {}
    for name in _INS:
        arrays[f"in_{name}_dram"] = _np.ascontiguousarray(inputs[name])
    arrays["in_const_dram"] = constants()
    for name in _INS + ["const"]:
        v = arrays[f"in_{name}_dram"]
        aps[name] = nc.dram_tensor(f"in_{name}_dram", v.shape, _mybir.dt.from_np(v.dtype), kind="ExternalInput").ap()
    result = nc.dram_tensor("out_0_dram", (1, T * P, D), _mybir.dt.float32, kind="ExternalOutput").ap()
    build(nc, aps, result)
    r = _run(nc, [arrays], core_ids=[0])
    return r.results[0]["out_0_dram"]
```
